# Optimizing a Trainium2 kernel written in Bass

```python
import math
import jax, jax.numpy as jnp
from jax import lax
import numpy as np

D_MODEL = 1024
BATCH = 1
SEQ = 512
DEPTH = 1

D_MIX = D_MODEL
MLA_HEADS = 4
MLA_NOPE = 128
MLA_ROPE = 64
MLA_QK = MLA_NOPE + MLA_ROPE
MLA_V = 128
MLA_Q_LORA = 384
MLA_KV_LORA = 256
DIFF_HEADS = 4
DIFF_DQK = 64
DIFF_DV = 2 * DIFF_DQK
IN_MLA = MLA_Q_LORA + MLA_KV_LORA + MLA_ROPE
IN_DIFF_Q = DIFF_HEADS * 2 * DIFF_DQK
IN_DIFF_V = DIFF_HEADS * DIFF_DV
IN_COLS = IN_MLA + 2 * IN_DIFF_Q + IN_DIFF_V
ROPE_THETA = 10000.0
Q_BLOCK = 128
RMS_EPS = 1e-6
PEER_HEADS = 8
PEER_NKEYS = 128
PEER_EXPERTS = PEER_NKEYS * PEER_NKEYS
PEER_DK_HALF = 128
PEER_TOPK = 16
PEER_CHUNK = 128
ADA_INIT = 0.2


def rms_norm(x, g):
    xf = x.astype(jnp.float32)
    y = xf * lax.rsqrt(jnp.mean(xf * xf, axis=-1, keepdims=True) + RMS_EPS)
    return (y * g.astype(jnp.float32)).astype(x.dtype)

def rope_tables(seq, dim):
    half = dim // 2
    inv = 1.0 / (ROPE_THETA ** (jnp.arange(half, dtype=jnp.float32) / half))
    ang = jnp.arange(seq, dtype=jnp.float32)[:, None] * inv[None, :]
    return jnp.cos(ang), jnp.sin(ang)

def apply_rope(x, cos, sin):
    half = x.shape[-1] // 2
    xf = x.astype(jnp.float32)
    x1, x2 = xf[..., :half], xf[..., half:]
    return jnp.concatenate([x1 * cos - x2 * sin, x2 * cos + x1 * sin], axis=-1).astype(x.dtype)

def causal_attention(qs, ks, coeffs, v, scale):
    B, H, S, dv = v.shape
    nb = S // Q_BLOCK
    qbs = tuple(q.reshape(B, H, nb, Q_BLOCK, q.shape[-1]).transpose(2, 0, 1, 3, 4) for q in qs)
    kpos = jnp.arange(S)

    def one_block(args):
        i, qb = args
        qpos = i * Q_BLOCK + jnp.arange(Q_BLOCK)
        mask = kpos[None, :] <= qpos[:, None]
        w = None
        for qi, ki, ci in zip(qb, ks, coeffs):
            s = jnp.einsum('bhqd,bhkd->bhqk', qi, ki).astype(jnp.float32) * scale
            p = jax.nn.softmax(jnp.where(mask, s, -jnp.inf), axis=-1)
            w = ci * p if w is None else w + ci * p
        return jnp.einsum('bhqk,bhkd->bhqd', w.astype(v.dtype), v)

    out = lax.map(one_block, (jnp.arange(nb), qbs))
    return out.transpose(1, 2, 0, 3, 4).reshape(B, H, S, dv)

def peer_ffn(h, w_q, sub_keys, u_tab, v_tab):
    T, D = h.shape
    hc = h.reshape(T // PEER_CHUNK, PEER_CHUNK, D)

    def one_chunk(hb):
        C = hb.shape[0]
        q = (hb @ w_q).reshape(C, PEER_HEADS, 2, PEER_DK_HALF)
        s = jnp.einsum('thpd,hpnd->thpn', q, sub_keys).astype(jnp.float32)
        sv, si = lax.top_k(s, PEER_TOPK)
        cand = sv[:, :, 0, :, None] + sv[:, :, 1, None, :]
        cidx = si[:, :, 0, :, None] * PEER_NKEYS + si[:, :, 1, None, :]
        cand = cand.reshape(C, PEER_HEADS, PEER_TOPK * PEER_TOPK)
        cidx = cidx.reshape(C, PEER_HEADS, PEER_TOPK * PEER_TOPK)
        fv, fpos = lax.top_k(cand, PEER_TOPK)
        eidx = jnp.take_along_axis(cidx, fpos, axis=-1).reshape(C, PEER_HEADS * PEER_TOPK)
        g = jax.nn.softmax(fv, axis=-1).reshape(C, PEER_HEADS * PEER_TOPK)
        u = u_tab[eidx]
        a = jax.nn.gelu(jnp.einsum('ted,td->te', u, hb).astype(jnp.float32), approximate=False)
        coef = (g * a).astype(hb.dtype)
        vv = v_tab[eidx]
        return jnp.einsum('te,ted->td', coef, vv)

    return lax.map(one_chunk, hc).reshape(T, D)

def first_inputs(seed: int = 0) -> dict:
    key = jax.random.key(seed)
    keys = iter(jax.random.split(key, 40))

    def nrm(shape, scale):
        return jax.random.normal(next(keys), shape, jnp.float32) * scale

    def gain(shape):
        return 1.0 + nrm(shape, 0.02)

    L = DEPTH
    return {
        'x': nrm((BATCH, SEQ, D_MODEL), 1.0),
        'c': nrm((BATCH, D_MODEL), 1.0),
        'ada_w': nrm((L, D_MODEL, 6 * D_MODEL), ADA_INIT * D_MODEL ** -0.5),
        'ada_b': nrm((L, 6 * D_MODEL), 0.02),
        'norm1_g': gain((L, D_MODEL)),
        'w_in': nrm((L, D_MODEL, IN_COLS), D_MODEL ** -0.5),
        'mla_q_lat_g': gain((L, MLA_Q_LORA)),
        'mla_w_q_up': nrm((L, MLA_Q_LORA, MLA_HEADS * MLA_QK), MLA_Q_LORA ** -0.5),
        'mla_kv_lat_g': gain((L, MLA_KV_LORA)),
        'mla_w_kv_up': nrm((L, MLA_KV_LORA, MLA_HEADS * (MLA_NOPE + MLA_V)), MLA_KV_LORA ** -0.5),
        'mla_q_g': gain((L, MLA_QK)),
        'mla_k_g': gain((L, MLA_QK)),
        'diff_q_g': gain((L, DIFF_DQK)),
        'diff_k_g': gain((L, DIFF_DQK)),
        'diff_lq1': nrm((L, DIFF_DQK), 0.1),
        'diff_lk1': nrm((L, DIFF_DQK), 0.1),
        'diff_lq2': nrm((L, DIFF_DQK), 0.1),
        'diff_lk2': nrm((L, DIFF_DQK), 0.1),
        'diff_subln_g': gain((L, DIFF_DV)),
        'w_out': nrm((L, D_MIX, D_MODEL), D_MIX ** -0.5),
        'norm2_g': gain((L, D_MODEL)),
        'peer_w_q': nrm((L, D_MODEL, PEER_HEADS * 2 * PEER_DK_HALF), D_MODEL ** -0.5),
        'peer_sub_keys': nrm((L, PEER_HEADS, 2, PEER_NKEYS, PEER_DK_HALF), PEER_DK_HALF ** -0.5),
        'peer_u': nrm((L, PEER_EXPERTS, D_MODEL), D_MODEL ** -0.5),
        'peer_v': nrm((L, PEER_EXPERTS, D_MODEL), PEER_HEADS ** -0.5),
    }

def first_block(x, c, ada_w, ada_b, norm1_g, w_in, mla_q_lat_g, mla_w_q_up, mla_kv_lat_g,
              mla_w_kv_up, mla_q_g, mla_k_g, diff_q_g, diff_k_g, diff_lq1, diff_lk1, diff_lq2,
              diff_lk2, diff_subln_g, w_out, norm2_g, peer_w_q, peer_sub_keys, peer_u, peer_v):
    B, S, D = x.shape
    cos_m, sin_m = rope_tables(S, MLA_ROPE)
    cos_d, sin_d = rope_tables(S, DIFF_DQK)

    for l in range(DEPTH):
        mod = jax.nn.silu(c) @ ada_w[l] + ada_b[l]
        sh1, sc1, g1, sh2, sc2, g2 = [m[:, None, :] for m in jnp.split(mod, 6, axis=-1)]

        h = rms_norm(x, norm1_g[l]) * (1.0 + sc1) + sh1
        proj = h @ w_in[l]
        o0 = MLA_Q_LORA
        o1 = o0 + MLA_KV_LORA
        o2 = o1 + MLA_ROPE
        o3 = o2 + IN_DIFF_Q
        o4 = o3 + IN_DIFF_Q
        q_lat, kv_lat, kpe_raw = proj[..., :o0], proj[..., o0:o1], proj[..., o1:o2]
        dq, dk, dv = proj[..., o2:o3], proj[..., o3:o4], proj[..., o4:]

        q = (rms_norm(q_lat, mla_q_lat_g[l]) @ mla_w_q_up[l]).reshape(B, S, MLA_HEADS, MLA_QK)
        q = q.transpose(0, 2, 1, 3)
        q_nope = rms_norm(q[..., :MLA_NOPE], mla_q_g[l, :MLA_NOPE])
        q_pe = apply_rope(rms_norm(q[..., MLA_NOPE:], mla_q_g[l, MLA_NOPE:]), cos_m, sin_m)
        kv = (rms_norm(kv_lat, mla_kv_lat_g[l]) @ mla_w_kv_up[l]).reshape(B, S, MLA_HEADS, MLA_NOPE + MLA_V)
        kv = kv.transpose(0, 2, 1, 3)
        k_nope = rms_norm(kv[..., :MLA_NOPE], mla_k_g[l, :MLA_NOPE])
        v_m = kv[..., MLA_NOPE:]
        k_pe = apply_rope(rms_norm(kpe_raw, mla_k_g[l, MLA_NOPE:])[:, None], cos_m, sin_m)
        k_m = jnp.concatenate([k_nope, jnp.broadcast_to(k_pe, (B, MLA_HEADS, S, MLA_ROPE))], axis=-1)
        q_m = jnp.concatenate([q_nope, q_pe], axis=-1)
        out_m = causal_attention((q_m,), (k_m,), (1.0,), v_m, MLA_QK ** -0.5)

        qd = dq.reshape(B, S, DIFF_HEADS, 2, DIFF_DQK).transpose(0, 2, 3, 1, 4)
        kd = dk.reshape(B, S, DIFF_HEADS, 2, DIFF_DQK).transpose(0, 2, 3, 1, 4)
        qd = apply_rope(rms_norm(qd, diff_q_g[l]), cos_d, sin_d)
        kd = apply_rope(rms_norm(kd, diff_k_g[l]), cos_d, sin_d)
        vd = dv.reshape(B, S, DIFF_HEADS, DIFF_DV).transpose(0, 2, 1, 3)
        lambda_init = 0.8 - 0.6 * math.exp(-0.3 * l)
        lam = (jnp.exp(jnp.sum(diff_lq1[l].astype(jnp.float32) * diff_lk1[l].astype(jnp.float32)))
               - jnp.exp(jnp.sum(diff_lq2[l].astype(jnp.float32) * diff_lk2[l].astype(jnp.float32)))
               + lambda_init)
        out_d = causal_attention((qd[:, :, 0], qd[:, :, 1]), (kd[:, :, 0], kd[:, :, 1]),
                                 (1.0, -lam), vd, DIFF_DQK ** -0.5)
        out_d = rms_norm(out_d, diff_subln_g[l]) * (1.0 - lambda_init)

        mixed = jnp.concatenate([out_m.transpose(0, 2, 1, 3).reshape(B, S, MLA_HEADS * MLA_V),
                                 out_d.transpose(0, 2, 1, 3).reshape(B, S, DIFF_HEADS * DIFF_DV)], axis=-1)
        x = x + g1 * (mixed @ w_out[l])

        h2 = rms_norm(x, norm2_g[l]) * (1.0 + sc2) + sh2
        y = peer_ffn(h2.reshape(B * S, D), peer_w_q[l], peer_sub_keys[l], peer_u[l], peer_v[l])
        x = x + g2 * y.reshape(B, S, D)
    return x


DEPTH_2 = 2

N_A_LAYERS = DEPTH_2 // 2
N_B_LAYERS = DEPTH_2 - N_A_LAYERS
EPS = 1e-6

EXPAND = 2
CONV_D = EXPAND * D_MODEL
CONV_WIDTH = 3

N_HEADS = 16
HEAD_DIM = D_MODEL // N_HEADS
N_KV_GROUPS = 4
HEADS_PER_GROUP = N_HEADS // N_KV_GROUPS
ATTN_D = N_HEADS * HEAD_DIM
KV_D = N_KV_GROUPS * HEAD_DIM
N_BRANCH = 3
N_KV_STREAMS = 6
ROT_DIM = HEAD_DIM // 4
ROPE_THETA_2 = 500000.0
CMP_BLOCK = 32
CMP_STRIDE = 16
CMP_R = CMP_BLOCK // CMP_STRIDE
CMP_HIDDEN = 4 * HEAD_DIM
SLC_BLOCK = 64
SLC_RATIO = SLC_BLOCK // CMP_STRIDE
N_SELECT = 16
N_LOCAL = 2
WINDOW = 512
Q_BLOCK_2 = 64
FORCE_SCORE = 1e4


def rmsnorm(x, g):
    xf = x.astype(jnp.float32)
    y = xf * lax.rsqrt(jnp.mean(xf * xf, axis=-1, keepdims=True) + EPS)
    return (y * g.astype(jnp.float32)).astype(x.dtype)

def partial_rope(x):
    S = x.shape[1]
    pos = jnp.arange(S, dtype=jnp.float32)
    inv = ROPE_THETA_2 ** (-jnp.arange(0, ROT_DIM, 2, dtype=jnp.float32) / ROT_DIM)
    ang = pos[:, None] * inv[None, :]
    cos = jnp.cos(ang)[None, :, None, :]
    sin = jnp.sin(ang)[None, :, None, :]
    xr = x[..., :ROT_DIM].astype(jnp.float32)
    x1, x2 = xr[..., :ROT_DIM // 2], xr[..., ROT_DIM // 2:]
    rot = jnp.concatenate([x1 * cos - x2 * sin, x2 * cos + x1 * sin], axis=-1).astype(x.dtype)
    return jnp.concatenate([rot, x[..., ROT_DIM:]], axis=-1)

def masked_softmax(s, mask, axis=-1):
    s = jnp.where(mask, s.astype(jnp.float32), -jnp.inf)
    m = jnp.max(s, axis=axis, keepdims=True)
    m = jnp.where(jnp.isfinite(m), m, 0.0)
    e = jnp.where(mask, jnp.exp(s - m), 0.0)
    d = jnp.sum(e, axis=axis, keepdims=True)
    return e / jnp.maximum(d, 1e-30)

def short_conv_layer(x, norm_g, w_in, conv_w, w_out):
    S = x.shape[1]
    h = rmsnorm(x, norm_g)
    proj = h @ w_in
    b, c, u, z = jnp.split(proj, 4, axis=-1)
    vp = jnp.pad(c * u, ((0, 0), (CONV_WIDTH - 1, 0), (0, 0)))
    conv = conv_w[0] * vp[:, 0:S]
    for k in range(1, CONV_WIDTH):
        conv = conv + conv_w[k] * vp[:, k:k + S]
    y = b * conv * jax.nn.silu(z)
    return x + y @ w_out

def compress_blocks(kv, pos_emb, w1, w2):
    B, S, G, D = kv.shape
    chunks = kv.reshape(B, S // CMP_STRIDE, CMP_STRIDE, G, D)
    n_cmp = S // CMP_STRIDE - CMP_R + 1
    blocks = jnp.concatenate([chunks[:, r:r + n_cmp] for r in range(CMP_R)], axis=2)
    blocks = blocks + pos_emb[None, None, :, None, :]
    flat = blocks.transpose(0, 1, 3, 2, 4).reshape(B, n_cmp, G, CMP_BLOCK * D)
    return jax.nn.gelu(flat @ w1) @ w2

def shared_kv(h, norm_g, w_kv, cmp_pos_k, cmp_w1_k, cmp_w2_k, cmp_pos_v, cmp_w1_v, cmp_w2_v):
    B, S, _ = h.shape
    kv = (rmsnorm(h, norm_g) @ w_kv).reshape(B, S, N_KV_STREAMS, N_KV_GROUPS, HEAD_DIM)
    k_c, v_c, k_s, v_s, k_w, v_w = [kv[:, :, i] for i in range(N_KV_STREAMS)]
    k_cmp = compress_blocks(k_c, cmp_pos_k, cmp_w1_k, cmp_w2_k)
    v_cmp = compress_blocks(v_c, cmp_pos_v, cmp_w1_v, cmp_w2_v)
    return (k_cmp, v_cmp, partial_rope(k_s), v_s, partial_rope(k_w), v_w)

def nsa_attention(q, q_rot, gates, k_cmp, v_cmp, k_slc, v_slc, k_win, v_win):
    B, S, H, D = q.shape
    G, I = N_KV_GROUPS, HEADS_PER_GROUP
    n_blk = S // Q_BLOCK_2
    n_cmp = k_cmp.shape[1]
    n_sb = S // SLC_BLOCK
    n_sel = min(N_SELECT, n_sb)
    scale = HEAD_DIM ** -0.5
    cmp_end = jnp.arange(n_cmp) * CMP_STRIDE + CMP_BLOCK - 1
    kb_slc = k_slc.reshape(B, n_sb, SLC_BLOCK, G, D).transpose(0, 3, 1, 2, 4)
    vb_slc = v_slc.reshape(B, n_sb, SLC_BLOCK, G, D).transpose(0, 3, 1, 2, 4)
    k_win_p = jnp.pad(k_win, ((0, 0), (WINDOW, 0), (0, 0), (0, 0)))
    v_win_p = jnp.pad(v_win, ((0, 0), (WINDOW, 0), (0, 0), (0, 0)))
    bi = jnp.arange(B)[:, None, None, None]
    gi = jnp.arange(G)[None, None, :, None]
    blk_ids = jnp.arange(n_sb)

    def to_blocks(a):
        return a.reshape(B, n_blk, Q_BLOCK_2, G, I, a.shape[-1]).transpose(1, 0, 2, 3, 4, 5)

    def block_fn(args):
        blk, qc, qr, g = args
        start = blk * Q_BLOCK_2
        t = start + jnp.arange(Q_BLOCK_2)

        s_c = jnp.einsum('bqgid,bngd->bqgin', qc, k_cmp) * scale
        m_c = (cmp_end[None, :] <= t[:, None])[None, :, None, None, :]
        p_c = masked_softmax(s_c, m_c)
        o_c = jnp.einsum('bqgin,bngd->bqgid', p_c.astype(v_cmp.dtype), v_cmp)

        p_grp = jnp.pad(p_c.sum(axis=3), ((0, 0), (0, 0), (0, 0), (CMP_R - 1, CMP_R - 1)))
        imp = 0.0
        for m in range(SLC_RATIO):
            for n in range(CMP_R):
                off = CMP_R - 1 + m - n
                imp = imp + p_grp[..., off:off + SLC_RATIO * (n_sb - 1) + 1:SLC_RATIO]
        cur = t // SLC_BLOCK
        valid = blk_ids[None, :] <= cur[:, None]
        forced = (blk_ids[None, :] == 0) | (valid & (blk_ids[None, :] > cur[:, None] - N_LOCAL))
        score = jnp.where(forced[None, :, None, :], FORCE_SCORE, imp)
        score = jnp.where(valid[None, :, None, :], score, -jnp.inf)
        top_s, idx = lax.top_k(score, n_sel)
        sel_ok = jnp.isfinite(top_s)

        kg = kb_slc[bi, gi, idx]
        vg = vb_slc[bi, gi, idx]
        s_s = jnp.einsum('bqgid,bqgnld->bqginl', qr, kg) * scale
        kpos = idx[..., None] * SLC_BLOCK + jnp.arange(SLC_BLOCK)
        m_s = sel_ok[..., None] & (kpos <= t[None, :, None, None, None])
        p_s = masked_softmax(s_s.reshape(B, Q_BLOCK_2, G, I, n_sel * SLC_BLOCK),
                             m_s.reshape(B, Q_BLOCK_2, G, 1, n_sel * SLC_BLOCK))
        p_s = p_s.reshape(B, Q_BLOCK_2, G, I, n_sel, SLC_BLOCK).astype(vg.dtype)
        o_s = jnp.einsum('bqginl,bqgnld->bqgid', p_s, vg)

        kw = lax.dynamic_slice_in_dim(k_win_p, start, WINDOW + Q_BLOCK_2, axis=1)
        vw = lax.dynamic_slice_in_dim(v_win_p, start, WINDOW + Q_BLOCK_2, axis=1)
        kpos_w = start - WINDOW + jnp.arange(WINDOW + Q_BLOCK_2)
        m_w = ((kpos_w[None, :] <= t[:, None]) & (kpos_w[None, :] > t[:, None] - WINDOW)
               & (kpos_w[None, :] >= 0))
        s_w = jnp.einsum('bqgid,bkgd->bqgik', qr, kw) * scale
        p_w = masked_softmax(s_w, m_w[None, :, None, None, :]).astype(vw.dtype)
        o_w = jnp.einsum('bqgik,bkgd->bqgid', p_w, vw)

        return g[..., 0:1] * o_c + g[..., 1:2] * o_s + g[..., 2:3] * o_w

    xs = (jnp.arange(n_blk), to_blocks(q), to_blocks(q_rot), to_blocks(gates))
    out = lax.map(block_fn, xs)
    return out.transpose(1, 0, 2, 3, 4, 5).reshape(B, S, H, D)

def nsa_layer(x, kvs, norm_g, w_in, w_out):
    B, S, _ = x.shape
    h = rmsnorm(x, norm_g)
    proj = h @ w_in
    q = proj[..., :ATTN_D].reshape(B, S, N_HEADS, HEAD_DIM)
    gates = jax.nn.sigmoid(proj[..., ATTN_D:ATTN_D + N_HEADS * N_BRANCH]
                           .reshape(B, S, N_HEADS, N_BRANCH))
    z = proj[..., ATTN_D + N_HEADS * N_BRANCH:]
    o = nsa_attention(q, partial_rope(q), gates, *kvs)
    y = o.reshape(B, S, ATTN_D) * jax.nn.silu(z)
    return x + y @ w_out

def second_inputs(seed: int = 0) -> dict:
    key = jax.random.key(seed)
    ks = jax.random.split(key, 20)
    f = jnp.float32
    nrm = lambda k, shape, s: jax.random.normal(k, shape, f) * s
    gain = lambda k, shape: 1.0 + 0.01 * jax.random.normal(k, shape, f)
    b_in_cols = ATTN_D + N_HEADS * N_BRANCH + ATTN_D
    return {
        "x": jax.random.normal(ks[0], (BATCH, SEQ, D_MODEL), f),
        "a_norm": gain(ks[1], (N_A_LAYERS, D_MODEL)),
        "a_w_in": nrm(ks[2], (N_A_LAYERS, D_MODEL, 4 * CONV_D), D_MODEL ** -0.5),
        "a_conv_w": nrm(ks[3], (N_A_LAYERS, CONV_WIDTH, CONV_D), CONV_WIDTH ** -0.5),
        "a_w_out": nrm(ks[4], (N_A_LAYERS, CONV_D, D_MODEL), CONV_D ** -0.5),
        "kv_norm": gain(ks[5], (D_MODEL,)),
        "w_kv": nrm(ks[6], (D_MODEL, N_KV_STREAMS * KV_D), D_MODEL ** -0.5),
        "cmp_pos_k": nrm(ks[7], (CMP_BLOCK, HEAD_DIM), 0.1),
        "cmp_w1_k": nrm(ks[8], (CMP_BLOCK * HEAD_DIM, CMP_HIDDEN), (CMP_BLOCK * HEAD_DIM) ** -0.5),
        "cmp_w2_k": nrm(ks[9], (CMP_HIDDEN, HEAD_DIM), CMP_HIDDEN ** -0.5),
        "cmp_pos_v": nrm(ks[10], (CMP_BLOCK, HEAD_DIM), 0.1),
        "cmp_w1_v": nrm(ks[11], (CMP_BLOCK * HEAD_DIM, CMP_HIDDEN), (CMP_BLOCK * HEAD_DIM) ** -0.5),
        "cmp_w2_v": nrm(ks[12], (CMP_HIDDEN, HEAD_DIM), CMP_HIDDEN ** -0.5),
        "b_norm": gain(ks[13], (N_B_LAYERS, D_MODEL)),
        "b_w_in": nrm(ks[14], (N_B_LAYERS, D_MODEL, b_in_cols), D_MODEL ** -0.5),
        "b_w_out": nrm(ks[15], (N_B_LAYERS, ATTN_D, D_MODEL), ATTN_D ** -0.5),
        "final_norm": gain(ks[16], (D_MODEL,)),
    }

def second_block(x, a_norm, a_w_in, a_conv_w, a_w_out, kv_norm, w_kv, cmp_pos_k, cmp_w1_k,
              cmp_w2_k, cmp_pos_v, cmp_w1_v, cmp_w2_v, b_norm, b_w_in, b_w_out, final_norm):
    h = x
    kvs = None
    for layer in range(DEPTH_2):
        if layer < N_A_LAYERS:
            h = short_conv_layer(h, a_norm[layer], a_w_in[layer], a_conv_w[layer], a_w_out[layer])
        else:
            if layer == N_A_LAYERS:
                kvs = shared_kv(h, kv_norm, w_kv, cmp_pos_k, cmp_w1_k, cmp_w2_k,
                                cmp_pos_v, cmp_w1_v, cmp_w2_v)
            j = layer - N_A_LAYERS
            h = nsa_layer(h, kvs, b_norm[j], b_w_in[j], b_w_out[j])
    return rmsnorm(h, final_norm)


def setup_inputs(seed=0):
    out = dict(first_inputs(seed))
    for name, value in second_inputs(seed + 1).items():
        if name != "x":
            out[name + "_2"] = value
    return out


def reference(
    x, c, ada_w, ada_b, norm1_g, w_in, mla_q_lat_g, mla_w_q_up, mla_kv_lat_g, mla_w_kv_up,
    mla_q_g, mla_k_g, diff_q_g, diff_k_g, diff_lq1, diff_lk1, diff_lq2, diff_lk2, diff_subln_g,
    w_out, norm2_g, peer_w_q, peer_sub_keys, peer_u, peer_v, a_norm_2, a_w_in_2, a_conv_w_2,
    a_w_out_2, kv_norm_2, w_kv_2, cmp_pos_k_2, cmp_w1_k_2, cmp_w2_k_2, cmp_pos_v_2, cmp_w1_v_2,
    cmp_w2_v_2, b_norm_2, b_w_in_2, b_w_out_2, final_norm_2,
):
    x = first_block(
        x, c, ada_w, ada_b, norm1_g, w_in, mla_q_lat_g, mla_w_q_up, mla_kv_lat_g, mla_w_kv_up,
        mla_q_g, mla_k_g, diff_q_g, diff_k_g, diff_lq1, diff_lk1, diff_lq2, diff_lk2,
        diff_subln_g, w_out, norm2_g, peer_w_q, peer_sub_keys, peer_u, peer_v,
    )
    return second_block(
        x, a_norm_2, a_w_in_2, a_conv_w_2, a_w_out_2, kv_norm_2, w_kv_2, cmp_pos_k_2,
        cmp_w1_k_2, cmp_w2_k_2, cmp_pos_v_2, cmp_w1_v_2, cmp_w2_v_2, b_norm_2, b_w_in_2,
        b_w_out_2, final_norm_2,
    )


_drawn_inputs = setup_inputs


def setup_inputs(seed=0):
    import zlib

    import numpy as np

    out = dict(_drawn_inputs(seed))
    spreads = {}
    factors = {'norm1_g': 8.0,
     'mla_q_lat_g': 8.0,
     'mla_w_q_up': 3.76,
     'mla_kv_lat_g': 8.0,
     'mla_q_g': 8.0,
     'mla_k_g': 8.0,
     'diff_q_g': 8.0,
     'diff_k_g': 8.0,
     'diff_lq1': 62.761,
     'diff_lk1': 6.235,
     'diff_lq2': 5.731,
     'diff_lk2': 2.947,
     'diff_subln_g': 8.0,
     'norm2_g': 8.0,
     'a_norm_2': 5.342,
     'kv_norm_2': 64.0,
     'cmp_pos_k_2': 58.207,
     'cmp_pos_v_2': 30.624,
     'b_norm_2': 64.0,
     'final_norm_2': 29.814}
    for name, (base, spread) in spreads.items():
        noise = np.random.default_rng([zlib.crc32(name.encode()), seed]).standard_normal(out[name].shape)
        drawn = base * np.exp(spread * noise) if base else spread * noise
        out[name] = __import__('jax').numpy.asarray(drawn.astype(out[name].dtype))
    for name, factor in factors.items():
        out[name] = (out[name] * factor).astype(out[name].dtype)
    return out
```

```python
from contextlib import ExitStack

import numpy as np

import concourse.bass as bass
from concourse import mybir

ALU = mybir.AluOpType
ACT = mybir.ActivationFunctionType
F32 = mybir.dt.float32
U32 = mybir.dt.uint32
AX_X = mybir.AxisListType.X

P = 128
S = 512
TB = S // P
D = 1024
DC = D // P
EPS = 1e-6
NEG = -1e30

MLA_H, NOPE, ROPE, MLA_V, Q_LORA, KV_LORA = 4, 128, 64, 128, 384, 256
QC, KVC = Q_LORA // P, KV_LORA // P
DIFF_H, DIFF_DQK = 4, 64
LAMBDA_INIT = 0.2
PEER_H, NKEYS, TOPK = 8, 128, 16
HP = PEER_H * 2
HK = PEER_H * TOPK
CONV_D = 2048
CC = CONV_D // P
NSA_H, GROUPS, HD = 16, 4, 64
CMP_BLOCK, CMP_STRIDE, CMP_HID = 32, 16, 256
NCMP = S // CMP_STRIDE - 1
NCP = NCMP + 1
CMP_PAIRS = CMP_BLOCK // 2
SLC_BLOCK, N_SELECT, WINDOW = 64, 16, 512
assert S // SLC_BLOCK <= N_SELECT and WINDOW >= S

ARENA = 22600
SLOT = 1024
SLOTS = 14
GT = 64
EG = 8

COLS = {}
_at = 0
for _name, _n in (("c", 8), ("ada_b", 48), ("norm1", 8), ("norm2", 8), ("a_norm", 8), ("kv_norm", 8),
                  ("b_norm", 8), ("final", 8), ("q_lat", 3), ("kv_lat", 2), ("q_nope", 1), ("q_pe", 1),
                  ("k_nope", 1), ("k_pe", 1), ("dq", 1), ("dk", 1), ("subln", 1), ("conv", 48),
                  ("lam_q", 2), ("lam_k", 2)):
    COLS[_name] = (_at, _at + _n)
    _at += _n
NCOLS = _at

EPS_N = (D, Q_LORA, KV_LORA, P, 64)

CONSTS = {}
_at = 0
for _name, _n in (("ident", P), ("ones", P), ("ones64", P), ("rot64", P), ("rot16", P), ("iota", P),
                  ("mask", P), ("cos64", S), ("sin64", S), ("cos16", S), ("sin16", S),
                  ("cmp_add", TB * NCP), ("cmp_mul", TB * NCP), ("eps", len(EPS_N))):
    CONSTS[_name] = (_at, _at + _n)
    _at += _n
NCONSTS = _at


class Line:

    def __init__(self, sem, chained):
        self.sem, self.chained, self.count, self.steps, self.waited = sem, chained, 0, [], {}

    def wait(self, *marks):
        for sem, value in marks:
            if self.waited.get(sem.name, 0) < value:
                self.waited[sem.name] = value
                self.steps.append(lambda e, s=sem, v=value: e.wait_ge(s, v))

    def do(self, emit, *marks):
        self.wait(*marks)
        if self.chained and self.count:
            self.wait((self.sem, self.count))
        self.count += 1
        self.steps.append(lambda e: emit(e).then_inc(self.sem, 1))
        return self.sem, self.count

    @property
    def last(self):
        return self.sem, self.count

    def run(self, engine):
        for step in self.steps:
            step(engine)


class Ring:

    def __init__(self, items):
        self.items, self.freed, self.turn = items, [()] * len(items), 0

    def take(self):
        k = self.turn % len(self.items)
        self.turn += 1
        marks, self.freed[k] = self.freed[k], None
        assert marks is not None, "a buffer is taken before it is freed"
        return k, self.items[k], marks

    def free(self, k, *marks):
        self.freed[k] = marks


def build(nc, ins, out):
    ctx = ExitStack()
    with ctx:
        def sem(name):
            return ctx.enter_context(nc.semaphore(name))

        def sb(name, shape, dt=F32):
            return ctx.enter_context(nc.sbuf_tensor(name, shape, dt))

        gates_dram = nc.dram_tensor("gates_scratch", [NKEYS, P, S], F32, kind="Internal").ap()

        consts = sb("consts", [P, NCONSTS])
        cols = sb("cols", [P, NCOLS])
        res = sb("res", [P, DC, S])
        act = sb("act", [P, DC, S])
        ring_mem = sb("ring_mem", [P, SLOTS, SLOT])
        mod = sb("mod", [P, 48])
        silu_c = sb("silu_c", [P, DC])
        gains = sb("gains", [P, 64])
        rstd_mem = sb("rstd_mem", [P, 2, S])
        sq_mem = sb("sq_mem", [P, 2, S])
        small = sb("small", [P, 8, 4])
        lam = sb("lam", [P, 8])
        newton = sb("newton", [P, S])[:, :]
        arena = sb("arena", [P, ARENA])
        banks_mem = ctx.enter_context(nc.psum_tensor("banks", [P, 8, 512], F32))

        def const(name):
            a, b = CONSTS[name]
            return consts[:, a:b]

        def col(name, i=0, n=1):
            a = COLS[name][0] + i
            return cols[:, a:a + n]

        pe = Line(sem("pe_done"), False)
        dve = Line(sem("dve_done"), True)
        act_e = Line(sem("act_done"), True)
        pool = Line(sem("pool_done"), True)
        sync = Line(sem("sync_unused"), False)
        slot_sems = [sem(f"slot{k}_loaded") for k in range(SLOTS)]
        slot_loads = [0] * SLOTS
        slots = Ring([ring_mem[:, k, :] for k in range(SLOTS)])
        banks = Ring([banks_mem[:, k, :] for k in range(6)])
        o_banks = Ring([banks_mem[:, k, :] for k in (6, 7)])
        rstds = Ring([rstd_mem[:, k, :] for k in range(2)])
        squares = Ring([sq_mem[:, k, :] for k in range(2)])

        def load(dst, src, s, n, *marks):
            sync.wait(*marks)
            sync.steps.append(lambda e: e.dma_start(dst, src).then_inc(s, 16))
            return s, 16 * n

        def fetch(src):
            k, tile, freed = slots.take()
            n = src.shape[1]
            slot_loads[k] += 1
            return k, tile[:, 0:n], load(tile[:, 0:n], src, slot_sems[k], slot_loads[k], *freed)

        def fence(*lines):
            for line in lines or (pe, dve, act_e, pool, sync):
                line.wait(*[x.last for x in (pe, dve, act_e, pool) if x is not line and x.count])

        def eps_col(n):
            return const("eps")[:, EPS_N.index(n):EPS_N.index(n) + 1]

        def mm(out_, pairs, *marks, start=True, stop=True):
            def emit(e):
                for n, (a, b) in enumerate(pairs):
                    last = e.matmul(out_, a, b, start=start and n == 0, stop=stop and n == len(pairs) - 1)
                return last
            return pe.do(emit, *marks)

        def linear(src, kc, acts, ready, m=P):
            k, w, loaded = fetch(src)
            b, bank, freed = banks.take()
            w = w.rearrange("p (c n) -> p c n", c=kc)
            done = mm(bank, [(w[:, c, :], acts[c]) for c in range(kc)], loaded, *freed, *ready)
            slots.free(k, done)
            return b, bank, done

        def linear_tokens(srcs, kc, per, acts, ready):
            got = [banks.take() for _ in range(TB)]
            done = None
            for s_, src in enumerate(srcs):
                k, w, loaded = fetch(src)
                w = w.rearrange("p (c n) -> p c n", c=per)
                for tb in range(TB):
                    pairs = [(acts[s_ * per + c][:, tb * P:(tb + 1) * P], w[:, c, :]) for c in range(per)]
                    done = mm(got[tb][1], pairs, loaded, *ready, *(got[tb][2] if s_ == 0 else ()),
                              start=s_ == 0, stop=s_ == len(srcs) - 1)
                slots.free(k, done)
            return [(g[0], g[1]) for g in got], done

        def rstd_of(chunks, ones, n, ready):
            b, bank, freed = banks.take()
            for i, x in enumerate(chunks):
                k, sq, sq_freed = squares.take()
                squared = act_e.do(lambda e, sq=sq, x=x: e.activation(sq, x, ACT.Square), *ready, *sq_freed)
                done = mm(bank, [(ones, sq)], squared, *(freed if i == 0 else ()), start=i == 0,
                          stop=i == len(chunks) - 1)
                squares.free(k, done)
            k, r, r_freed = rstds.take()
            root = act_e.do(lambda e: e.activation(r, bank, ACT.Sqrt, bias=eps_col(n)), done, *r_freed)
            dve.do(lambda e: e.reciprocal(r, r), root)
            dve.do(lambda e: e.tensor_tensor(newton, r, r, ALU.mult))
            m = dve.do(lambda e: e.scalar_tensor_tensor(newton, bank, n * EPS, newton, ALU.add, ALU.mult))
            banks.free(b, m)
            dve.do(lambda e: e.tensor_scalar(newton, newton, -0.5, 1.5, ALU.mult, ALU.add))
            made = dve.do(lambda e: e.tensor_tensor(r, r, newton, ALU.mult))
            return k, r, made

        def scaled(dst, x, gain, r, ready):
            return dve.do(lambda e: e.scalar_tensor_tensor(dst, x, gain, r, ALU.mult, ALU.mult), *ready)

        def norm_model(dst, gain, shift, ready):
            k, r, made = rstd_of([res[:, c, :] for c in range(DC)], const("ones"), D, ready)
            marks = []
            for c in range(DC):
                m = scaled(dst[:, c, :], res[:, c, :], gain[:, c:c + 1], r, (made,))
                if shift is not None:
                    m = act_e.do(lambda e, c=c: e.activation(dst[:, c, :], dst[:, c, :], ACT.Identity,
                                                             bias=shift[:, c:c + 1]), m)
                marks.append(m)
            rstds.free(k, dve.last)
            return marks

        def normed(dst, bank, ones, n, gain, done):
            k, r, made = rstd_of([bank], ones, n, (done,))
            m = scaled(dst, bank, gain, r, (made,))
            rstds.free(k, m)
            return m

        def rope(parts, x, rot, cos, sin, tmp, ready):
            b, bank, freed = banks.take()
            turned = mm(bank, [(rot, x)], ready, *freed)
            made = pool.do(lambda e: e.tensor_tensor(tmp[0], x, cos, ALU.mult), ready, dve.last)
            m = dve.do(lambda e: e.tensor_tensor(tmp[1], bank, sin, ALU.mult), turned)
            banks.free(b, m)
            for dst, rows in parts:
                m = dve.do(lambda e, dst=dst, rows=rows: e.tensor_tensor(dst, tmp[0][rows, :], tmp[1][rows, :],
                                                                         ALU.add), made)
            return m

        s_x, s_cols, s_consts = sem("x_loaded"), sem("cols_loaded"), sem("consts_loaded")
        cols_in = load(cols[:, :], ins["cols"], s_cols, 1)
        consts_in = load(consts[:, :], ins["consts"], s_consts, 1)
        x_in = load(res[:, :, :].rearrange("p c t -> p (c t)"), ins["x"], s_x, 1)

        spans = {}
        at = 0
        for name, n, factor in (("norm1", 8, D ** 0.5), ("norm2", 8, D ** 0.5), ("a_norm", 8, D ** 0.5),
                                ("kv_norm", 8, D ** 0.5), ("b_norm", 8, D ** 0.5), ("final", 8, D ** 0.5),
                                ("q_lat", 3, Q_LORA ** 0.5), ("kv_lat", 2, KV_LORA ** 0.5),
                                ("q_nope", 1, NOPE ** 0.5 * (NOPE + ROPE) ** -0.5),
                                ("q_pe", 1, ROPE ** 0.5 * (NOPE + ROPE) ** -0.5),
                                ("k_nope", 1, NOPE ** 0.5), ("k_pe", 1, ROPE ** 0.5),
                                ("dq", 1, 1.0), ("dk", 1, DIFF_DQK ** 0.5),
                                ("subln", 1, P ** 0.5 * (1.0 - LAMBDA_INIT))):
            g = gains[:, at:at + n]
            spans[name] = g
            dve.do(lambda e, g=g, name=name, n=n, f=factor: e.tensor_scalar(g, col(name, 0, n), f, None, ALU.mult),
                   cols_in)
            at += n

        silu_done = act_e.do(lambda e: e.activation(silu_c[:, :], col("c", 0, 8), ACT.Silu), cols_in)

        def modulation(first, n):
            b, bank, freed = banks.take()
            for j in range(first, first + n):
                k, w, loaded = fetch(ins["ada_w"][j])
                w = w.rearrange("p (c n) -> p c n", c=DC)
                done = mm(bank[:, j:j + 1], [(w[:, c, :], silu_c[:, c:c + 1]) for c in range(DC)],
                          loaded, silu_done, *freed)
                freed = ()
                slots.free(k, done)
            m = dve.do(lambda e: e.tensor_tensor(mod[:, first:first + n], bank[:, first:first + n],
                                                 col("ada_b", first, n), ALU.add), done)
            banks.free(b, m)
            return m

        def modulated_gain(dst, scale_at):
            return dve.do(lambda e: e.scalar_tensor_tensor(dst, mod[:, scale_at:scale_at + 8], 1.0, dst,
                                                           ALU.add, ALU.mult))

        modulation(0, 16)
        ready = modulated_gain(spans["norm1"], 8)
        acts = [act[:, c, :] for c in range(DC)]
        h_ready = norm_model(act, spans["norm1"], mod[:, 0:8], (x_in, consts_in, ready))

        pos = [0]

        def view(n, *dims):
            a = arena[:, pos[0]:pos[0] + n]
            pos[0] += n
            assert pos[0] <= ARENA, pos[0]
            if len(dims) == 2:
                return a.rearrange("p (a b) -> p a b", a=dims[0])
            if len(dims) == 3:
                return a.rearrange("p (a b c) -> p a b c", a=dims[0], b=dims[1])
            return a

        q_nope = view(4 * S, 4, S)
        q_pe = view(2 * S, 2, S)
        k_nope = view(4 * S, 4, S)
        k_pe = view(2 * S, 2, S)
        v_mla = view(TB * S, TB, S)
        q_diff = view(4 * S, 4, S)
        k_diff = view(8 * S, 8, S)
        v_diff = view(TB * S, TB, S)
        lat = view(3 * S, 3, S)
        normed_tmp = view(S)
        rope_tmp = (view(S), view(S))
        halves = (slice(0, 64), slice(64, 128))

        for h in range(2):
            pool.do(lambda e, h=h: e.memset(k_pe[halves[1 - h], h, :], 0.0))
        for h in range(8):
            pool.do(lambda e, h=h: e.memset(k_diff[halves[1 - h % 2], h, :], 0.0))

        w_in = iter(range(14))

        def latent(n, gain):
            for c in range(n):
                b, bank, done = linear(ins["w_in"][next(w_in)], DC, acts, h_ready)
                m = act_e.do(lambda e, c=c, bank=bank: e.activation(lat[:, c, :], bank, ACT.Copy), done, pe.last)
                banks.free(b, m)
            k, r, made = rstd_of([lat[:, c, :] for c in range(n)], const("ones"), n * P, (m,))
            for c in range(n):
                m = scaled(lat[:, c, :], lat[:, c, :], gain[:, c:c + 1], r, (made,))
            rstds.free(k, m)
            return m

        lat_ready = latent(KVC, spans["kv_lat"])
        lats = [lat[:, c, :] for c in range(QC)]
        for h in range(MLA_H):
            b, bank, done = linear(ins["kv_up"][h], KVC, lats, (lat_ready,))
            banks.free(b, normed(k_nope[:, h, :], bank, const("ones"), NOPE, spans["k_nope"], done))
        got, done = linear_tokens([ins["kv_up_v"]], KVC, KVC, lats, (lat_ready,))
        for tb, (b, bank) in enumerate(got):
            banks.free(b, act_e.do(lambda e, tb=tb, bank=bank: e.activation(v_mla[:, tb, :], bank, ACT.Copy), done))

        def rotated(b, bank, done, ones, gain, parts, rot, cos, sin):
            m = normed(normed_tmp, bank, ones, DIFF_DQK, gain, done)
            banks.free(b, m)
            return rope(parts, normed_tmp, rot, cos, sin, rope_tmp, m)

        rope64 = (const("rot64"), const("cos64"), const("sin64"))
        b, bank, done = linear(ins["w_in"][next(w_in)], DC, acts, h_ready)
        rotated(b, bank, done, const("ones64"), spans["k_pe"],
                [(k_pe[halves[j], j, :], halves[j]) for j in range(2)], *rope64)
        lat_ready = latent(QC, spans["q_lat"])
        for h in range(MLA_H):
            b, bank, done = linear(ins["q_up"][h], QC, lats, (lat_ready,))
            banks.free(b, normed(q_nope[:, h, :], bank, const("ones"), NOPE, spans["q_nope"], done))
        for j in range(2):
            b, bank, done = linear(ins["q_up"][MLA_H + j], QC, lats, (lat_ready,))
            rotated(b, bank, done, const("ones64"), spans["q_pe"], [(q_pe[:, j, :], slice(0, P))], *rope64)
        for h in range(DIFF_H):
            b, bank, done = linear(ins["w_in"][next(w_in)], DC, acts, h_ready)
            rotated(b, bank, done, const("ones64"), spans["dq"], [(q_diff[:, h, :], slice(0, P))], *rope64)
        for h in range(DIFF_H):
            b, bank, done = linear(ins["w_in"][next(w_in)], DC, acts, h_ready)
            rotated(b, bank, done, const("ones64"), spans["dk"],
                    [(k_diff[halves[j], 2 * h + j, :], halves[j]) for j in range(2)], *rope64)
        got, done = linear_tokens([ins["w_dv"][i] for i in range(4)], DC, 2, acts, h_ready)
        for tb, (b, bank) in enumerate(got):
            banks.free(b, act_e.do(lambda e, tb=tb, bank=bank: e.activation(v_diff[:, tb, :], bank, ACT.Copy), done))

        dve.do(lambda e: e.tensor_tensor(lam[:, 0:2], col("lam_q", 0, 2), col("lam_k", 0, 2), ALU.mult))
        b, bank, freed = banks.take()
        done = mm(bank[:, 0:2], [(const("ones"), lam[:, 0:2])], dve.last, *freed)
        m = act_e.do(lambda e, bank=bank: e.activation(lam[:, 2:4], bank[:, 0:2], ACT.Exp), done)
        banks.free(b, m)
        dve.do(lambda e: e.tensor_tensor(lam[:, 4:5], lam[:, 3:4], lam[:, 2:3], ALU.subtract), m)
        dve.do(lambda e: e.tensor_scalar(lam[:, 5:6], lam[:, 4:5], -LAMBDA_INIT, None, ALU.add))
        neg_lam = lam[:, 5:6]

        fence(act_e, dve)
        pos[0] -= 6 * S
        probs = Ring([view(S) for _ in range(4)])
        transposed = Ring([view(TB * S, TB, S) for _ in range(2)])
        stats = Ring([small[:, k, :] for k in range(8)])

        def softmax_rows(score_pairs, qb, out_scale):
            w = (qb + 1) * P
            b, bank, freed = banks.take()

            def emit(e):
                for n, (q, k) in enumerate(score_pairs):
                    e.matmul(bank[:, 0:w], q[:, qb * P:w], k[:, 0:w], start=n == 0, stop=False)
                return e.matmul(bank[:, w - P:w], const("ident"), const("mask"), start=False, stop=True)
            scored = pe.do(emit, *freed)
            sk, st, st_freed = stats.take()
            maxed = dve.do(lambda e: e.tensor_reduce(st[:, 0:1], bank[:, 0:w], AX_X, ALU.max, negate=True),
                           scored, *st_freed)
            pk, p, p_freed = probs.take()
            exped = act_e.do(lambda e: e.activation(p[:, 0:w], bank[:, 0:w], ACT.Exp, bias=st[:, 0:1],
                                                    scale=1.0, accum_out=st[:, 1:2]), maxed, *p_freed)
            banks.free(b, exped)
            return (pk, p, sk, st, exped)

        def transpose_rows(p, qb, dst, ready, freed, on):
            b, bank, b_freed = banks.take()

            def emit(e):
                for kb in range(qb + 1):
                    last = e.transpose(bank[:, kb * P:(kb + 1) * P], p[:, kb * P:(kb + 1) * P], const("ident"))
                return last
            turned = pe.do(emit, ready, *b_freed)
            src = bank[:, 0:(qb + 1) * P].rearrange("p (k q) -> p k q", q=P)
            to = dst[:, 0:qb + 1, qb * P:(qb + 1) * P]
            if on is dve:
                m = dve.do(lambda e: e.tensor_copy(to, src), turned, *freed)
            else:
                m = act_e.do(lambda e: e.activation(to, src, ACT.Copy), turned, *freed)
            banks.free(b, m)
            return turned, m

        def values_mm(out_, v, turned, ready, first, last, *freed):
            def emit(e):
                for kb in range(TB):
                    x = e.matmul(out_[:, kb * P:S], v(kb), turned[:, kb, kb * P:S], start=first and kb == 0,
                                 stop=last and kb == TB - 1)
                return x
            return pe.do(emit, *ready, *freed)

        mixed = act
        state = {}

        def front(h, qb):
            if h < MLA_H:
                pk, p, sk, st, exped = softmax_rows(
                    [(q_nope[:, h, :], k_nope[:, h, :]), (q_pe[:, h // 2, :], k_pe[:, h % 2, :])], qb, None)
                dve.do(lambda e: e.reciprocal(st[:, 2:3], st[:, 1:2]), exped)
                w = (qb + 1) * P
                m = dve.do(lambda e: e.tensor_scalar(p[:, 0:w], p[:, 0:w], st[:, 2:3], None, ALU.mult))
                stats.free(sk, m)
                return (pk, p, m, ())
            h -= MLA_H
            w = (qb + 1) * P
            pk, p, sk, st, exped = softmax_rows([(q_diff[:, h, :], k_diff[:, 2 * h, :])], qb, None)
            pk2, p2, sk2, st2, exped2 = softmax_rows([(q_diff[:, h, :], k_diff[:, 2 * h + 1, :])], qb, None)
            dve.do(lambda e: e.reciprocal(st[:, 2:3], st[:, 1:2]), exped)
            m = dve.do(lambda e: e.tensor_scalar(p[:, 0:w], p[:, 0:w], st[:, 2:3], None, ALU.mult))
            stats.free(sk, m)
            dve.do(lambda e: e.reciprocal(st2[:, 2:3], st2[:, 1:2]), exped2)
            dve.do(lambda e: e.tensor_tensor(st2[:, 3:4], st2[:, 2:3], neg_lam, ALU.mult))
            m = dve.do(lambda e: e.scalar_tensor_tensor(p[:, 0:w], p2[:, 0:w], st2[:, 3:4], p[:, 0:w],
                                                        ALU.mult, ALU.add))
            stats.free(sk2, m)
            probs.free(pk2, m)
            return (pk, p, m, ())

        def back(h, qb, unit):
            pk, p, ready, _ = unit
            if qb == 0:
                state["t"] = transposed.take()
            tk, t, t_freed = state["t"]
            turned, m = transpose_rows(p, qb, t, ready, t_freed, act_e if qb % 2 else dve)
            state[qb] = m
            probs.free(pk, turned)
            if qb < TB - 1:
                return
            b, bank, freed = o_banks.take()
            hd = h % 4
            v = v_mla if h < MLA_H else v_diff
            done = values_mm(bank, lambda kb: v[:, kb, hd * P:(hd + 1) * P], t, [state[q] for q in range(TB)],
                             True, True, *freed)
            transposed.free(tk, done)
            if h < MLA_H:
                m = act_e.do(lambda e: e.activation(mixed[:, h, :], bank, ACT.Copy), done)
            else:
                m = normed(mixed[:, h, :], bank, const("ones"), P, spans["subln"], done)
            o_banks.free(b, m)
            state.setdefault("mixed", []).append(m)

        fence(pe)
        units = [(h, qb) for h in range(MLA_H + DIFF_H) for qb in range(TB)]
        lag, waiting, done_mod = 1, [], 16
        for n, (h, qb) in enumerate(units):
            waiting.append((h, qb, front(h, qb)))
            if n % 4 == 1:
                modulation(done_mod, 4)
                done_mod += 4
            if len(waiting) > lag:
                back(*waiting.pop(0))
        while waiting:
            back(*waiting.pop(0))
        assert done_mod == 48
        mod_ready = dve.last

        def project_back(srcs, kc, acts_, ready, gate):
            for n in range(DC):
                if kc <= DC:
                    b, bank, done = linear(srcs[n], kc, acts_, ready)
                else:
                    b, bank, freed = banks.take()
                    for half in range(kc // DC):
                        k, w, loaded = fetch(srcs[n * (kc // DC) + half])
                        w = w.rearrange("p (c n) -> p c n", c=DC)
                        done = mm(bank, [(w[:, c, :], acts_[half * DC + c]) for c in range(DC)], loaded,
                                  *ready, *freed, start=half == 0, stop=half == kc // DC - 1)
                        freed = ()
                        slots.free(k, done)
                g = gate[:, n:n + 1] if gate is not None else 1.0
                m = dve.do(lambda e, n=n, bank=bank, g=g: e.scalar_tensor_tensor(
                    res[:, n, :], bank, g, res[:, n, :], ALU.mult, ALU.add), done)
                banks.free(b, m)
            return m

        x1 = project_back(ins["w_out"], DC, [mixed[:, c, :] for c in range(DC)], state["mixed"], mod[:, 16:24])

        modulated_gain(spans["norm2"], 32)
        fence(act_e, dve)
        h2_ready = norm_model(act, spans["norm2"], mod[:, 24:32], (x1, mod_ready))

        fence()
        pos[0] = 0
        peer_q = view(HP * S, HP, S)
        g_t = view(S)
        i_t = view(S)
        j_t = view(S)
        after_q = pos[0]
        keys = view(HP * P, HP, P)
        top_s = view(HP * P, HP, P)
        replaced = view(P)
        sums_b = view(256)
        topv = view(HP * TOPK, HP, TOPK)
        topi_u = view(HP * TOPK, HP, TOPK).bitcast(U32)
        topi = view(HP * TOPK, HP, TOPK)
        cand = view(PEER_H * 256, PEER_H, 256)
        fv = view(HK, PEER_H, TOPK)
        fpos = view(HK, PEER_H, TOPK).bitcast(U32)
        part_u = view(HK, PEER_H, TOPK).bitcast(U32)
        part = view(HK, PEER_H, TOPK)
        picked = view(HK * TOPK)
        gij = view(3 * HK, 3, HK)
        gsum = view(PEER_H)

        s_keys = sem("keys_loaded")
        keys_in = load(keys.rearrange("p a b -> p (a b)"), ins["keys"], s_keys, 1)
        for hp in range(HP):
            b, bank, done = linear(ins["peer_q"][hp], DC, acts, h2_ready)
            if hp % 2:
                m = dve.do(lambda e, hp=hp, bank=bank: e.tensor_copy(peer_q[:, hp, :], bank), done)
            else:
                m = act_e.do(lambda e, hp=hp, bank=bank: e.activation(peer_q[:, hp, :], bank, ACT.Copy), done)
            banks.free(b, m)
        q_marks = (dve.last, act_e.last)

        def top16(vals, idx, src, scratch):
            dve.do(lambda e: e.max(vals[:, 0:8], src))
            dve.do(lambda e: e.max_index(idx[:, 0:8], vals[:, 0:8], src))
            dve.do(lambda e: e.match_replace(scratch, vals[:, 0:8], src, -3e38))
            dve.do(lambda e: e.max(vals[:, 8:16], scratch))
            return dve.do(lambda e: e.max_index(idx[:, 8:16], vals[:, 8:16], scratch))

        iota16 = const("iota")[:, 0:TOPK]

        def pick(dst, half):
            p3 = picked.rearrange("p (a b) -> p a b", b=TOPK)
            p4 = picked.rearrange("p (h k b) -> p h k b", h=PEER_H, k=TOPK)
            flat = part.rearrange("p h k -> p (h k)").unsqueeze(2).broadcast_to([P, HK, TOPK])
            dve.do(lambda e: e.tensor_tensor(p3, flat, iota16.unsqueeze(1).broadcast_to([P, HK, TOPK]), ALU.is_equal))
            lists = topi.rearrange("p (h two) k -> p h two k", two=2)[:, :, half, :]
            dve.do(lambda e: e.tensor_tensor(p4, p4, lists.unsqueeze(2).broadcast_to([P, PEER_H, TOPK, TOPK]),
                                             ALU.mult))
            return dve.do(lambda e: e.tensor_reduce(dst, p3, AX_X, ALU.add))

        for tb in range(TB):
            for quad in range(HP // 4):
                b, bank, freed = banks.take()

                def emit(e, quad=quad, bank=bank, tb=tb):
                    for j in range(4):
                        hp = 4 * quad + j
                        last = e.matmul(bank[:, j * P:(j + 1) * P], peer_q[:, hp, tb * P:(tb + 1) * P],
                                        keys[:, hp, :], start=True, stop=True)
                    return last
                done = pe.do(emit, *q_marks, keys_in, *freed)
                m = act_e.do(lambda e, quad=quad, bank=bank: e.activation(
                    top_s[:, 4 * quad:4 * quad + 4, :], bank.rearrange("p (a b) -> p a b", a=4), ACT.Copy),
                    done, dve.last)
                banks.free(b, m)
            dve.wait(m)
            for hp in range(HP):
                top16(topv[:, hp, :], topi_u[:, hp, :], top_s[:, hp, :], replaced)
            dve.do(lambda e: e.tensor_copy(topi, topi_u))
            v4 = topv.rearrange("p (h two) k -> p h two k", two=2)
            dve.do(lambda e: e.tensor_tensor(
                cand.rearrange("p h (a b) -> p h a b", a=TOPK),
                v4[:, :, 0, :].unsqueeze(3).broadcast_to([P, PEER_H, TOPK, TOPK]),
                v4[:, :, 1, :].unsqueeze(2).broadcast_to([P, PEER_H, TOPK, TOPK]), ALU.add))
            for h in range(PEER_H):
                top16(fv[:, h, :], fpos[:, h, :], cand[:, h, :], sums_b)
            dve.do(lambda e: e.tensor_tensor(gij[:, 0, :].rearrange("p (h k) -> p h k", h=PEER_H), fv,
                                             fv[:, :, 0:1].broadcast_to([P, PEER_H, TOPK]), ALU.subtract),
                   pe.last)
            exped = act_e.do(lambda e: e.activation(gij[:, 0, :], gij[:, 0, :], ACT.Exp), dve.last)
            dve.do(lambda e: e.tensor_single_scalar(part_u, fpos, 4, ALU.logical_shift_right))
            dve.do(lambda e: e.tensor_copy(part, part_u))
            pick(gij[:, 1, :], 0)
            dve.do(lambda e: e.tensor_single_scalar(part_u, fpos, 15, ALU.bitwise_and))
            dve.do(lambda e: e.tensor_copy(part, part_u))
            pick(gij[:, 2, :], 1)
            g3 = gij[:, 0, :].rearrange("p (h k) -> p h k", h=PEER_H)
            dve.do(lambda e: e.tensor_reduce(gsum, g3, AX_X, ALU.add), exped)
            dve.do(lambda e: e.reciprocal(gsum, gsum))
            m = dve.do(lambda e: e.tensor_tensor(g3, g3, gsum.unsqueeze(2).broadcast_to([P, PEER_H, TOPK]), ALU.mult))
            b, bank, freed = banks.take()

            def emit(e, bank=bank):
                for j in range(3):
                    last = e.transpose(bank[:, j * P:(j + 1) * P], gij[:, j, :], const("ident"))
                return last
            done = pe.do(emit, m, *freed)
            for j, dst in enumerate((g_t, i_t, j_t)):
                m = dve.do(lambda e, j=j, dst=dst, bank=bank, tb=tb: e.tensor_copy(
                    dst[:, tb * P:(tb + 1) * P], bank[:, j * P:(j + 1) * P]), done)
            banks.free(b, m)

        fence()
        pos[0] = after_q
        stage_a = peer_q.rearrange("p a b -> p (a b)").rearrange("p (i t) -> p i t", t=GT)
        stage_b = view(GT * P, P, GT)
        stages = Ring([stage_a, stage_b])
        hot_i = Ring([view(4 * P, 4, P) for _ in range(2)])
        hot_j = Ring([view(4 * P, 4, P) for _ in range(2)])
        s_gates = [sem("gates_stored_a"), sem("gates_stored_b")]
        stores = [0, 0]
        for t0 in range(0, S, GT):
            gk, stage, stage_freed = stages.take()
            for q0 in range(t0, t0 + GT, 4):
                ik, hi, i_freed = hot_i.take()
                jk, hj, j_freed = hot_j.take()
                dve.wait(*i_freed)
                for j in range(4):
                    t = q0 + j
                    m = dve.do(lambda e, hi=hi, j=j, t=t: e.tensor_scalar(
                        hi[:, j, :], const("iota"), i_t[:, t:t + 1], g_t[:, t:t + 1], ALU.is_equal, ALU.mult))
                for j in range(4):
                    t = q0 + j
                    m2 = dve.do(lambda e, hj=hj, j=j, t=t: e.tensor_scalar(
                        hj[:, j, :], const("iota"), j_t[:, t:t + 1], None, ALU.is_equal))
                b, bank, freed = banks.take()

                def emit(e, bank=bank, hi=hi, hj=hj):
                    for j in range(4):
                        last = e.matmul(bank[:, j * P:(j + 1) * P], hj[:, j, :], hi[:, j, :], start=True, stop=True)
                    return last
                done = pe.do(emit, m, m2, *freed)
                hot_i.free(ik, done)
                hot_j.free(jk, done)
                src = bank.rearrange("p (t i) -> p i t", i=P)
                m = act_e.do(lambda e, stage=stage, src=src, a=q0 - t0: e.activation(
                    stage[:, :, a:a + 4], src, ACT.Copy), done, *stage_freed)
                banks.free(b, m)
            stores[gk] += 1
            stages.free(gk, load(gates_dram[:, :, t0:t0 + GT].rearrange("i j t -> j i t"), stage, s_gates[gk],
                                 stores[gk], m))
        gates_ready = [(s_gates[k], 16 * stores[k]) for k in range(2)]

        fence()
        for line in (sync, act_e, dve):
            line.wait(*gates_ready)
        pos[0] = 0
        coefs = Ring([view(S) for _ in range(2 * EG)])
        acts_e = Ring([view(S) for _ in range(4)])
        gate_tiles = [view(S) for _ in range(4)]
        gate_sems = [sem(f"gate{k}_loaded") for k in range(4)]
        gate_loads = [0] * 4
        gates = Ring(gate_tiles)

        def expert_gates(i):
            k, tile, freed = gates.take()
            gate_loads[k] += 1
            return k, tile, load(tile, gates_dram[i], gate_sems[k], gate_loads[k], *freed)

        def down(group):
            held = []
            for dh in range(2):
                got = [banks.take() for _ in range(4)]
                for n, (i, ck, coef, ready) in enumerate(group):
                    if dh == 0:
                        held.append(fetch(ins["peer_v"][i]))
                    k, w, loaded = held[n]
                    for d in range(4):
                        c = dh * 4 + d
                        done = mm(got[d][1], [(w[:, c * P:(c + 1) * P], coef)], ready, loaded,
                                  *(got[d][2] if n == 0 else ()), start=n == 0, stop=n == EG - 1)
                    if dh == 1:
                        slots.free(k, done)
                        coefs.free(ck, done)
                for d in range(4):
                    c = dh * 4 + d
                    m = dve.do(lambda e, c=c, bank=got[d][1]: e.scalar_tensor_tensor(
                        res[:, c, :], bank, mod[:, 40 + c:41 + c], res[:, c, :], ALU.mult, ALU.add), done)
                    banks.free(got[d][0], m)

        last_group = None
        for i0 in range(0, NKEYS, EG):
            group = []
            for i in range(i0, i0 + EG):
                gk, gate, gate_in = expert_gates(i)
                b, bank, done = linear(ins["peer_u"][i], DC, acts, ())
                ak, a, a_freed = acts_e.take()
                gelu = act_e.do(lambda e, a=a, bank=bank: e.activation(a, bank, ACT.Gelu), done, *a_freed)
                banks.free(b, gelu)
                ck, coef, c_freed = coefs.take()
                m = dve.do(lambda e, coef=coef, a=a, gate=gate: e.tensor_tensor(coef, a, gate, ALU.mult),
                           gelu, gate_in, *c_freed)
                acts_e.free(ak, m)
                gates.free(gk, m)
                group.append((i, ck, coef, m))
            if last_group:
                down(last_group)
            last_group = group
        down(last_group)

        fence()
        h_ready = norm_model(act, spans["a_norm"], None, (dve.last,))
        pos[0] = 0
        conv_y = view(CC * S, CC, S)
        padded = Ring([view(S + 2) for _ in range(2)])
        work = Ring([view(S) for _ in range(8)])
        for k in range(2):
            pool.do(lambda e, k=k: e.memset(padded.items[k][:, 0:2], 0.0))
        dve.wait(pool.last)

        for n in range(CC):
            got = [linear(ins["a_w_in"][part_ * CC + n], DC, acts, h_ready) for part_ in (1, 2, 0, 3)]
            (bc, c_bank, c_done), (bu, u_bank, u_done), (bb, b_bank, b_done), (bz, z_bank, z_done) = got
            wc, c_sb, c_freed = work.take()
            m = act_e.do(lambda e, c_sb=c_sb, c_bank=c_bank: e.activation(c_sb, c_bank, ACT.Copy), c_done, *c_freed)
            banks.free(bc, m)
            vk, vp, v_freed = padded.take()
            m = dve.do(lambda e, vp=vp, c_sb=c_sb, u_bank=u_bank: e.tensor_tensor(vp[:, 2:S + 2], c_sb, u_bank,
                                                                                ALU.mult), m, u_done, *v_freed)
            banks.free(bu, m)
            work.free(wc, m)
            wz, z_sb, z_freed = work.take()
            zm = act_e.do(lambda e, z_sb=z_sb, z_bank=z_bank: e.activation(z_sb, z_bank, ACT.Silu), z_done, *z_freed)
            banks.free(bz, zm)
            wt, acc, a_freed = work.take()
            dve.do(lambda e, acc=acc, vp=vp, n=n: e.tensor_scalar(acc, vp[:, 0:S], col("conv", n), None, ALU.mult),
                   *a_freed)
            for k in (1, 2):
                m = dve.do(lambda e, acc=acc, vp=vp, n=n, k=k: e.scalar_tensor_tensor(
                    acc, vp[:, k:k + S], col("conv", k * CC + n), acc, ALU.mult, ALU.add))
            padded.free(vk, m)
            m = dve.do(lambda e, acc=acc, b_bank=b_bank: e.tensor_tensor(acc, acc, b_bank, ALU.mult), b_done)
            banks.free(bb, m)
            m = pool.do(lambda e, acc=acc, z_sb=z_sb, n=n: e.tensor_tensor(conv_y[:, n, :], acc, z_sb, ALU.mult),
                        m, zm)
            work.free(wt, m)
            work.free(wz, m)
        x3 = project_back(ins["a_w_out"], CC, [conv_y[:, c, :] for c in range(CC)], (pool.last,), None)

        fence()
        kv_ready = norm_model(act, spans["kv_norm"], None, (x3,))
        pos[0] = 0
        k_slc = view(GROUPS * S, GROUPS, S)
        k_win = view(GROUPS * S, GROUPS, S)
        v_sw = view(TB * S, TB, S)
        kcmp = view(GROUPS * NCP, GROUPS, NCP)
        vcmp = view(GROUPS * GROUPS * HD, GROUPS, GROUPS * HD)
        gate_rows = view(TB * 48, TB, 48)
        hidden = view(4 * P, 4, P)
        bias_cols = view(4)
        after_kv = pos[0]
        strm = [view(GROUPS * 528, GROUPS, 528) for _ in range(2)]
        pe_cols = view(32)
        w2 = view(2 * P * 2 , 2, 2 * P)
        hidden_v = view(2 * GROUPS * P, 2 * GROUPS, P)
        tmpx = view(S)
        rope_tmp = (view(S), view(S))
        s_pos, s_w2 = sem("pos_loaded"), sem("w2_loaded")
        pos_in = load(pe_cols, ins["cmp_pos"], s_pos, 1)
        w2_in = load(w2.rearrange("p a b -> p (a b)"), ins["cmp_w2"], s_w2, 1)
        for g in range(GROUPS):
            other = halves[1 - g % 2]
            for t in (k_slc, k_win, kcmp):
                pool.do(lambda e, t=t, g=g, other=other: e.memset(t[other, g, :], 0.0))
        pool.do(lambda e: e.memset(vcmp, 0.0))
        for t in strm:
            pool.do(lambda e, t=t: e.memset(t[:, :, S - 1:528], 0.0))
        zeroed = pool.last

        for which in range(2):
            for g in range(GROUPS):
                b, bank, done = linear(ins["w_kvc"][which * GROUPS + g], DC, acts, kv_ready)
                t = strm[which]
                m = act_e.do(lambda e, t=t, g=g, bank=bank: e.activation(t[0:64, g, 0:S], bank[0:64, :], ACT.Copy),
                             done, zeroed)
                m2 = dve.do(lambda e, t=t, g=g, bank=bank: e.tensor_copy(t[64:128, g, 0:S - 1], bank[64:128, 1:S]),
                            done, zeroed)
                banks.free(b, m, m2)
        strm_ready = (act_e.last, dve.last)
        rope16 = (const("rot16"), const("cos16"), const("sin16"))
        for which, dst in enumerate((k_slc, k_win)):
            for m_ in range(2):
                b, bank, done = linear(ins["w_kvs"][which * 2 + m_], DC, acts, kv_ready)
                m = act_e.do(lambda e, bank=bank: e.activation(tmpx, bank, ACT.Copy), done, dve.last, pe.last,
                             pool.last)
                banks.free(b, m)
                rope([(dst[halves[j], 2 * m_ + j, :], halves[j]) for j in range(2)], tmpx, *rope16, rope_tmp, m)
        got, done = linear_tokens([ins["w_vsw"][i] for i in range(4)], DC, 2, acts, kv_ready)
        for tb, (b, bank) in enumerate(got):
            banks.free(b, act_e.do(lambda e, tb=tb, bank=bank: e.activation(v_sw[:, tb, :], bank, ACT.Copy), done))

        for which in range(2):
            w1 = [fetch(ins["cmp_w1"][which * 4 + i]) for i in range(4)]
            w1v = [w.rearrange("p (l n) -> p l n", l=4) for _, w, _ in w1]
            loaded = [x[2] for x in w1]
            for hc in range(2):
                b, bank, freed = banks.take()
                b2, bank2, freed2 = banks.take()

                def emit(e, which=which, hc=hc, bank=bank, bank2=bank2, w1v=w1v):
                    for l in range(CMP_PAIRS):
                        e.matmul(bank[:, 0:1], w1v[l // 4][:, l % 4, hc * P:(hc + 1) * P],
                                 pe_cols[:, which * 16 + l:which * 16 + l + 1], start=l == 0, stop=l == CMP_PAIRS - 1)
                    for l in range(CMP_PAIRS):
                        a = 2 * l
                        last = e.matmul(bank2[:, 0:P].rearrange("p (g n) -> p g n", g=GROUPS),
                                        w1v[l // 4][:, l % 4, hc * P:(hc + 1) * P],
                                        strm[which][:, :, a:a + CMP_STRIDE * (NCP - 1) + 1:CMP_STRIDE],
                                        start=l == 0, stop=l == CMP_PAIRS - 1)
                    return last
                done = pe.do(emit, *loaded, *strm_ready, pos_in, *freed, *freed2)
                slot = which * 2 + hc
                m = dve.do(lambda e, slot=slot, bank=bank: e.tensor_copy(bias_cols[:, slot:slot + 1], bank[:, 0:1]),
                           done)
                banks.free(b, m)
                m = act_e.do(lambda e, slot=slot, bank2=bank2: e.activation(
                    hidden[:, slot, :], bank2[:, 0:P], ACT.Gelu_apprx_tanh, bias=bias_cols[:, slot:slot + 1]), m)
                banks.free(b2, m)
            for k, _, _ in w1:
                slots.free(k, done)
        b, bank, freed = banks.take()
        done = mm(bank[:, 0:P], [(w2[:, hc, 0:P], hidden[:, hc, :]) for hc in range(2)], m, w2_in, *freed)
        for g in range(GROUPS):
            hf = halves[g % 2]
            m = dve.do(lambda e, g=g, hf=hf, bank=bank: e.tensor_copy(kcmp[hf, g, :], bank[hf, g * NCP:(g + 1) * NCP]),
                       done)
        banks.free(b, m)
        m4 = dve.do(lambda e: e.tensor_copy(
            hidden_v.rearrange("p a (i n) -> p a i n", i=GROUPS),
            hidden[:, 2:4, :].rearrange("p c (g n) -> p (c g) n", g=GROUPS).unsqueeze(2).broadcast_to(
                [P, 2 * GROUPS, GROUPS, NCP])), act_e.last)
        b, bank, freed = banks.take()

        def emit(e, bank=bank):
            for g in range(GROUPS):
                for hc in range(2):
                    last = e.matmul(bank[:, g * HD:(g + 1) * HD], hidden_v[:, hc * GROUPS + g, :], w2[:, hc, P:P + HD], start=hc == 0,
                                    stop=hc == 1)
            return last
        done = pe.do(emit, m4, *freed)
        for g in range(GROUPS):
            for i in range(GROUPS):
                rows = slice(i * NCP, (i + 1) * NCP)
                m = dve.do(lambda e, g=g, i=i, rows=rows, bank=bank: e.tensor_copy(
                    vcmp[rows, g, i * HD:(i + 1) * HD], bank[rows, g * HD:(g + 1) * HD]), done)
        banks.free(b, m)

        fence()
        hb_ready = norm_model(act, spans["b_norm"], None, ())
        pos[0] = after_kv
        q_raw = view(DC * S, DC, S)
        z_act = None
        rope_tmp = (view(S), view(S))
        pc_t = view(GROUPS * S, GROUPS, S)
        cmp_p = view(NSA_H * NCP, NSA_H, NCP)
        cmp_st = view(4 * NSA_H)
        probs = Ring([view(S) for _ in range(4)])
        after_nsa = pos[0]

        got_g = banks.take()
        k, w, loaded = fetch(ins["w_gates"])
        w = w.rearrange("p (c n) -> p c n", c=DC)

        def emit(e, w=w):
            for tb in range(TB):
                for c in range(DC):
                    last = e.matmul(got_g[1][:, tb * 48:(tb + 1) * 48], acts[c][:, tb * P:(tb + 1) * P], w[:, c, :],
                                    start=c == 0, stop=c == DC - 1)
            return last
        done = pe.do(emit, loaded, *got_g[2], *hb_ready)
        slots.free(k, done)
        m = act_e.do(lambda e: e.activation(gate_rows.rearrange("p a b -> p (a b)"), got_g[1][:, 0:TB * 48],
                                            ACT.Sigmoid), done)
        banks.free(got_g[0], m)
        for c in range(DC):
            b, bank, done = linear(ins["b_q"][c], DC, acts, hb_ready)
            m = act_e.do(lambda e, c=c, bank=bank: e.activation(q_raw[:, c, :], bank, ACT.Copy, scale=HD ** -0.5), done)
            banks.free(b, m)
        q_ready = act_e.last
        gates4 = gate_rows.rearrange("p t (h b) -> p t h b", b=3)

        for qb in range(TB):
            b, bank, freed = banks.take()

            def emit(e, qb=qb, bank=bank):
                for c in range(DC):
                    for j in range(2):
                        g = 2 * (c // 4) + j
                        n = g * 4 + c % 4
                        last = e.matmul(bank[:, n * NCP:(n + 1) * NCP], q_raw[:, c, qb * P:(qb + 1) * P],
                                        kcmp[:, g, :], start=True, stop=True)
                return last
            done = pe.do(emit, q_ready, dve.last, *freed)
            s3 = bank.rearrange("p (h n) -> p h n", n=NCP)
            wide = [P, NSA_H, NCP]
            a0, b0 = qb * NCP, (qb + 1) * NCP
            add = const("cmp_add")[:, a0:b0].unsqueeze(1).broadcast_to(wide)
            mul = const("cmp_mul")[:, a0:b0].unsqueeze(1).broadcast_to(wide)
            mx, sm = cmp_st[:, 0:16], cmp_st[:, 16:32]
            m = dve.do(lambda e, s3=s3, add=add: e.tensor_tensor(cmp_p, s3, add, ALU.add), done, pe.last)
            banks.free(b, m)
            dve.do(lambda e: e.tensor_reduce(mx, cmp_p, AX_X, ALU.max))
            m = dve.do(lambda e: e.tensor_tensor(cmp_p, cmp_p, mx.unsqueeze(2).broadcast_to(wide), ALU.subtract))
            m = act_e.do(lambda e: e.activation(cmp_p, cmp_p, ACT.Exp), m)
            dve.do(lambda e, mul=mul: e.tensor_tensor(cmp_p, cmp_p, mul, ALU.mult), m)
            dve.do(lambda e: e.tensor_reduce(sm, cmp_p, AX_X, ALU.add))
            dve.do(lambda e: e.tensor_scalar(sm, sm, 1e-30, None, ALU.max))
            dve.do(lambda e: e.reciprocal(sm, sm))
            dve.do(lambda e, qb=qb: e.tensor_tensor(sm, sm, gates4[:, qb, :, 0], ALU.mult))
            m = dve.do(lambda e: e.tensor_tensor(cmp_p, cmp_p, sm.unsqueeze(2).broadcast_to(wide), ALU.mult))
            b, bank, freed = banks.take()

            def emit(e, bank=bank):
                for g in range(GROUPS):
                    last = e.transpose(bank[:, g * P:(g + 1) * P],
                                       cmp_p[:, 4 * g:4 * g + 4, :].rearrange("p h n -> p (h n)"), const("ident"))
                return last
            done = pe.do(emit, m, *freed)
            m = act_e.do(lambda e, qb=qb, bank=bank: e.activation(
                pc_t[:, :, qb * P:(qb + 1) * P], bank.rearrange("p (g q) -> p g q", g=GROUPS), ACT.Copy), done)
            banks.free(b, m)
        pc_ready = act_e.last

        for c in range(DC):
            m = rope([(q_raw[:, c, :], slice(0, P))], q_raw[:, c, :], *rope16, rope_tmp, q_ready)
        q_rot = q_raw

        fence(dve, act_e)
        turned_mem = [[view(TB * S, TB, S) for _ in range(2)] for _ in range(1)]
        turned_ring = Ring(turned_mem)
        y = ring_y = None

        def z_chunk(c, zbuf, zfreed):
            b, bank, done = linear(ins["b_z"][c], DC, acts, hb_ready)
            m = act_e.do(lambda e: e.activation(zbuf, bank, ACT.Silu), done, *zfreed)
            banks.free(b, m)
            return m

        z_ring = Ring([rope_tmp[0], rope_tmp[1]])
        o_held = {}

        def nsa_front(c, j, qb, branch):
            g = 2 * (c // 4) + j
            head = g * 4 + c % 4
            keys_ = (k_slc, k_win)[branch]
            pk, p, sk, st, exped = softmax_rows([(q_rot[:, c, :], keys_[:, g, :])], qb, None)
            w = (qb + 1) * P
            dve.do(lambda e: e.reciprocal(st[:, 2:3], st[:, 1:2]), exped)
            dve.do(lambda e: e.tensor_tensor(st[:, 3:4], st[:, 2:3], gates4[:, qb, head, branch + 1:branch + 2],
                                             ALU.mult))
            m = dve.do(lambda e: e.tensor_scalar(p[:, 0:w], p[:, 0:w], st[:, 3:4], None, ALU.mult))
            stats.free(sk, m)
            return (pk, p, m)

        nsa_state = {}

        def nsa_back(c, j, qb, branch, unit):
            pk, p, ready = unit
            g = 2 * (c // 4) + j
            if qb == 0 and branch == 0:
                nsa_state["t"] = turned_ring.take()
            tk, t, t_freed = nsa_state["t"]
            turned, m = transpose_rows(p, qb, t[branch], ready, t_freed, act_e if branch else dve)
            nsa_state[qb, branch] = m
            probs.free(pk, turned)
            if (qb, branch) != (TB - 1, 1):
                return
            if j == 0:
                o_held["bank"] = o_banks.take()
            b, bank, freed = o_held["bank"]
            o = bank[halves[j], :]
            i = c % 4
            ready = [nsa_state[q, br] for q in range(TB) for br in range(2)]
            for br in range(2):
                values_mm(o, lambda kb, br=br: v_sw[:, kb, br * 256 + g * HD:br * 256 + (g + 1) * HD], t[br],
                          ready if br == 0 else (), br == 0, False, *(freed if br == 0 else ()))
            done = mm(o, [(vcmp[:, g, i * HD:(i + 1) * HD], pc_t[:, g, :])], pc_ready, start=False, stop=True)
            turned_ring.free(tk, done)
            if j == 0:
                return
            zk, zbuf, zfreed = z_ring.take()
            zm = z_chunk(c, zbuf, zfreed)
            o_held.setdefault("y", []).append((c, b, bank, zbuf, zk, zm, done))

        def finish_y():
            c, b, bank, zbuf, zk, zm, done = o_held["y"].pop(0)
            m = dve.do(lambda e: e.tensor_tensor(q_rot[:, c, :], bank, zbuf, ALU.mult), zm, done, pe.last)
            o_banks.free(b, m)
            z_ring.free(zk, m)
            return m

        fence(pe)
        waiting = []
        for c in range(DC):
            for j in range(2):
                for qb in range(TB):
                    for branch in range(2):
                        waiting.append((c, j, qb, branch, nsa_front(c, j, qb, branch)))
                        if len(waiting) > 2:
                            nsa_back(*waiting.pop(0))
                            if o_held.get("y"):
                                finish_y()
        while waiting:
            nsa_back(*waiting.pop(0))
        y_ready = finish_y()
        x4 = project_back(ins["b_w_out"], DC, [q_rot[:, c, :] for c in range(DC)], (y_ready,), None)

        fence(dve)
        marks = norm_model(act, spans["final"], None, (x4,))
        s_out = sem("out_stored")
        for c in range(DC):
            stored = load(out[c], act[:, c, :], s_out, c + 1, marks[c])
        sync.wait(stored)

        with nc.Block() as block:
            @block.sync
            def _(e):
                sync.run(e)

            @block.tensor
            def _(e):
                pe.run(e)

            @block.vector
            def _(e):
                dve.run(e)

            @block.scalar
            def _(e):
                act_e.run(e)

            @block.gpsimd
            def _(e):
                pool.run(e)


def rotation(dim, block):
    r = np.zeros((P, P), np.float32)
    for b in range(0, P, block):
        for i in range(dim // 2):
            r[b + i + dim // 2, b + i] = -1.0
            r[b + i, b + i + dim // 2] = 1.0
    return r


def make_consts():
    c = np.zeros((P, NCONSTS), np.float32)

    def put(name, a):
        c[:, CONSTS[name][0]:CONSTS[name][1]] = a

    put("ident", np.eye(P, dtype=np.float32))
    put("ones", 1.0)
    put("ones64", np.kron(np.eye(2), np.ones((64, 64))))
    put("rot64", rotation(64, 64))
    put("rot16", rotation(16, 64))
    put("iota", np.arange(P)[None, :])
    put("mask", np.where(np.arange(P)[None, :] > np.arange(P)[:, None], NEG, 0.0))
    pos = np.arange(S, dtype=np.float32)
    inv = (np.float32(1.0) / (np.float32(10000.0) ** (np.arange(32, dtype=np.float32) / np.float32(32)))).astype(np.float32)
    ang = (pos[None, :] * inv[:, None]).astype(np.float32)
    put("cos64", np.tile(np.cos(ang), (4, 1)))
    put("sin64", np.tile(np.sin(ang), (4, 1)))
    inv = (np.float32(500000.0) ** (-np.arange(0, 16, 2, dtype=np.float32) / np.float32(16))).astype(np.float32)
    ang = (pos[None, :] * inv[:, None]).astype(np.float32)
    cos, sin = np.ones((64, S), np.float32), np.zeros((64, S), np.float32)
    cos[0:16], sin[0:16] = np.tile(np.cos(ang), (2, 1)), np.tile(np.sin(ang), (2, 1))
    put("cos16", np.tile(cos, (2, 1)))
    put("sin16", np.tile(sin, (2, 1)))
    t = np.arange(P)[:, None, None] + P * np.arange(TB)[None, :, None]
    n = np.arange(NCP)[None, None, :]
    ok = (n * CMP_STRIDE + CMP_BLOCK - 1 <= t) & (n < NCMP)
    put("eps", np.array([n * EPS for n in EPS_N])[None, :])
    put("cmp_add", np.where(ok, 0.0, NEG).reshape(P, -1))
    put("cmp_mul", ok.astype(np.float32).reshape(P, -1))
    return c


def chunked(w):
    k, n = w.shape
    return np.ascontiguousarray(w.reshape(k // P, P, n // P, P).transpose(2, 1, 0, 3)).reshape(n // P, P, -1)


def moving(w, per):
    k, n = w.shape
    return np.ascontiguousarray(w.reshape(k // P // per, per, P, n).transpose(0, 2, 1, 3)).reshape(k // P // per, P, -1)


def columns(v):
    return np.asarray(v).reshape(-1, P).T


def lay_out(a):
    g = {k: np.asarray(v) for k, v in a.items()}
    cols = np.zeros((P, NCOLS), np.float32)

    def put(name, v):
        cols[:, COLS[name][0]:COLS[name][1]] = v

    twice = lambda v: np.concatenate([v, v])[:, None]
    put("c", columns(g["c"][0]))
    put("ada_b", columns(g["ada_b"][0]))
    put("norm1", columns(g["norm1_g"][0]))
    put("norm2", columns(g["norm2_g"][0]))
    put("a_norm", columns(g["a_norm_2"][0]))
    put("kv_norm", columns(g["kv_norm_2"]))
    put("b_norm", columns(g["b_norm_2"][0]))
    put("final", columns(g["final_norm_2"]))
    put("q_lat", columns(g["mla_q_lat_g"][0]))
    put("kv_lat", columns(g["mla_kv_lat_g"][0]))
    put("q_nope", g["mla_q_g"][0][:NOPE, None])
    put("q_pe", twice(g["mla_q_g"][0][NOPE:]))
    put("k_nope", g["mla_k_g"][0][:NOPE, None])
    put("k_pe", twice(g["mla_k_g"][0][NOPE:]))
    put("dq", twice(g["diff_q_g"][0]))
    put("dk", twice(g["diff_k_g"][0]))
    put("subln", g["diff_subln_g"][0][:, None])
    put("conv", columns(g["a_conv_w_2"][0]))
    for name, one, two in (("lam_q", "diff_lq1", "diff_lq2"), ("lam_k", "diff_lk1", "diff_lk2")):
        cols[0:64, COLS[name][0]] = g[one][0]
        cols[0:64, COLS[name][0] + 1] = g[two][0]

    w = g["w_in"][0]
    o0, o1, o2 = Q_LORA, Q_LORA + KV_LORA, Q_LORA + KV_LORA + ROPE
    o3, o4 = o2 + 512, o2 + 1024
    kpe = w[:, o1:o2]
    w_in = np.concatenate([w[:, o0:o1], kpe, kpe, w[:, :o0], w[:, o2:o4]], axis=1)
    qu = g["mla_w_q_up"][0].reshape(Q_LORA, MLA_H, NOPE + ROPE)
    q_up = np.concatenate([qu[:, :, :NOPE].reshape(Q_LORA, -1), qu[:, :, NOPE:].reshape(Q_LORA, -1)], axis=1)
    ku = g["mla_w_kv_up"][0].reshape(KV_LORA, MLA_H, NOPE + MLA_V)
    kv = g["w_kv_2"].reshape(D, 6, GROUPS, HD)
    kc = np.concatenate([kv[:, 0:2], kv[:, 0:2]], axis=3).reshape(D, -1)
    ks = np.concatenate([kv[:, 2].reshape(D, -1), kv[:, 4].reshape(D, -1)], axis=1)
    vsw = np.concatenate([kv[:, 3].reshape(D, -1), kv[:, 5].reshape(D, -1)], axis=1)
    order = [h for m in range(2) for i in range(4) for h in (8 * m + i, 8 * m + 4 + i)]
    bw = g["b_w_in_2"][0]
    bq = bw[:, :D].reshape(D, NSA_H, HD)[:, order].reshape(D, D)
    bz = bw[:, D + 48:].reshape(D, NSA_H, HD)[:, order].reshape(D, D)
    bo = g["b_w_out_2"][0].reshape(NSA_H, HD, D)[order].reshape(D, D)
    w1 = [g[n].reshape(CMP_PAIRS // 4, 4, P, CMP_HID).transpose(0, 2, 1, 3).reshape(4, P, -1)
          for n in ("cmp_w1_k_2", "cmp_w1_v_2")]
    pos = [g[n].reshape(CMP_PAIRS, P).T for n in ("cmp_pos_k_2", "cmp_pos_v_2")]
    w2k, w2v = (g[n].reshape(2, P, HD).transpose(1, 0, 2) for n in ("cmp_w2_k_2", "cmp_w2_v_2"))
    w_out = chunked(g["a_w_out_2"][0]).reshape(DC, P, 2, -1).transpose(0, 2, 1, 3).reshape(2 * DC, P, -1)
    return {
        "x": g["x"][0].T.reshape(DC, P, S).transpose(1, 0, 2).reshape(P, -1),
        "cols": cols,
        "consts": make_consts(),
        "ada_w": chunked(g["ada_w"][0]),
        "w_in": chunked(w_in),
        "w_dv": moving(w[:, o4:], 2),
        "q_up": chunked(q_up),
        "kv_up": chunked(ku[:, :, :NOPE].reshape(KV_LORA, -1)),
        "kv_up_v": moving(ku[:, :, NOPE:].reshape(KV_LORA, -1), 2)[0],
        "w_out": chunked(g["w_out"][0]),
        "peer_q": chunked(g["peer_w_q"][0]),
        "keys": g["peer_sub_keys"][0].reshape(HP, NKEYS, P).transpose(2, 0, 1).reshape(P, -1),
        "peer_u": g["peer_u"][0].reshape(NKEYS, P, DC, P).transpose(0, 3, 2, 1).reshape(NKEYS, P, -1),
        "peer_v": g["peer_v"][0].reshape(NKEYS, P, D),
        "a_w_in": chunked(g["a_w_in_2"][0]),
        "a_w_out": w_out,
        "w_kvc": chunked(kc),
        "w_kvs": chunked(ks),
        "w_vsw": moving(vsw, 2),
        "cmp_w1": np.concatenate(w1),
        "cmp_pos": np.concatenate(pos, axis=1),
        "cmp_w2": np.concatenate([w2k, w2k, w2v, w2v], axis=2).reshape(P, -1),
        "w_gates": moving(bw[:, D:D + 48], DC)[0],
        "b_q": chunked(bq),
        "b_z": chunked(bz),
        "b_w_out": chunked(bo),
    }


def kernel(**inputs):
    import concourse.bacc as bacc
    from concourse.bass_utils import run_bass_kernel_spmd

    nc = bacc.Bacc("TRN2", target_bir_lowering=False, num_devices=1)
    arrays = {f"in_{k}": np.ascontiguousarray(v) for k, v in lay_out(inputs).items()}
    ins = {k[3:]: nc.dram_tensor(k, list(v.shape), F32, kind="ExternalInput").ap() for k, v in arrays.items()}
    out = nc.dram_tensor("out", [DC, P, S], F32, kind="ExternalOutput").ap()
    build(nc, ins, out)
    r = run_bass_kernel_spmd(nc, [arrays], core_ids=[0])
    return np.ascontiguousarray(r.results[0]["out"].reshape(D, S).T).reshape(1, S, D)
```

```python
from contextlib import ExitStack

import numpy as np

import concourse.bass as bass
from concourse import mybir

ALU = mybir.AluOpType
ACT = mybir.ActivationFunctionType
F32 = mybir.dt.float32
F32R = mybir.dt.float32r
U32 = mybir.dt.uint32
HI_BITS = 0xFFFFF000
AX_X = mybir.AxisListType.X

P = 128
S = 512
TB = S // P
D = 1024
DC = D // P
EPS = 1e-6
NEG = -1e30

MLA_H, NOPE, ROPE, MLA_V, Q_LORA, KV_LORA = 4, 128, 64, 128, 384, 256
QC, KVC = Q_LORA // P, KV_LORA // P
DIFF_H, DIFF_DQK = 4, 64
LAMBDA_INIT = 0.2
PEER_H, NKEYS, TOPK = 8, 128, 16
HP = PEER_H * 2
HK = PEER_H * TOPK
CONV_D = 2048
CC = CONV_D // P
NSA_H, GROUPS, HD = 16, 4, 64
CMP_BLOCK, CMP_STRIDE, CMP_HID = 32, 16, 256
NCMP = S // CMP_STRIDE - 1
NCP = NCMP + 1
CMP_PAIRS = CMP_BLOCK // 2
SLC_BLOCK, N_SELECT, WINDOW = 64, 16, 512
assert S // SLC_BLOCK <= N_SELECT and WINDOW >= S

ARENA = 23040
SLOT = 1024
SLOTS = 4
AHEAD = 2
GT = 64
EG = 4

COLS = {}
_at = 0
for _name, _n in (("c", 8), ("ada_b", 48), ("norm1", 8), ("norm2", 8), ("a_norm", 8), ("kv_norm", 8),
                  ("b_norm", 8), ("final", 8), ("q_lat", 3), ("kv_lat", 2), ("q_nope", 1), ("q_pe", 1),
                  ("k_nope", 1), ("k_pe", 1), ("dq", 1), ("dk", 1), ("subln", 1), ("conv", 48),
                  ("lam_q", 2), ("lam_k", 2)):
    COLS[_name] = (_at, _at + _n)
    _at += _n
NCOLS = _at

EPS_N = (D, Q_LORA, KV_LORA, P, 64)

CONSTS = {}
_at = 0
for _name, _n in (("ident", P), ("ones", P), ("ones64", P), ("rot64", P), ("rot16", P), ("iota", P),
                  ("mask", P), ("cos", S), ("sin", S),
                  ("cmp_add", TB * NCP), ("cmp_mul", TB * NCP), ("eps", len(EPS_N))):
    CONSTS[_name] = (_at, _at + _n)
    _at += _n
NCONSTS = _at


class Line:

    def __init__(self, sem, chained):
        self.sem, self.chained, self.count, self.steps, self.waited = sem, chained, 0, [], {}

    def wait(self, *marks):
        for sem, value in marks:
            if self.waited.get(sem.name, 0) < value:
                self.waited[sem.name] = value
                self.steps.append(lambda e, s=sem, v=value: e.wait_ge(s, v))

    def do(self, emit, *marks, alone=False):
        self.wait(*marks)
        if self.chained and self.count and not alone:
            self.wait((self.sem, self.count))
        self.count += 1
        self.steps.append(lambda e: emit(e).then_inc(self.sem, 1))
        return self.sem, self.count

    @property
    def last(self):
        return self.sem, self.count

    def run(self, engine):
        for step in self.steps:
            step(engine)


class Ring:

    def __init__(self, items):
        self.items, self.idle = items, [(k, ()) for k in range(len(items))]

    def take(self):
        assert self.idle, "no buffer is free"
        k, marks = self.idle.pop(0)
        return k, self.items[k], marks

    def free(self, k, *marks):
        self.idle.append((k, marks))


def skewed(tasks):
    active = []
    for task in tasks:
        active.insert(0, task)
        active = [x for x in active if next(x, "ended") != "ended"]
    while active:
        active = [x for x in active if next(x, "ended") != "ended"]


def build(nc, ins, out):
    ctx = ExitStack()
    with ctx:
        def sem(name):
            return ctx.enter_context(nc.semaphore(name))

        def sb(name, shape, dt=F32):
            return ctx.enter_context(nc.sbuf_tensor(name, shape, dt))

        gates_dram = nc.dram_tensor("gates_scratch", [NKEYS, P, S], F32, kind="Internal").ap()

        consts = sb("consts", [P, NCONSTS])
        cols = sb("cols", [P, NCOLS])
        res = sb("res", [P, DC, S])
        act_r = sb("act_r", [P, 2, DC, S], F32R)
        weights_r = sb("weights_r", [P, AHEAD + 1, 2, SLOT], F32R)
        mask_mem = sb("mask_mem", [P, 2, S])
        whole_mem = sb("whole_mem", [P, 2, S])
        ring_mem = sb("ring_mem", [P, SLOTS, SLOT])
        mod = sb("mod", [P, 48])
        silu_c = sb("silu_c", [P, DC])
        gains = sb("gains", [P, 64])
        rstd_mem = sb("rstd_mem", [P, 3, S])
        newton_mem = sb("newton_mem", [P, 1, S])
        sq_mem = sb("sq_mem", [P, 2, S])
        small = sb("small", [P, 8, 4])
        lam = sb("lam", [P, 8])
        arena = sb("arena", [P, ARENA])
        arena_r = nc.alloc_sbuf_tensor_at("arena_r", [P, ARENA], F32R, offset=nc.lookup_mloc(arena).addr)
        banks_mem = ctx.enter_context(nc.psum_tensor("banks", [P, 8, 512], F32))

        def const(name):
            a, b = CONSTS[name]
            return consts[:, a:b]

        def col(name, i=0, n=1):
            a = COLS[name][0] + i
            return cols[:, a:a + n]

        pe = Line(sem("pe_done"), False)
        dve = Line(sem("dve_done"), True)
        act_e = Line(sem("act_done"), False)
        pool = Line(sem("pool_done"), True)
        sync = Line(sem("sync_unused"), False)
        slot_sems = [sem(f"slot{k}_loaded") for k in range(SLOTS)]
        slot_loads = [0] * SLOTS
        slots = Ring([ring_mem[:, k, :] for k in range(SLOTS)])
        banks = Ring([banks_mem[:, k, :] for k in range(8)])
        rstds = Ring([rstd_mem[:, k, :] for k in range(3)])
        newtons = Ring([newton_mem[:, 0, :]])
        splits = Ring([weights_r[:, k, :, :] for k in range(AHEAD + 1)])
        masks = Ring([mask_mem[:, k, :] for k in range(2)])
        wholes = Ring([whole_mem[:, k, :] for k in range(2)])
        act_hl = [(act_r[:, 0, c, :], act_r[:, 1, c, :]) for c in range(DC)]
        squares = Ring([sq_mem[:, k, :] for k in range(2)])

        def load(dst, src, s, n, *marks):
            sync.wait(*marks)
            sync.steps.append(lambda e: e.dma_start(dst, src).then_inc(s, 16))
            return s, 16 * n

        def fetch(src):
            k, tile, freed = slots.take()
            n = src.shape[1]
            slot_loads[k] += 1
            return k, tile[:, 0:n], load(tile[:, 0:n], src, slot_sems[k], slot_loads[k], *freed)

        def fence(*lines):
            for line in lines or (pe, dve, act_e, pool, sync):
                line.wait(*[x.last for x in (pe, dve, act_e, pool) if x is not line and x.count])

        def eps_col(n):
            return const("eps")[:, EPS_N.index(n):EPS_N.index(n) + 1]

        def mm(out_, pairs, *marks, start=True, stop=True):
            def emit(e):
                for n, (a, b) in enumerate(pairs):
                    last = e.matmul(out_, a, b, start=start and n == 0, stop=stop and n == len(pairs) - 1)
                return last
            return pe.do(emit, *marks)

        def split(src, hi, lo, ready, freed=()):
            for at in range(0, src.shape[1], S):
                piece = slice(at, min(at + S, src.shape[1]))
                n = piece.stop - at
                tk, mask, mask_freed = masks.take()
                x, top, hi_, lo_ = src[:, piece], mask[:, 0:n], hi[:, piece], lo[:, piece]
                masked = dve.do(lambda e, x=x, top=top: e.tensor_single_scalar(
                    top.bitcast(U32), x.bitcast(U32), HI_BITS, ALU.bitwise_and), *ready, *mask_freed, alone=True)
                hi_done = act_e.do(lambda e, hi_=hi_, top=top: e.activation(hi_, top, ACT.Copy), masked, *freed)
                lo_done = dve.do(lambda e, lo_=lo_, x=x, top=top: e.tensor_tensor(lo_, x, top, ALU.subtract),
                                 masked, *freed, alone=True)
                masks.free(tk, hi_done, lo_done)
            return hi_done, lo_done

        def fetch_split(src, ring):
            k, raw, loaded = fetch(src)
            n = src.shape[1]
            rk, r, freed = ring.take()
            hi, lo = r[:, 0, 0:n], r[:, 1, 0:n]
            made = split(raw, hi, lo, (loaded,), freed)
            slots.free(k, made[1])
            return rk, (hi, lo), made

        plan = [ins[name][i] for name in ("w_in", "w_dv", "w_out", "peer_q", "peer_u", "a_w_in", "a_w_out",
                                          "w_kvc", "w_kvs", "w_vsw", "w_gates", "b_q", "b_z", "b_w_out")
                for i in range(ins[name].shape[0])]
        prepared = []

        def prepare(n):
            while len(prepared) < n and plan:
                prepared.append(fetch_split(plan.pop(0), splits))

        def next_split():
            prepare(AHEAD + 1)
            return prepared.pop(0)

        def three(w, x):
            return [(w[0], x[0]), (w[0], x[1]), (w[1], x[0])]

        def linear_whole(src, kc, acts, ready):
            k, w, loaded = fetch(src)
            b, bank, freed = banks.take()
            w = w.rearrange("p (c n) -> p c n", c=kc)
            done = mm(bank, [(w[:, c, :], acts[c]) for c in range(kc)], loaded, *freed, *ready)
            slots.free(k, done)
            return b, bank, done

        def linear(n_chunks, acts, ready):
            b, bank, freed = banks.take()
            for n in range(n_chunks):
                k, w, made = next_split()
                w = [x.rearrange("p (c n) -> p c n", c=DC) for x in w]
                for c in range(DC):
                    first, last = n + c == 0, (n, c) == (n_chunks - 1, DC - 1)
                    done = mm(bank, three([x[:, c, :] for x in w], acts[n * DC + c]), *made, *freed,
                              *ready[n * DC + c], start=first, stop=last)
                splits.free(k, done)
            return b, bank, done

        def linear_tokens(n_chunks, per, acts, ready):
            got = [banks.take() for _ in range(TB)]
            done = None
            for s_ in range(n_chunks):
                k, w, made = next_split()
                w = [x.rearrange("p (c n) -> p c n", c=per) for x in w]
                for tb in range(TB):
                    rows = slice(tb * P, (tb + 1) * P)
                    pairs = [p for c in range(per) for p in
                             three([x[:, rows] for x in acts[s_ * per + c]], [x[:, c, :] for x in w])]
                    done = mm(got[tb][1], pairs, *made, *(m for c in range(per) for m in ready[s_ * per + c]),
                              *(got[tb][2] if s_ == 0 else ()), start=s_ == 0, stop=s_ == n_chunks - 1)
                splits.free(k, done)
            return [(g[0], g[1]) for g in got], done

        def squares_of(chunks, ones, ready):
            b, bank, freed = banks.take()
            for i, x in enumerate(chunks):
                k, sq, sq_freed = squares.take()
                squared = act_e.do(lambda e, sq=sq, x=x: e.activation(sq, x, ACT.Square), *ready, *sq_freed)
                done = mm(bank, [(ones, sq)], squared, *(freed if i == 0 else ()), start=i == 0,
                          stop=i == len(chunks) - 1)
                squares.free(k, done)
            return b, bank, done

        def rstd_of(b, bank, done, n):
            k, r, r_freed = rstds.take()
            nk, newton, n_freed = newtons.take()
            root = act_e.do(lambda e: e.activation(r, bank, ACT.Sqrt, bias=eps_col(n)), done, *r_freed)
            m = dve.do(lambda e: e.reciprocal(r, r), root, alone=True)
            m2 = dve.do(lambda e: e.tensor_tensor(newton, r, r, ALU.mult), m, *n_freed)
            m = dve.do(lambda e: e.scalar_tensor_tensor(newton, bank, n * EPS, newton, ALU.add, ALU.mult), m2)
            banks.free(b, m)
            dve.do(lambda e: e.tensor_scalar(newton, newton, -0.5, 1.5, ALU.mult, ALU.add))
            made = dve.do(lambda e: e.tensor_tensor(r, r, newton, ALU.mult))
            newtons.free(nk, made)
            return k, r, made

        def scaled(dst, x, gain, r, ready):
            return dve.do(lambda e: e.scalar_tensor_tensor(dst, x, gain, r, ALU.mult, ALU.mult), *ready, alone=True)

        def apply_norm(gain, shift, k, r, made):
            marks = []
            for c in range(DC):
                wk, whole, w_freed = wholes.take()
                m = last = scaled(whole, res[:, c, :], gain[:, c:c + 1], r, (made, *w_freed))
                if shift is not None:
                    m = act_e.do(lambda e, c=c, whole=whole: e.activation(whole, whole, ACT.Identity,
                                                                          bias=shift[:, c:c + 1]), m)
                both = split(whole, *act_hl[c], (m,))
                wholes.free(wk, both[1])
                marks.append(both)
            rstds.free(k, last)
            return marks

        def norm_model(gain, shift, ready):
            b, bank, done = squares_of([res[:, c, :] for c in range(DC)], const("ones"), ready)
            return apply_norm(gain, shift, *rstd_of(b, bank, done, D))

        def norm_stages(dst, src, ones, n, gain, done, freed, out_marks):
            sb_, ssq, s_done = squares_of([src], ones, (done,))
            yield
            k, r, made = rstd_of(sb_, ssq, s_done, n)
            m = scaled(dst, src, gain, r, (made, *freed))
            rstds.free(k, m)
            out_marks.append(m)

        def rope_stages(rings, parts, x, rot, cos, sin, ready, out_marks):
            cos_ring, sin_ring = rings
            b, bank, freed = banks.take()
            turned = mm(bank, [(rot, x)], ready, *freed)
            ck, tc, tc_freed = cos_ring.take()
            made = pool.do(lambda e: e.tensor_tensor(tc, x, cos, ALU.mult), ready, *tc_freed)
            yield
            sk, ts, ts_freed = sin_ring.take()
            m = dve.do(lambda e: e.tensor_tensor(ts, bank, sin, ALU.mult), turned, *ts_freed, alone=True)
            banks.free(b, m)
            for dst, rows in parts:
                m2 = dve.do(lambda e, dst=dst, rows=rows: e.tensor_tensor(dst, tc[rows, :], ts[rows, :], ALU.add),
                            made, m, alone=True)
            cos_ring.free(ck, m2)
            sin_ring.free(sk, m2)
            out_marks.append(m2)

        s_x, s_cols, s_consts = sem("x_loaded"), sem("cols_loaded"), sem("consts_loaded")
        cols_in = load(cols[:, :], ins["cols"], s_cols, 1)
        x_in = load(res[:, :, :].rearrange("p c t -> p (c t)"), ins["x"], s_x, 1)
        consts_in = load(consts[:, :], ins["consts"], s_consts, 1)

        spans = {}
        at = 0
        for name, n, factor in (("norm1", 8, D ** 0.5), ("norm2", 8, D ** 0.5), ("a_norm", 8, D ** 0.5),
                                ("kv_norm", 8, D ** 0.5), ("b_norm", 8, D ** 0.5), ("final", 8, D ** 0.5),
                                ("q_lat", 3, Q_LORA ** 0.5), ("kv_lat", 2, KV_LORA ** 0.5),
                                ("q_nope", 1, NOPE ** 0.5 * (NOPE + ROPE) ** -0.5),
                                ("q_pe", 1, ROPE ** 0.5 * (NOPE + ROPE) ** -0.5),
                                ("k_nope", 1, NOPE ** 0.5), ("k_pe", 1, ROPE ** 0.5),
                                ("dq", 1, 1.0), ("dk", 1, DIFF_DQK ** 0.5),
                                ("subln", 1, P ** 0.5 * (1.0 - LAMBDA_INIT))):
            g = gains[:, at:at + n]
            spans[name] = g
            dve.do(lambda e, g=g, name=name, n=n, f=factor: e.tensor_scalar(g, col(name, 0, n), f, None, ALU.mult),
                   cols_in)
            at += n

        silu_done = act_e.do(lambda e: e.activation(silu_c[:, :], col("c", 0, 8), ACT.Silu), cols_in)

        def modulation(first, n):
            b, bank, freed = banks.take()
            for j in range(first, first + n):
                k, w, loaded = fetch(ins["ada_w"][j])
                w = w.rearrange("p (c n) -> p c n", c=DC)
                done = mm(bank[:, j:j + 1], [(w[:, c, :], silu_c[:, c:c + 1]) for c in range(DC)],
                          loaded, silu_done, *freed)
                freed = ()
                slots.free(k, done)
            m = dve.do(lambda e: e.tensor_tensor(mod[:, first:first + n], bank[:, first:first + n],
                                                 col("ada_b", first, n), ALU.add), done)
            banks.free(b, m)
            return m

        def modulated_gain(dst, scale_at):
            return dve.do(lambda e: e.scalar_tensor_tensor(dst, mod[:, scale_at:scale_at + 8], 1.0, dst,
                                                           ALU.add, ALU.mult))

        x_squares = squares_of([res[:, c, :] for c in range(DC)], const("ones"), (x_in, consts_in))
        x_rstd = rstd_of(*x_squares, D)
        modulation(0, 16)
        gain_ready = modulated_gain(spans["norm1"], 8)
        act_e.wait(gain_ready)
        dve.wait(gain_ready)
        h_ready = apply_norm(spans["norm1"], mod[:, 0:8], *x_rstd)

        pos = [0]

        def view(n, *dims):
            a = arena[:, pos[0]:pos[0] + n]
            pos[0] += n
            assert pos[0] <= ARENA, pos[0]
            if len(dims) == 2:
                return a.rearrange("p (a b) -> p a b", a=dims[0])
            if len(dims) == 3:
                return a.rearrange("p (a b c) -> p a b c", a=dims[0], b=dims[1])
            return a

        q_nope = view(4 * S, 4, S)
        q_pe = view(2 * S, 2, S)
        k_nope = view(4 * S, 4, S)
        k_pe = view(2 * S, 2, S)
        v_mla = view(TB * S, TB, S)
        q_diff = view(4 * S, 4, S)
        k_diff = view(8 * S, 8, S)
        v_diff = view(TB * S, TB, S)
        head_end = pos[0]
        lat = view(3 * S, 3, S)
        normed_ring = Ring([view(S) for _ in range(4)])
        rope_rings = Ring([view(S) for _ in range(3)]), Ring([view(S) for _ in range(2)])
        halves = (slice(0, 64), slice(64, 128))

        for h in range(2):
            pool.do(lambda e, h=h: e.memset(k_pe[halves[1 - h], h, :], 0.0))
        for h in range(8):
            pool.do(lambda e, h=h: e.memset(k_diff[halves[1 - h % 2], h, :], 0.0))

        lats = [lat[:, c, :] for c in range(QC)]
        rope64 = (const("rot64"), const("cos"), const("sin"))

        def latent(n, gain):
            before = (pe.last, dve.last)
            for c in range(n):
                b, bank, done = linear(1, act_hl, h_ready)
                m = act_e.do(lambda e, c=c, bank=bank: e.activation(lat[:, c, :], bank, ACT.Copy), done, *before)
                banks.free(b, m)
            k, r, made = rstd_of(*squares_of([lat[:, c, :] for c in range(n)], const("ones"), (m,)), n * P)
            for c in range(n):
                m = scaled(lat[:, c, :], lat[:, c, :], gain[:, c:c + 1], r, (made,))
            rstds.free(k, m)
            return m

        def normed_head(make, dst, ones, n, gain):
            b, bank, done = make()
            yield
            got_ = []
            yield from norm_stages(dst, bank, ones, n, gain, done, (), got_)
            banks.free(b, got_[0])

        def rotated_head(make, gain, parts):
            b, bank, done = make()
            yield
            got_ = []
            nk, x, x_freed = normed_ring.take()
            yield from norm_stages(x, bank, const("ones64"), DIFF_DQK, gain, done, x_freed, got_)
            banks.free(b, got_[0])
            yield
            yield from rope_stages(rope_rings, parts, x, *rope64, got_[0], got_)
            normed_ring.free(nk, got_[1])

        def from_act():
            return lambda: linear(1, act_hl, h_ready)

        def from_lat(src, n, ready):
            return lambda: linear_whole(src, n, lats, (ready,))

        lat_ready = latent(KVC, spans["kv_lat"])
        skewed([normed_head(from_lat(ins["kv_up"][h], KVC, lat_ready), k_nope[:, h, :], const("ones"), NOPE,
                            spans["k_nope"]) for h in range(MLA_H)]
               + [rotated_head(from_act(), spans["k_pe"], [(k_pe[halves[j], j, :], halves[j]) for j in range(2)])])
        k, w, loaded = fetch(ins["kv_up_v"])
        w = w.rearrange("p (c n) -> p c n", c=KVC)
        for tb in range(TB):
            b, bank, freed = banks.take()
            done = mm(bank, [(lats[c][:, tb * P:(tb + 1) * P], w[:, c, :]) for c in range(KVC)], loaded, *freed)
            banks.free(b, act_e.do(lambda e, tb=tb, bank=bank: e.activation(v_mla[:, tb, :], bank, ACT.Copy), done))
        slots.free(k, done)
        lat_ready = latent(QC, spans["q_lat"])
        skewed([normed_head(from_lat(ins["q_up"][h], QC, lat_ready), q_nope[:, h, :], const("ones"), NOPE,
                            spans["q_nope"]) for h in range(MLA_H)]
               + [rotated_head(from_lat(ins["q_up"][MLA_H + j], QC, lat_ready), spans["q_pe"],
                               [(q_pe[:, j, :], slice(0, P))]) for j in range(2)]
               + [rotated_head(from_act(), spans["dq"], [(q_diff[:, h, :], slice(0, P))]) for h in range(DIFF_H)]
               + [rotated_head(from_act(), spans["dk"],
                               [(k_diff[halves[j], 2 * h + j, :], halves[j]) for j in range(2)])
                  for h in range(DIFF_H)])
        got, done = linear_tokens(4, 2, act_hl, h_ready)
        for tb, (b, bank) in enumerate(got):
            banks.free(b, act_e.do(lambda e, tb=tb, bank=bank: e.activation(v_diff[:, tb, :], bank, ACT.Copy), done))

        dve.do(lambda e: e.tensor_tensor(lam[:, 0:2], col("lam_q", 0, 2), col("lam_k", 0, 2), ALU.mult))
        b, bank, freed = banks.take()
        done = mm(bank[:, 0:2], [(const("ones"), lam[:, 0:2])], dve.last, *freed)
        m = act_e.do(lambda e, bank=bank: e.activation(lam[:, 2:4], bank[:, 0:2], ACT.Exp), done)
        banks.free(b, m)
        dve.do(lambda e: e.tensor_tensor(lam[:, 4:5], lam[:, 3:4], lam[:, 2:3], ALU.subtract), m)
        dve.do(lambda e: e.tensor_scalar(lam[:, 5:6], lam[:, 4:5], -LAMBDA_INIT, None, ALU.add))
        neg_lam = lam[:, 5:6]

        fence(act_e, dve, pe)
        pos[0] = head_end
        probs = Ring([view(S) for _ in range(5)])
        transposed = Ring([view(TB * S, TB, S) for _ in range(2)])
        stats = Ring([small[:, k, :] for k in range(8)])

        def exp_rows(score_pairs, qb):
            w = (qb + 1) * P
            b, bank, freed = banks.take()

            def emit(e):
                for n, (q, k) in enumerate(score_pairs):
                    e.matmul(bank[:, 0:w], q[:, qb * P:w], k[:, 0:w], start=n == 0, stop=False)
                return e.matmul(bank[:, w - P:w], const("ident"), const("mask"), start=False, stop=True)
            scored = pe.do(emit, *freed)
            sk, st, st_freed = stats.take()
            maxed = dve.do(lambda e: e.tensor_reduce(st[:, 0:1], bank[:, 0:w], AX_X, ALU.max, negate=True),
                           scored, *st_freed, alone=True)
            pk, p, p_freed = probs.take()
            exped = act_e.do(lambda e: e.activation(p[:, 0:w], bank[:, 0:w], ACT.Exp, bias=st[:, 0:1],
                                                    scale=1.0, accum_out=st[:, 1:2]), maxed, *p_freed)
            banks.free(b, exped)
            return pk, p[:, 0:w], sk, st, exped

        def transpose_rows(p, qb, dst, ready, freed, on):
            b, bank, b_freed = banks.take()

            def emit(e):
                for kb in range(qb + 1):
                    last = e.transpose(bank[:, kb * P:(kb + 1) * P], p[:, kb * P:(kb + 1) * P], const("ident"))
                return last
            turned = pe.do(emit, ready, *b_freed)
            src = bank[:, 0:(qb + 1) * P].rearrange("p (k q) -> p k q", q=P)
            to = dst[:, 0:qb + 1, qb * P:(qb + 1) * P]
            if on is dve:
                m = dve.do(lambda e: e.tensor_copy(to, src), turned, *freed, alone=True)
            else:
                m = act_e.do(lambda e: e.activation(to, src, ACT.Copy), turned, *freed)
            banks.free(b, m)
            return turned, m

        def values_mm(out_, v, turned, ready, first, last, *freed):
            def emit(e):
                for kb in range(TB):
                    x = e.matmul(out_[:, kb * P:S], v(kb), turned[:, kb, kb * P:S], start=first and kb == 0,
                                 stop=last and kb == TB - 1)
                return x
            return pe.do(emit, *ready, *freed)

        state = {}
        mixed_marks = [None] * DC

        def attend(h, qb):
            hd = h % 4
            if h < MLA_H:
                pk, p, sk, st, exped = exp_rows(
                    [(q_nope[:, h, :], k_nope[:, h, :]), (q_pe[:, h // 2, :], k_pe[:, h % 2, :])], qb)
                yield
                m = dve.do(lambda e: e.reciprocal(st[:, 2:3], st[:, 1:2]), exped, alone=True)
                m = dve.do(lambda e: e.tensor_scalar(p, p, st[:, 2:3], None, ALU.mult), m)
                stats.free(sk, m)
            else:
                pk, p, sk, st, exped = exp_rows([(q_diff[:, hd, :], k_diff[:, 2 * hd, :])], qb)
                pk2, p2, sk2, st2, exped2 = exp_rows([(q_diff[:, hd, :], k_diff[:, 2 * hd + 1, :])], qb)
                yield
                a = dve.do(lambda e: e.reciprocal(st[:, 2:3], st[:, 1:2]), exped, alone=True)
                b_ = dve.do(lambda e: e.reciprocal(st2[:, 2:3], st2[:, 1:2]), exped2, alone=True)
                m = dve.do(lambda e: e.tensor_scalar(p, p, st[:, 2:3], None, ALU.mult), a, alone=True)
                m2 = dve.do(lambda e: e.tensor_tensor(st2[:, 3:4], st2[:, 2:3], neg_lam, ALU.mult), b_, alone=True)
                stats.free(sk, m)
                m = dve.do(lambda e: e.scalar_tensor_tensor(p, p2, st2[:, 3:4], p, ALU.mult, ALU.add), m, m2)
                stats.free(sk2, m)
                probs.free(pk2, m)
            yield
            if qb == 0:
                state["t"] = transposed.take()
            tk, t, t_freed = state["t"]
            turned, copied = transpose_rows(p, qb, t, m, t_freed, act_e if qb % 2 else dve)
            state[qb] = copied
            probs.free(pk, turned)
            if qb < TB - 1:
                return
            b, bank, freed = banks.take()
            v = v_mla if h < MLA_H else v_diff
            done = values_mm(bank, lambda kb: v[:, kb, hd * P:(hd + 1) * P], t, [state[q] for q in range(TB)],
                             True, True, *freed)
            transposed.free(tk, done)
            wk, whole, w_freed = wholes.take()
            if h < MLA_H:
                m = act_e.do(lambda e: e.activation(whole, bank, ACT.Copy), done, *w_freed)
            else:
                yield
                got_ = []
                yield from norm_stages(whole, bank, const("ones"), P, spans["subln"], done, w_freed, got_)
                m = got_[0]
            banks.free(b, m)
            both = split(whole, *act_hl[h], (m,))
            wholes.free(wk, both[1])
            mixed_marks[h] = both

        def modulate(first, n):
            modulation(first, n)
            yield

        tasks, at = [], 16
        for h in range(MLA_H + DIFF_H):
            tasks += [attend(h, qb) for qb in range(TB)]
            tasks.append(modulate(at, 4))
            at += 4
        assert at == 48
        skewed(tasks)
        mod_ready = dve.last

        def project_back(per, acts_, ready, gate):
            for n in range(DC):
                b, bank, done = linear(per, acts_, ready)
                g = gate[:, n:n + 1] if gate is not None else 1.0
                m = dve.do(lambda e, n=n, bank=bank, g=g: e.scalar_tensor_tensor(
                    res[:, n, :], bank, g, res[:, n, :], ALU.mult, ALU.add), done, alone=True)
                banks.free(b, m)
            return m

        x1 = project_back(1, act_hl, mixed_marks, mod[:, 16:24])

        modulated_gain(spans["norm2"], 32)
        fence(act_e, dve)
        dve.wait(dve.last)
        h2_ready = norm_model(spans["norm2"], mod[:, 24:32], (x1, mod_ready))

        fence()
        s_tables = sem("tables_loaded")
        a = CONSTS["cos"][0]
        tables_in = load(consts[:, a:a + 2 * S], ins["tables2"], s_tables, 1)
        pos[0] = 0
        peer_q = view(HP * S, HP, S)
        g_t = view(S)
        i_t = view(S)
        j_t = view(S)
        after_q = pos[0]
        keys = view(HP * P, HP, P)
        top_s = view(HP * P, HP, P)
        replaced = view(P)
        sums_b = view(256)
        topv = view(HP * TOPK, HP, TOPK)
        topi_u = view(HP * TOPK, HP, TOPK).bitcast(U32)
        topi = view(HP * TOPK, HP, TOPK)
        cand = view(PEER_H * 256, PEER_H, 256)
        fv = view(HK, PEER_H, TOPK)
        fpos = view(HK, PEER_H, TOPK).bitcast(U32)
        part_u = view(HK, PEER_H, TOPK).bitcast(U32)
        part = view(HK, PEER_H, TOPK)
        picked = view(HK * TOPK)
        gij = view(3 * HK, 3, HK)
        gsum = view(PEER_H)

        s_keys = sem("keys_loaded")
        keys_in = load(keys.rearrange("p a b -> p (a b)"), ins["keys"], s_keys, 1)
        for hp in range(HP):
            b, bank, done = linear(1, act_hl, h2_ready)
            if hp % 2:
                m = dve.do(lambda e, hp=hp, bank=bank: e.tensor_copy(peer_q[:, hp, :], bank), done, alone=True)
            else:
                m = act_e.do(lambda e, hp=hp, bank=bank: e.activation(peer_q[:, hp, :], bank, ACT.Copy), done)
            banks.free(b, m)
        q_marks = (dve.last, act_e.last)

        def top16(vals, idx, src, scratch):
            dve.do(lambda e: e.max(vals[:, 0:8], src))
            dve.do(lambda e: e.max_index(idx[:, 0:8], vals[:, 0:8], src))
            dve.do(lambda e: e.match_replace(scratch, vals[:, 0:8], src, -3e38))
            dve.do(lambda e: e.max(vals[:, 8:16], scratch))
            return dve.do(lambda e: e.max_index(idx[:, 8:16], vals[:, 8:16], scratch))

        iota16 = const("iota")[:, 0:TOPK]

        def pick(dst, half):
            p3 = picked.rearrange("p (a b) -> p a b", b=TOPK)
            p4 = picked.rearrange("p (h k b) -> p h k b", h=PEER_H, k=TOPK)
            flat = part.rearrange("p h k -> p (h k)").unsqueeze(2).broadcast_to([P, HK, TOPK])
            dve.do(lambda e: e.tensor_tensor(p3, flat, iota16.unsqueeze(1).broadcast_to([P, HK, TOPK]), ALU.is_equal))
            lists = topi.rearrange("p (h two) k -> p h two k", two=2)[:, :, half, :]
            dve.do(lambda e: e.tensor_tensor(p4, p4, lists.unsqueeze(2).broadcast_to([P, PEER_H, TOPK, TOPK]),
                                             ALU.mult))
            return dve.do(lambda e: e.tensor_reduce(dst, p3, AX_X, ALU.add))

        for tb in range(TB):
            for quad in range(HP // 4):
                b, bank, freed = banks.take()

                def emit(e, quad=quad, bank=bank, tb=tb):
                    for j in range(4):
                        hp = 4 * quad + j
                        last = e.matmul(bank[:, j * P:(j + 1) * P], peer_q[:, hp, tb * P:(tb + 1) * P],
                                        keys[:, hp, :], start=True, stop=True)
                    return last
                done = pe.do(emit, *q_marks, keys_in, *freed)
                m = act_e.do(lambda e, quad=quad, bank=bank: e.activation(
                    top_s[:, 4 * quad:4 * quad + 4, :], bank.rearrange("p (a b) -> p a b", a=4), ACT.Copy),
                    done, dve.last)
                banks.free(b, m)
            dve.wait(m)
            for hp in range(HP):
                top16(topv[:, hp, :], topi_u[:, hp, :], top_s[:, hp, :], replaced)
            dve.do(lambda e: e.tensor_copy(topi, topi_u))
            v4 = topv.rearrange("p (h two) k -> p h two k", two=2)
            dve.do(lambda e: e.tensor_tensor(
                cand.rearrange("p h (a b) -> p h a b", a=TOPK),
                v4[:, :, 0, :].unsqueeze(3).broadcast_to([P, PEER_H, TOPK, TOPK]),
                v4[:, :, 1, :].unsqueeze(2).broadcast_to([P, PEER_H, TOPK, TOPK]), ALU.add))
            for h in range(PEER_H):
                top16(fv[:, h, :], fpos[:, h, :], cand[:, h, :], sums_b)
            dve.do(lambda e: e.tensor_tensor(gij[:, 0, :].rearrange("p (h k) -> p h k", h=PEER_H), fv,
                                             fv[:, :, 0:1].broadcast_to([P, PEER_H, TOPK]), ALU.subtract),
                   pe.last)
            exped = act_e.do(lambda e: e.activation(gij[:, 0, :], gij[:, 0, :], ACT.Exp), dve.last)
            dve.do(lambda e: e.tensor_single_scalar(part_u, fpos, 4, ALU.logical_shift_right))
            dve.do(lambda e: e.tensor_copy(part, part_u))
            pick(gij[:, 1, :], 0)
            dve.do(lambda e: e.tensor_single_scalar(part_u, fpos, 15, ALU.bitwise_and))
            dve.do(lambda e: e.tensor_copy(part, part_u))
            pick(gij[:, 2, :], 1)
            g3 = gij[:, 0, :].rearrange("p (h k) -> p h k", h=PEER_H)
            dve.do(lambda e: e.tensor_reduce(gsum, g3, AX_X, ALU.add), exped)
            dve.do(lambda e: e.reciprocal(gsum, gsum))
            m = dve.do(lambda e: e.tensor_tensor(g3, g3, gsum.unsqueeze(2).broadcast_to([P, PEER_H, TOPK]), ALU.mult))
            b, bank, freed = banks.take()

            def emit(e, bank=bank):
                for j in range(3):
                    last = e.transpose(bank[:, j * P:(j + 1) * P], gij[:, j, :], const("ident"))
                return last
            done = pe.do(emit, m, *freed)
            for j, dst in enumerate((g_t, i_t, j_t)):
                m = dve.do(lambda e, j=j, dst=dst, bank=bank, tb=tb: e.tensor_copy(
                    dst[:, tb * P:(tb + 1) * P], bank[:, j * P:(j + 1) * P]), done)
            banks.free(b, m)

        fence()
        pos[0] = after_q
        stage_a = peer_q.rearrange("p a b -> p (a b)").rearrange("p (i t) -> p i t", t=GT)
        stage_b = view(GT * P, P, GT)
        stages = Ring([stage_a, stage_b])
        hot_i = Ring([view(4 * P, 4, P) for _ in range(3)])
        hot_j = Ring([view(4 * P, 4, P) for _ in range(3)])
        dve.wait(dve.last)
        s_gates = [sem("gates_stored_a"), sem("gates_stored_b")]
        stores = [0, 0]
        for t0 in range(0, S, GT):
            gk, stage, stage_freed = stages.take()
            for q0 in range(t0, t0 + GT, 4):
                ik, hi, i_freed = hot_i.take()
                jk, hj, j_freed = hot_j.take()
                dve.wait(*i_freed, *j_freed)
                for j in range(4):
                    t = q0 + j
                    m = dve.do(lambda e, hi=hi, j=j, t=t: e.tensor_scalar(
                        hi[:, j, :], const("iota"), i_t[:, t:t + 1], g_t[:, t:t + 1], ALU.is_equal, ALU.mult),
                        alone=True)
                for j in range(4):
                    t = q0 + j
                    m2 = dve.do(lambda e, hj=hj, j=j, t=t: e.tensor_scalar(
                        hj[:, j, :], const("iota"), j_t[:, t:t + 1], None, ALU.is_equal), alone=True)
                b, bank, freed = banks.take()

                def emit(e, bank=bank, hi=hi, hj=hj):
                    for j in range(4):
                        last = e.matmul(bank[:, j * P:(j + 1) * P], hj[:, j, :], hi[:, j, :], start=True, stop=True)
                    return last
                done = pe.do(emit, m, m2, *freed)
                hot_i.free(ik, done)
                hot_j.free(jk, done)
                src = bank.rearrange("p (t i) -> p i t", i=P)
                m = act_e.do(lambda e, stage=stage, src=src, a=q0 - t0: e.activation(
                    stage[:, :, a:a + 4], src, ACT.Copy), done, *stage_freed)
                banks.free(b, m)
            stores[gk] += 1
            stages.free(gk, load(gates_dram[:, :, t0:t0 + GT].rearrange("i j t -> j i t"), stage, s_gates[gk],
                                 stores[gk], m))
        gates_ready = [(s_gates[k], 16 * stores[k]) for k in range(2)]

        fence()
        for line in (sync, act_e, dve):
            line.wait(*gates_ready)
        pos[0] = 0
        gate_tiles = [view(S) for _ in range(4)]
        gelus = Ring([view(S)])
        coef_whole = Ring([view(S)])

        def views_r(n, width):
            base = pos[0]
            view(n * 2 * width)
            return [arena_r[:, base + k * 2 * width:base + (k + 1) * 2 * width].rearrange("p (s t) -> p s t", s=2)
                    for k in range(n)]

        coefs = Ring(views_r(EG + 2, S))
        down_w = Ring(views_r(EG + 2, SLOT))
        gate_sems = [sem(f"gate{k}_loaded") for k in range(4)]
        gate_loads = [0] * 4
        gates = Ring(gate_tiles)

        def expert_gates(i):
            k, tile, freed = gates.take()
            gate_loads[k] += 1
            return k, tile, load(tile, gates_dram[i], gate_sems[k], gate_loads[k], *freed)

        def split_down():
            i = len(v_split)
            if i < NKEYS:
                v_split.append(fetch_split(ins["peer_v"][i], down_w))

        def down(i0):
            prepare(AHEAD + 1)
            for c in range(DC):
                b, bank, freed = banks.take()
                for i in range(i0, i0 + EG):
                    (_, coef, ready), (_, w, made) = coef_split[i], v_split[i]
                    done = mm(bank, three([x[:, c * P:(c + 1) * P] for x in w], coef), *ready, *made, *freed,
                              start=i == i0, stop=i == i0 + EG - 1)
                m = dve.do(lambda e, c=c, bank=bank: e.scalar_tensor_tensor(
                    res[:, c, :], bank, mod[:, 40 + c:41 + c], res[:, c, :], ALU.mult, ALU.add), done, alone=True)
                banks.free(b, m)
                if c == 3:
                    split_down()
            for i in range(i0, i0 + EG):
                coefs.free(coef_split[i][0], done)
                down_w.free(v_split[i][0], done)

        coef_split, v_split = [], []
        for i in range(NKEYS):
            gk, gate, gate_in = expert_gates(i)
            b, bank, done = linear(1, act_hl, h2_ready)
            if len(v_split) <= i:
                split_down()
            ak, a, a_freed = gelus.take()
            gelu = act_e.do(lambda e, a=a, bank=bank: e.activation(a, bank, ACT.Gelu), done, *a_freed)
            banks.free(b, gelu)
            hk, whole, h_freed = coef_whole.take()
            m = dve.do(lambda e, whole=whole, a=a, gate=gate: e.tensor_tensor(whole, a, gate, ALU.mult),
                       gelu, gate_in, *h_freed, alone=True)
            gelus.free(ak, m)
            gates.free(gk, m)
            ck, coef, c_freed = coefs.take()
            both = split(whole, coef[:, 0, :], coef[:, 1, :], (m,), c_freed)
            coef_whole.free(hk, both[1])
            coef_split.append((ck, (coef[:, 0, :], coef[:, 1, :]), both))
            if i >= EG and i % EG == 0:
                down(i - EG)
        down(NKEYS - EG)

        fence()
        dve.wait(dve.last)
        h_ready = norm_model(spans["a_norm"], None, (dve.last,))
        conv_y = arena_r[:, 0:2 * CC * S].rearrange("p (s c t) -> p s c t", s=2, c=CC)
        conv_hl = [(conv_y[:, 0, c, :], conv_y[:, 1, c, :]) for c in range(CC)]
        conv_marks = []
        pos[0] = 2 * CC * S
        padded = Ring([view(S + 2) for _ in range(2)])
        work = Ring([view(S) for _ in range(8)])
        for k in range(2):
            pool.do(lambda e, k=k: e.memset(padded.items[k][:, 0:2], 0.0))
        dve.wait(pool.last)

        for n in range(CC):
            got = [linear(1, act_hl, h_ready) for _ in ("c", "u", "b", "z")]
            (bc, c_bank, c_done), (bu, u_bank, u_done), (bb, b_bank, b_done), (bz, z_bank, z_done) = got
            wc, c_sb, c_freed = work.take()
            m = act_e.do(lambda e, c_sb=c_sb, c_bank=c_bank: e.activation(c_sb, c_bank, ACT.Copy), c_done, *c_freed)
            banks.free(bc, m)
            vk, vp, v_freed = padded.take()
            m = dve.do(lambda e, vp=vp, c_sb=c_sb, u_bank=u_bank: e.tensor_tensor(vp[:, 2:S + 2], c_sb, u_bank,
                                                                                ALU.mult), m, u_done, *v_freed)
            banks.free(bu, m)
            work.free(wc, m)
            wz, z_sb, z_freed = work.take()
            zm = act_e.do(lambda e, z_sb=z_sb, z_bank=z_bank: e.activation(z_sb, z_bank, ACT.Silu), z_done, *z_freed)
            banks.free(bz, zm)
            wt, acc, a_freed = work.take()
            dve.do(lambda e, acc=acc, vp=vp, n=n: e.tensor_scalar(acc, vp[:, 0:S], col("conv", n), None, ALU.mult),
                   *a_freed)
            for k in (1, 2):
                m = dve.do(lambda e, acc=acc, vp=vp, n=n, k=k: e.scalar_tensor_tensor(
                    acc, vp[:, k:k + S], col("conv", k * CC + n), acc, ALU.mult, ALU.add))
            padded.free(vk, m)
            m = dve.do(lambda e, acc=acc, b_bank=b_bank: e.tensor_tensor(acc, acc, b_bank, ALU.mult), b_done)
            banks.free(bb, m)
            m = pool.do(lambda e, acc=acc, z_sb=z_sb: e.tensor_tensor(acc, acc, z_sb, ALU.mult), m, zm)
            work.free(wz, m)
            both = split(acc, *conv_hl[n], (m,))
            work.free(wt, both[1])
            conv_marks.append(both)
        x3 = project_back(2, conv_hl, conv_marks, None)

        fence()
        dve.wait(x3)
        kv_ready = norm_model(spans["kv_norm"], None, (x3,))
        pos[0] = 0
        k_slc = view(GROUPS * S, GROUPS, S)
        k_win = view(GROUPS * S, GROUPS, S)
        v_sw = view(TB * S, TB, S)
        kcmp = view(GROUPS * NCP, GROUPS, NCP)
        vcmp = view(GROUPS * GROUPS * HD, GROUPS, GROUPS * HD)
        gate_rows = view(TB * 48, TB, 48)
        hidden = view(4 * P, 4, P)
        bias_cols = view(4)
        after_kv = pos[0]
        strm = [view(GROUPS * 528, GROUPS, 528) for _ in range(2)]
        pe_cols = view(32)
        w2 = view(2 * P * 2 , 2, 2 * P)
        hidden_v = view(2 * GROUPS * P, 2 * GROUPS, P)
        raw_keys = Ring([view(S) for _ in range(3)])
        rope_rings = Ring([view(S) for _ in range(2)]), Ring([view(S) for _ in range(2)])
        s_pos, s_w2 = sem("pos_loaded"), sem("w2_loaded")
        pos_in = load(pe_cols, ins["cmp_pos"], s_pos, 1)
        w2_in = load(w2.rearrange("p a b -> p (a b)"), ins["cmp_w2"], s_w2, 1)
        for g in range(GROUPS):
            other = halves[1 - g % 2]
            for t in (k_slc, k_win, kcmp):
                pool.do(lambda e, t=t, g=g, other=other: e.memset(t[other, g, :], 0.0))
        pool.do(lambda e: e.memset(vcmp, 0.0))
        for t in strm:
            pool.do(lambda e, t=t: e.memset(t[:, :, S - 1:528], 0.0))
        zeroed = pool.last

        for which in range(2):
            for g in range(GROUPS):
                b, bank, done = linear(1, act_hl, kv_ready)
                t = strm[which]
                m = act_e.do(lambda e, t=t, g=g, bank=bank: e.activation(t[0:64, g, 0:S], bank[0:64, :], ACT.Copy),
                             done, zeroed)
                m2 = dve.do(lambda e, t=t, g=g, bank=bank: e.tensor_copy(t[64:128, g, 0:S - 1], bank[64:128, 1:S]),
                            done, zeroed)
                banks.free(b, m, m2)
        strm_ready = (act_e.last, dve.last)
        pool.wait(tables_in)
        dve.wait(tables_in)
        rope16 = (const("rot16"), const("cos"), const("sin"))

        def rotated_keys(which, m_, dst):
            b, bank, done = linear(1, act_hl, kv_ready)
            xk, x, x_freed = raw_keys.take()
            m = act_e.do(lambda e: e.activation(x, bank, ACT.Copy), done, *x_freed)
            banks.free(b, m)
            yield
            got_ = []
            yield from rope_stages(rope_rings, [(dst[halves[j], 2 * m_ + j, :], halves[j]) for j in range(2)], x,
                                   *rope16, m, got_)
            raw_keys.free(xk, got_[0])

        skewed([rotated_keys(which, m_, dst) for which, dst in enumerate((k_slc, k_win)) for m_ in range(2)])
        got, done = linear_tokens(4, 2, act_hl, kv_ready)
        for tb, (b, bank) in enumerate(got):
            banks.free(b, act_e.do(lambda e, tb=tb, bank=bank: e.activation(v_sw[:, tb, :], bank, ACT.Copy), done))

        for which in range(2):
            w1 = [fetch(ins["cmp_w1"][which * 4 + i]) for i in range(4)]
            w1v = [w.rearrange("p (l n) -> p l n", l=4) for _, w, _ in w1]
            loaded = [x[2] for x in w1]
            for hc in range(2):
                b, bank, freed = banks.take()
                b2, bank2, freed2 = banks.take()

                def emit(e, which=which, hc=hc, bank=bank, bank2=bank2, w1v=w1v):
                    for l in range(CMP_PAIRS):
                        e.matmul(bank[:, 0:1], w1v[l // 4][:, l % 4, hc * P:(hc + 1) * P],
                                 pe_cols[:, which * 16 + l:which * 16 + l + 1], start=l == 0, stop=l == CMP_PAIRS - 1)
                    for l in range(CMP_PAIRS):
                        a = 2 * l
                        last = e.matmul(bank2[:, 0:P].rearrange("p (g n) -> p g n", g=GROUPS),
                                        w1v[l // 4][:, l % 4, hc * P:(hc + 1) * P],
                                        strm[which][:, :, a:a + CMP_STRIDE * (NCP - 1) + 1:CMP_STRIDE],
                                        start=l == 0, stop=l == CMP_PAIRS - 1)
                    return last
                done = pe.do(emit, *loaded, *strm_ready, pos_in, *freed, *freed2)
                slot = which * 2 + hc
                m = dve.do(lambda e, slot=slot, bank=bank: e.tensor_copy(bias_cols[:, slot:slot + 1], bank[:, 0:1]),
                           done)
                banks.free(b, m)
                m = act_e.do(lambda e, slot=slot, bank2=bank2: e.activation(
                    hidden[:, slot, :], bank2[:, 0:P], ACT.Gelu_apprx_tanh, bias=bias_cols[:, slot:slot + 1]), m)
                banks.free(b2, m)
            for k, _, _ in w1:
                slots.free(k, done)
        b, bank, freed = banks.take()
        done = mm(bank[:, 0:P], [(w2[:, hc, 0:P], hidden[:, hc, :]) for hc in range(2)], m, w2_in, *freed)
        for g in range(GROUPS):
            hf = halves[g % 2]
            m = dve.do(lambda e, g=g, hf=hf, bank=bank: e.tensor_copy(kcmp[hf, g, :], bank[hf, g * NCP:(g + 1) * NCP]),
                       done)
        banks.free(b, m)
        m4 = dve.do(lambda e: e.tensor_copy(
            hidden_v.rearrange("p a (i n) -> p a i n", i=GROUPS),
            hidden[:, 2:4, :].rearrange("p c (g n) -> p (c g) n", g=GROUPS).unsqueeze(2).broadcast_to(
                [P, 2 * GROUPS, GROUPS, NCP])), act_e.last)
        b, bank, freed = banks.take()

        def emit(e, bank=bank):
            for g in range(GROUPS):
                for hc in range(2):
                    last = e.matmul(bank[:, g * HD:(g + 1) * HD], hidden_v[:, hc * GROUPS + g, :], w2[:, hc, P:P + HD], start=hc == 0,
                                    stop=hc == 1)
            return last
        done = pe.do(emit, m4, *freed)
        for g in range(GROUPS):
            for i in range(GROUPS):
                rows = slice(i * NCP, (i + 1) * NCP)
                m = dve.do(lambda e, g=g, i=i, rows=rows, bank=bank: e.tensor_copy(
                    vcmp[rows, g, i * HD:(i + 1) * HD], bank[rows, g * HD:(g + 1) * HD]), done)
        banks.free(b, m)

        fence()
        hb_ready = norm_model(spans["b_norm"], None, ())
        pos[0] = after_kv
        q_raw = view(DC * S, DC, S)
        z_ring = Ring([view(S) for _ in range(2)])
        rope_mem = [view(S) for _ in range(4)]
        rope_rings = Ring(rope_mem[0:2]), Ring(rope_mem[2:4])
        pc_t = view(GROUPS * S, GROUPS, S)
        cmp_mem = view(NSA_H * NCP)
        cmp_p = cmp_mem.rearrange("p (h n) -> p h n", n=NCP)
        cmp_st = view(4 * NSA_H)

        got_g = banks.take()
        k, w, made = next_split()
        w = [x.rearrange("p (c n) -> p c n", c=DC) for x in w]
        for tb in range(TB):
            rows = slice(tb * P, (tb + 1) * P)
            done = mm(got_g[1][:, tb * 48:(tb + 1) * 48],
                      [p for c in range(DC) for p in three([x[:, rows] for x in act_hl[c]], [x[:, c, :] for x in w])],
                      *made, *got_g[2], *(m for marks in hb_ready for m in marks))
        splits.free(k, done)
        m = act_e.do(lambda e: e.activation(gate_rows.rearrange("p a b -> p (a b)"), got_g[1][:, 0:TB * 48],
                                            ACT.Sigmoid), done)
        banks.free(got_g[0], m)
        for c in range(DC):
            b, bank, done = linear(1, act_hl, hb_ready)
            m = act_e.do(lambda e, c=c, bank=bank: e.activation(q_raw[:, c, :], bank, ACT.Copy, scale=HD ** -0.5), done)
            banks.free(b, m)
        q_ready = act_e.last
        gates4 = gate_rows.rearrange("p t (h b) -> p t h b", b=3)

        for qb in range(TB):
            b, bank, freed = banks.take()

            def emit(e, qb=qb, bank=bank):
                for c in range(DC):
                    for j in range(2):
                        g = 2 * (c // 4) + j
                        n = g * 4 + c % 4
                        last = e.matmul(bank[:, n * NCP:(n + 1) * NCP], q_raw[:, c, qb * P:(qb + 1) * P],
                                        kcmp[:, g, :], start=True, stop=True)
                return last
            done = pe.do(emit, q_ready, dve.last, *freed)
            s3 = bank.rearrange("p (h n) -> p h n", n=NCP)
            wide = [P, NSA_H, NCP]
            a0, b0 = qb * NCP, (qb + 1) * NCP
            add = const("cmp_add")[:, a0:b0].unsqueeze(1).broadcast_to(wide)
            mul = const("cmp_mul")[:, a0:b0].unsqueeze(1).broadcast_to(wide)
            mx, sm = cmp_st[:, 0:16], cmp_st[:, 16:32]
            m = dve.do(lambda e, s3=s3, add=add: e.tensor_tensor(cmp_p, s3, add, ALU.add), done, pe.last)
            banks.free(b, m)
            dve.do(lambda e: e.tensor_reduce(mx, cmp_p, AX_X, ALU.max))
            m = dve.do(lambda e: e.tensor_tensor(cmp_p, cmp_p, mx.unsqueeze(2).broadcast_to(wide), ALU.subtract))
            m = act_e.do(lambda e: e.activation(cmp_p, cmp_p, ACT.Exp), m)
            dve.do(lambda e, mul=mul: e.tensor_tensor(cmp_p, cmp_p, mul, ALU.mult), m)
            dve.do(lambda e: e.tensor_reduce(sm, cmp_p, AX_X, ALU.add))
            dve.do(lambda e: e.tensor_scalar(sm, sm, 1e-30, None, ALU.max))
            dve.do(lambda e: e.reciprocal(sm, sm))
            dve.do(lambda e, qb=qb: e.tensor_tensor(sm, sm, gates4[:, qb, :, 0], ALU.mult))
            m = dve.do(lambda e: e.tensor_tensor(cmp_p, cmp_p, sm.unsqueeze(2).broadcast_to(wide), ALU.mult))
            b, bank, freed = banks.take()

            def emit(e, bank=bank):
                for g in range(GROUPS):
                    last = e.transpose(bank[:, g * P:(g + 1) * P],
                                       cmp_p[:, 4 * g:4 * g + 4, :].rearrange("p h n -> p (h n)"), const("ident"))
                return last
            done = pe.do(emit, m, *freed)
            m = act_e.do(lambda e, qb=qb, bank=bank: e.activation(
                pc_t[:, :, qb * P:(qb + 1) * P], bank.rearrange("p (g q) -> p g q", g=GROUPS), ACT.Copy), done)
            banks.free(b, m)
        pc_ready = act_e.last
        after_cmp = pos[0]

        def rotated_queries(c):
            yield from rope_stages(rope_rings, [(q_raw[:, c, :], slice(0, P))], q_raw[:, c, :], *rope16, q_ready, [])

        skewed([rotated_queries(c) for c in range(DC)])
        q_rot = q_raw

        fence(dve, act_e, pe)
        probs = Ring([*rope_mem, cmp_mem])
        turned_ring = Ring([[view(TB * S, TB, S) for _ in range(2)]])
        nsa, y_marks = {}, []

        def nsa_attend(c, j, qb, branch):
            g = 2 * (c // 4) + j
            i = c % 4
            keys_ = (k_slc, k_win)[branch]
            pk, p, sk, st, exped = exp_rows([(q_rot[:, c, :], keys_[:, g, :])], qb)
            yield
            gate = gates4[:, qb, g * 4 + i, branch + 1:branch + 2]
            m = dve.do(lambda e: e.reciprocal(st[:, 2:3], st[:, 1:2]), exped, alone=True)
            m = dve.do(lambda e: e.tensor_tensor(st[:, 3:4], st[:, 2:3], gate, ALU.mult), m)
            m = dve.do(lambda e: e.tensor_scalar(p, p, st[:, 3:4], None, ALU.mult), m)
            stats.free(sk, m)
            yield
            if qb == 0 and branch == 0:
                nsa["t"] = turned_ring.take()
            tk, t, t_freed = nsa["t"]
            turned, copied = transpose_rows(p, qb, t[branch], m, t_freed, act_e if branch else dve)
            nsa[qb, branch] = copied
            probs.free(pk, turned)
            if (qb, branch) != (TB - 1, 1):
                return
            if j == 0:
                nsa["bank"] = banks.take()
            b, bank, freed = nsa["bank"]
            o = bank[halves[j], :]
            marks = [nsa[q, br] for q in range(TB) for br in range(2)]
            for br in range(2):
                values_mm(o, lambda kb, br=br: v_sw[:, kb, br * 256 + g * HD:br * 256 + (g + 1) * HD], t[br],
                          marks if br == 0 else (), br == 0, False, *(freed if br == 0 else ()))
            done = pe.do(lambda e: e.matmul(o, vcmp[:, g, i * HD:(i + 1) * HD], pc_t[:, g, :], start=False, stop=True),
                         pc_ready)
            turned_ring.free(tk, done)
            if j == 0:
                return
            yield
            zb, z_bank, z_done = linear(1, act_hl, hb_ready)
            zk, z, z_freed = z_ring.take()
            zm = act_e.do(lambda e: e.activation(z, z_bank, ACT.Silu), z_done, *z_freed)
            banks.free(zb, zm)
            m = dve.do(lambda e: e.tensor_tensor(q_rot[:, c, :], bank, z, ALU.mult), zm, done, alone=True)
            banks.free(b, m)
            z_ring.free(zk, m)
            y_marks.append(m)

        skewed([nsa_attend(c, j, qb, branch) for c in range(DC) for j in range(2) for qb in range(TB)
                for branch in range(2)])
        fence(act_e, dve)
        y_split = [split(q_rot[:, c, :], *act_hl[c], (y_marks[c],)) for c in range(DC)]
        x4 = project_back(1, act_hl, y_split, None)

        fence(dve, act_e)
        pos[0] = 0
        result = view(DC * S, DC, S)
        k, r, made = rstd_of(*squares_of([res[:, c, :] for c in range(DC)], const("ones"), (x4,)), D)
        s_out = sem("out_stored")
        for c in range(DC):
            m = scaled(result[:, c, :], res[:, c, :], spans["final"][:, c:c + 1], r, (made,))
            stored = load(out[c], result[:, c, :], s_out, c + 1, m)
        sync.wait(stored)

        with nc.Block() as block:
            @block.sync
            def _(e):
                sync.run(e)

            @block.tensor
            def _(e):
                pe.run(e)

            @block.vector
            def _(e):
                dve.run(e)

            @block.scalar
            def _(e):
                act_e.run(e)

            @block.gpsimd
            def _(e):
                pool.run(e)


def rotation(dim, block):
    r = np.zeros((P, P), np.float32)
    for b in range(0, P, block):
        for i in range(dim // 2):
            r[b + i + dim // 2, b + i] = -1.0
            r[b + i, b + i + dim // 2] = 1.0
    return r


def make_consts():
    c = np.zeros((P, NCONSTS), np.float32)

    def put(name, a):
        c[:, CONSTS[name][0]:CONSTS[name][1]] = a

    put("ident", np.eye(P, dtype=np.float32))
    put("ones", 1.0)
    put("ones64", np.kron(np.eye(2), np.ones((64, 64))))
    put("rot64", rotation(64, 64))
    put("rot16", rotation(16, 64))
    put("iota", np.arange(P)[None, :])
    put("mask", np.where(np.arange(P)[None, :] > np.arange(P)[:, None], NEG, 0.0))
    pos = np.arange(S, dtype=np.float32)
    inv = (np.float32(1.0) / (np.float32(10000.0) ** (np.arange(32, dtype=np.float32) / np.float32(32)))).astype(np.float32)
    ang = (pos[None, :] * inv[:, None]).astype(np.float32)
    put("cos", np.tile(np.cos(ang), (4, 1)))
    put("sin", np.tile(np.sin(ang), (4, 1)))
    inv = (np.float32(500000.0) ** (-np.arange(0, 16, 2, dtype=np.float32) / np.float32(16))).astype(np.float32)
    ang = (pos[None, :] * inv[:, None]).astype(np.float32)
    cos, sin = np.ones((64, S), np.float32), np.zeros((64, S), np.float32)
    cos[0:16], sin[0:16] = np.tile(np.cos(ang), (2, 1)), np.tile(np.sin(ang), (2, 1))
    tables2 = np.concatenate([np.tile(cos, (2, 1)), np.tile(sin, (2, 1))], axis=1)
    t = np.arange(P)[:, None, None] + P * np.arange(TB)[None, :, None]
    n = np.arange(NCP)[None, None, :]
    ok = (n * CMP_STRIDE + CMP_BLOCK - 1 <= t) & (n < NCMP)
    put("eps", np.array([n * EPS for n in EPS_N])[None, :])
    put("cmp_add", np.where(ok, 0.0, NEG).reshape(P, -1))
    put("cmp_mul", ok.astype(np.float32).reshape(P, -1))
    return c, tables2


def chunked(w):
    k, n = w.shape
    return np.ascontiguousarray(w.reshape(k // P, P, n // P, P).transpose(2, 1, 0, 3)).reshape(n // P, P, -1)


def moving(w, per):
    k, n = w.shape
    return np.ascontiguousarray(w.reshape(k // P // per, per, P, n).transpose(0, 2, 1, 3)).reshape(k // P // per, P, -1)


def columns(v):
    return np.asarray(v).reshape(-1, P).T


def lay_out(a):
    g = {k: np.asarray(v) for k, v in a.items()}
    cols = np.zeros((P, NCOLS), np.float32)

    def put(name, v):
        cols[:, COLS[name][0]:COLS[name][1]] = v

    twice = lambda v: np.concatenate([v, v])[:, None]
    put("c", columns(g["c"][0]))
    put("ada_b", columns(g["ada_b"][0]))
    put("norm1", columns(g["norm1_g"][0]))
    put("norm2", columns(g["norm2_g"][0]))
    put("a_norm", columns(g["a_norm_2"][0]))
    put("kv_norm", columns(g["kv_norm_2"]))
    put("b_norm", columns(g["b_norm_2"][0]))
    put("final", columns(g["final_norm_2"]))
    put("q_lat", columns(g["mla_q_lat_g"][0]))
    put("kv_lat", columns(g["mla_kv_lat_g"][0]))
    put("q_nope", g["mla_q_g"][0][:NOPE, None])
    put("q_pe", twice(g["mla_q_g"][0][NOPE:]))
    put("k_nope", g["mla_k_g"][0][:NOPE, None])
    put("k_pe", twice(g["mla_k_g"][0][NOPE:]))
    put("dq", twice(g["diff_q_g"][0]))
    put("dk", twice(g["diff_k_g"][0]))
    put("subln", g["diff_subln_g"][0][:, None])
    put("conv", columns(g["a_conv_w_2"][0]))
    for name, one, two in (("lam_q", "diff_lq1", "diff_lq2"), ("lam_k", "diff_lk1", "diff_lk2")):
        cols[0:64, COLS[name][0]] = g[one][0]
        cols[0:64, COLS[name][0] + 1] = g[two][0]

    consts, tables2 = make_consts()
    w = g["w_in"][0]
    o0, o1, o2 = Q_LORA, Q_LORA + KV_LORA, Q_LORA + KV_LORA + ROPE
    o3, o4 = o2 + 512, o2 + 1024
    kpe = w[:, o1:o2]
    w_in = np.concatenate([w[:, o0:o1], kpe, kpe, w[:, :o0], w[:, o2:o4]], axis=1)
    qu = g["mla_w_q_up"][0].reshape(Q_LORA, MLA_H, NOPE + ROPE)
    q_up = np.concatenate([qu[:, :, :NOPE].reshape(Q_LORA, -1), qu[:, :, NOPE:].reshape(Q_LORA, -1)], axis=1)
    ku = g["mla_w_kv_up"][0].reshape(KV_LORA, MLA_H, NOPE + MLA_V)
    kv = g["w_kv_2"].reshape(D, 6, GROUPS, HD)
    kc = np.concatenate([kv[:, 0:2], kv[:, 0:2]], axis=3).reshape(D, -1)
    ks = np.concatenate([kv[:, 2].reshape(D, -1), kv[:, 4].reshape(D, -1)], axis=1)
    vsw = np.concatenate([kv[:, 3].reshape(D, -1), kv[:, 5].reshape(D, -1)], axis=1)
    order = [h for m in range(2) for i in range(4) for h in (8 * m + i, 8 * m + 4 + i)]
    bw = g["b_w_in_2"][0]
    bq = bw[:, :D].reshape(D, NSA_H, HD)[:, order].reshape(D, D)
    bz = bw[:, D + 48:].reshape(D, NSA_H, HD)[:, order].reshape(D, D)
    bo = g["b_w_out_2"][0].reshape(NSA_H, HD, D)[order].reshape(D, D)
    w1 = [g[n].reshape(CMP_PAIRS // 4, 4, P, CMP_HID).transpose(0, 2, 1, 3).reshape(4, P, -1)
          for n in ("cmp_w1_k_2", "cmp_w1_v_2")]
    pos = [g[n].reshape(CMP_PAIRS, P).T for n in ("cmp_pos_k_2", "cmp_pos_v_2")]
    w2k, w2v = (g[n].reshape(2, P, HD).transpose(1, 0, 2) for n in ("cmp_w2_k_2", "cmp_w2_v_2"))
    a_w_in = chunked(g["a_w_in_2"][0]).reshape(4, CC, P, -1)[[1, 2, 0, 3]].transpose(1, 0, 2, 3).reshape(4 * CC, P, -1)
    w_out = chunked(g["a_w_out_2"][0]).reshape(DC, P, 2, -1).transpose(0, 2, 1, 3).reshape(2 * DC, P, -1)
    return {
        "x": g["x"][0].T.reshape(DC, P, S).transpose(1, 0, 2).reshape(P, -1),
        "cols": cols,
        "consts": consts,
        "tables2": tables2,
        "ada_w": chunked(g["ada_w"][0]),
        "w_in": chunked(w_in),
        "w_dv": moving(w[:, o4:], 2),
        "q_up": chunked(q_up),
        "kv_up": chunked(ku[:, :, :NOPE].reshape(KV_LORA, -1)),
        "kv_up_v": moving(ku[:, :, NOPE:].reshape(KV_LORA, -1), 2)[0],
        "w_out": chunked(g["w_out"][0]),
        "peer_q": chunked(g["peer_w_q"][0]),
        "keys": g["peer_sub_keys"][0].reshape(HP, NKEYS, P).transpose(2, 0, 1).reshape(P, -1),
        "peer_u": g["peer_u"][0].reshape(NKEYS, P, DC, P).transpose(0, 3, 2, 1).reshape(NKEYS, P, -1),
        "peer_v": g["peer_v"][0].reshape(NKEYS, P, D),
        "a_w_in": a_w_in,
        "a_w_out": w_out,
        "w_kvc": chunked(kc),
        "w_kvs": chunked(ks),
        "w_vsw": moving(vsw, 2),
        "cmp_w1": np.concatenate(w1),
        "cmp_pos": np.concatenate(pos, axis=1),
        "cmp_w2": np.concatenate([w2k, w2k, w2v, w2v], axis=2).reshape(P, -1),
        "w_gates": moving(bw[:, D:D + 48], DC),
        "b_q": chunked(bq),
        "b_z": chunked(bz),
        "b_w_out": chunked(bo),
    }


def kernel(**inputs):
    import concourse.bacc as bacc
    from concourse.bass_utils import run_bass_kernel_spmd

    nc = bacc.Bacc("TRN2", target_bir_lowering=False, num_devices=1)
    arrays = {f"in_{k}": np.ascontiguousarray(v) for k, v in lay_out(inputs).items()}
    ins = {k[3:]: nc.dram_tensor(k, list(v.shape), F32, kind="ExternalInput").ap() for k, v in arrays.items()}
    out = nc.dram_tensor("out", [DC, P, S], F32, kind="ExternalOutput").ap()
    build(nc, ins, out)
    r = run_bass_kernel_spmd(nc, [arrays], core_ids=[0])
    return np.ascontiguousarray(r.results[0]["out"].reshape(D, S).T).reshape(1, S, D)
```

```python
from contextlib import ExitStack

import numpy as np

import concourse.bass as bass
from concourse import mybir

ALU = mybir.AluOpType
ACT = mybir.ActivationFunctionType
F32 = mybir.dt.float32
F32R = mybir.dt.float32r
U32 = mybir.dt.uint32
BF16 = mybir.dt.bfloat16
HI_BITS = 0xFFFFF000
AX_X = mybir.AxisListType.X

P = 128
S = 512
TB = S // P
D = 1024
DC = D // P
EPS = 1e-6
NEG = -1e30

MLA_H, NOPE, ROPE, MLA_V, Q_LORA, KV_LORA = 4, 128, 64, 128, 384, 256
QC, KVC = Q_LORA // P, KV_LORA // P
DIFF_H, DIFF_DQK = 4, 64
LAMBDA_INIT = 0.2
PEER_H, NKEYS, TOPK = 8, 128, 16
HP = PEER_H * 2
HK = PEER_H * TOPK
CONV_D = 2048
CC = CONV_D // P
NSA_H, GROUPS, HD = 16, 4, 64
CMP_BLOCK, CMP_STRIDE, CMP_HID = 32, 16, 256
NCMP = S // CMP_STRIDE - 1
NCP = NCMP + 1
CMP_PAIRS = CMP_BLOCK // 2
SLC_BLOCK, N_SELECT, WINDOW = 64, 16, 512
assert S // SLC_BLOCK <= N_SELECT and WINDOW >= S

ARENA = 23040
SLOT = 1024
SLOTS = 4
AHEAD = 2
GT = 32
EG = 4
STASHED = [i for i in range(96) if i % 2]
STASH_EVERY = 5

COLS = {}
_at = 0
for _name, _n in (("ada_b", 48), ("norm1", 8), ("norm2", 8), ("a_norm", 8), ("kv_norm", 8),
                  ("b_norm", 8), ("final", 8), ("q_lat", 3), ("kv_lat", 2), ("q_nope", 1), ("q_pe", 1),
                  ("k_nope", 1), ("k_pe", 1), ("dq", 1), ("dk", 1), ("subln", 1), ("conv", 48),
                  ("lam_q", 2), ("lam_k", 2)):
    COLS[_name] = (_at, _at + _n)
    _at += _n
NCOLS = _at

EPS_N = (D, Q_LORA, KV_LORA, P, 64)

CONSTS = {}
_at = 0
for _name, _n in (("ident", P), ("ones", P), ("ones64", P), ("rot64", P), ("rot16", P), ("iota", P),
                  ("mask16", P), ("cos", S), ("sin", S),
                  ("cmp_add", TB * NCP), ("cmp_mul", TB * NCP), ("eps", len(EPS_N))):
    CONSTS[_name] = (_at, _at + _n)
    _at += _n
NCONSTS = _at


class Line:

    def __init__(self, sem, chained):
        self.sem, self.chained, self.count, self.steps, self.waited = sem, chained, 0, [], {}

    def wait(self, *marks):
        for sem, value in marks:
            if self.waited.get(sem.name, 0) < value:
                self.waited[sem.name] = value
                self.steps.append(lambda e, s=sem, v=value: e.wait_ge(s, v))

    def do(self, emit, *marks, alone=False):
        self.wait(*marks)
        if self.chained and self.count and not alone:
            self.wait((self.sem, self.count))
        self.count += 1
        self.steps.append(lambda e: emit(e).then_inc(self.sem, 1))
        return self.sem, self.count

    @property
    def last(self):
        return self.sem, self.count

    def run(self, engine):
        for step in self.steps:
            step(engine)


class Ring:

    def __init__(self, items):
        self.items, self.idle = items, [(k, ()) for k in range(len(items))]

    def take(self):
        assert self.idle, "no buffer is free"
        k, marks = self.idle.pop(0)
        return k, self.items[k], marks

    def free(self, k, *marks):
        self.idle.append((k, marks))


def skewed(tasks):
    active = []
    for task in tasks:
        active.insert(0, task)
        active = [x for x in active if next(x, "ended") != "ended"]
    while active:
        active = [x for x in active if next(x, "ended") != "ended"]


def build(nc, ins, out):
    ctx = ExitStack()
    with ctx:
        def sem(name):
            return ctx.enter_context(nc.semaphore(name))

        def sb(name, shape, dt=F32):
            return ctx.enter_context(nc.sbuf_tensor(name, shape, dt))

        gates_dram = nc.dram_tensor("gates_scratch", [S // GT, P, NKEYS * GT], F32, kind="Internal").ap()
        gelus_dram = nc.dram_tensor("gelus_scratch", [len(STASHED), P, S], F32, kind="Internal").ap()

        consts = sb("consts", [P, NCONSTS])
        cols = sb("cols", [P, NCOLS])
        res = sb("res", [P, DC, S])
        act_r = sb("act_r", [P, DC, 2, S], F32R)
        weights_r = sb("weights_r", [P, AHEAD + 1, 2, SLOT], F32R)
        mask_mem = sb("mask_mem", [P, 2, S])
        whole_mem = sb("whole_mem", [P, 2, S])
        ring_mem = sb("ring_mem", [P, SLOTS, SLOT])
        mod = sb("mod", [P, 48])
        gains = sb("gains", [P, 64])
        rstd_mem = sb("rstd_mem", [P, 3, S])
        newton_mem = sb("newton_mem", [P, 1, S])
        sq_mem = sb("sq_mem", [P, 2, S])
        small = sb("small", [P, 8, 4])
        lam = sb("lam", [P, 8])
        arena = sb("arena", [P, ARENA])
        arena_r = nc.alloc_sbuf_tensor_at("arena_r", [P, ARENA], F32R, offset=nc.lookup_mloc(arena).addr)
        act_tail = nc.alloc_sbuf_tensor_at("act_tail", [P, D], F32,
                                           offset=nc.lookup_mloc(act_r).addr + (DC - 1) * 2 * S * 4)
        banks_mem = ctx.enter_context(nc.psum_tensor("banks", [P, 8, 512], F32))

        def const(name):
            a, b = CONSTS[name]
            return consts[:, a:b]

        def col(name, i=0, n=1):
            a = COLS[name][0] + i
            return cols[:, a:a + n]

        pe = Line(sem("pe_done"), False)
        dve = Line(sem("dve_done"), True)
        act_e = Line(sem("act_done"), False)
        pool = Line(sem("pool_done"), True)
        sync = Line(sem("sync_unused"), False)
        slot_sems = [sem(f"slot{k}_loaded") for k in range(SLOTS)]
        slot_loads = [0] * SLOTS
        slots = Ring([ring_mem[:, k, :] for k in range(SLOTS)])
        banks = Ring([banks_mem[:, k, :] for k in range(8)])
        rstds = Ring([rstd_mem[:, k, :] for k in range(3)])
        newtons = Ring([newton_mem[:, 0, :]])
        splits = Ring([weights_r[:, k, :, :] for k in range(AHEAD + 1)])
        masks = Ring([mask_mem[:, k, :] for k in range(2)])
        wholes = Ring([whole_mem[:, k, :] for k in range(2)])
        act_hl = [(act_r[:, c, 0, :], act_r[:, c, 1, :]) for c in range(DC)]
        squares = Ring([sq_mem[:, k, :] for k in range(2)])

        def load(dst, src, s, n, *marks):
            sync.wait(*marks)
            sync.steps.append(lambda e: e.dma_start(dst, src).then_inc(s, 16))
            return s, 16 * n

        def fetch(src):
            k, tile, freed = slots.take()
            n = src.shape[1]
            slot_loads[k] += 1
            return k, tile[:, 0:n], load(tile[:, 0:n], src, slot_sems[k], slot_loads[k], *freed)

        def fence(*lines):
            for line in lines or (dve, act_e, pool, sync):
                line.wait(*[x.last for x in (pe, dve, act_e, pool) if x is not line and x.count])

        def eps_col(n):
            return const("eps")[:, EPS_N.index(n):EPS_N.index(n) + 1]

        def mm(out_, pairs, *marks, start=True, stop=True):
            def emit(e):
                for n, (a, b) in enumerate(pairs):
                    last = e.matmul(out_, a, b, start=start and n == 0, stop=stop and n == len(pairs) - 1)
                return last
            return pe.do(emit, *marks)

        def split(src, hi, lo, ready, freed=()):
            for at in range(0, src.shape[1], S):
                piece = slice(at, min(at + S, src.shape[1]))
                n = piece.stop - at
                tk, mask, mask_freed = masks.take()
                x, top, hi_, lo_ = src[:, piece], mask[:, 0:n], hi[:, piece], lo[:, piece]
                masked = dve.do(lambda e, x=x, top=top: e.tensor_single_scalar(
                    top.bitcast(U32), x.bitcast(U32), HI_BITS, ALU.bitwise_and), *ready, *mask_freed, alone=True)
                hi_done = act_e.do(lambda e, hi_=hi_, top=top: e.activation(hi_, top, ACT.Copy), masked, *freed)
                lo_done = dve.do(lambda e, lo_=lo_, x=x, top=top: e.tensor_tensor(lo_, x, top, ALU.subtract),
                                 masked, *freed, alone=True)
                masks.free(tk, hi_done, lo_done)
            return hi_done, lo_done

        def fetch_split(src, ring):
            k, raw, loaded = fetch(src)
            n = src.shape[1]
            rk, r, freed = ring.take()
            hi, lo = r[:, 0, 0:n], r[:, 1, 0:n]
            made = split(raw, hi, lo, (loaded,), freed)
            slots.free(k, made[1])
            return rk, (hi, lo), made

        plan = [ins[name][i] for name in ("w_in", "w_dv", "w_out", "peer_q") for i in range(ins[name].shape[0])]
        last_q = plan[-2:]
        plan[-2:] = [ins["peer_u"][STASHED[0]], last_q[0], ins["peer_u"][STASHED[1]], last_q[1]]
        plan += [ins["peer_u"][i] for i in STASHED[2:]]
        plan += [ins["peer_u"][i] for i in range(NKEYS) if i not in STASHED]
        plan += [ins[name][i] for name in ("a_w_in", "a_w_out", "w_kvc", "w_kvs", "w_vsw", "w_gates", "b_q", "b_z",
                                           "b_w_out") for i in range(ins[name].shape[0])]
        prepared = []

        def prepare(n):
            while len(prepared) < n and plan and splits.idle:
                prepared.append(fetch_split(plan.pop(0), splits))

        def next_split():
            prepare(AHEAD + 1)
            return prepared.pop(0)

        def three(w, x):
            return [(w[0], x[0]), (w[0], x[1]), (w[1], x[0])]

        def linear_whole(src, kc, acts, ready):
            k, w, loaded = fetch(src)
            b, bank, freed = banks.take()
            w = w.rearrange("p (c n) -> p c n", c=kc)
            done = mm(bank, [(w[:, c, :], acts[c]) for c in range(kc)], loaded, *freed, *ready)
            slots.free(k, done)
            return b, bank, done

        begun = []

        def begin(n, acts, ready):
            got = [banks.take() for _ in range(n)]
            weights = [next_split() for _ in range(n)]
            done = [None] * n
            for c in range(DC):
                for j, ((_, bank, freed), (_, w, made)) in enumerate(zip(got, weights)):
                    w = [x.rearrange("p (c n) -> p c n", c=DC)[:, c, :] for x in w]
                    done[j] = mm(bank, three(w, acts[c]), *made, *freed, *ready[c], start=c == 0, stop=c == DC - 1)
            for (k, _, _), d in zip(weights, done):
                splits.free(k, d)
            begun.extend((b, bank, d) for (b, bank, _), d in zip(got, done))

        def linear(n_chunks, acts, ready):
            if begun:
                return begun.pop(0)
            b, bank, freed = banks.take()
            for n in range(n_chunks):
                k, w, made = next_split()
                w = [x.rearrange("p (c n) -> p c n", c=DC) for x in w]
                for c in range(DC):
                    first, last = n + c == 0, (n, c) == (n_chunks - 1, DC - 1)
                    done = mm(bank, three([x[:, c, :] for x in w], acts[n * DC + c]), *made, *freed,
                              *ready[n * DC + c], start=first, stop=last)
                splits.free(k, done)
            return b, bank, done

        def linear_tokens(n_chunks, per, acts, ready):
            got = [banks.take() for _ in range(TB)]
            done = None
            for s_ in range(n_chunks):
                k, w, made = next_split()
                w = [x.rearrange("p (c n) -> p c n", c=per) for x in w]
                for tb in range(TB):
                    rows = slice(tb * P, (tb + 1) * P)
                    pairs = [p for c in range(per) for p in
                             three([x[:, rows] for x in acts[s_ * per + c]], [x[:, c, :] for x in w])]
                    done = mm(got[tb][1], pairs, *made, *(m for c in range(per) for m in ready[s_ * per + c]),
                              *(got[tb][2] if s_ == 0 else ()), start=s_ == 0, stop=s_ == n_chunks - 1)
                splits.free(k, done)
            return [(g[0], g[1]) for g in got], done

        def squares_of(chunks, ones, ready):
            b, bank, freed = banks.take()
            for i, x in enumerate(chunks):
                k, sq, sq_freed = squares.take()
                squared = act_e.do(lambda e, sq=sq, x=x: e.activation(sq, x, ACT.Square), *ready, *sq_freed)
                done = mm(bank, [(ones, sq)], squared, *(freed if i == 0 else ()), start=i == 0,
                          stop=i == len(chunks) - 1)
                squares.free(k, done)
            return b, bank, done

        class RunningSquares:

            def __init__(self):
                self.made, self.count, self.done = [], 0, None

            def square(self, c, ready):
                k, sq, sq_freed = squares.take()
                self.made.append((k, sq, act_e.do(lambda e: e.activation(sq, res[:, c, :], ACT.Square),
                                                  ready, *sq_freed)))

            def add(self):
                freed = ()
                if not self.count:
                    self.b, self.bank, freed = banks.take()
                while self.made:
                    k, sq, squared = self.made.pop(0)
                    self.done = mm(self.bank, [(const("ones"), sq)], squared, *freed, start=self.count == 0,
                                   stop=self.count == DC - 1)
                    squares.free(k, self.done)
                    self.count += 1

            def result(self):
                self.add()
                return self.b, self.bank, self.done

        def rstd_of(b, bank, done, n):
            return refined(b, bank, n, *rough_rstd(bank, done, n))

        def rough_rstd(bank, done, n):
            k, r, r_freed = rstds.take()
            root = act_e.do(lambda e: e.activation(r, bank, ACT.Abs_reciprocal_sqrt, bias=eps_col(n)), done, *r_freed)
            return k, r, root

        def refined(b, bank, n, k, r, root):
            nk, newton, n_freed = newtons.take()
            m2 = dve.do(lambda e: e.tensor_tensor(newton, r, r, ALU.mult), root, *n_freed, alone=True)
            m = dve.do(lambda e: e.scalar_tensor_tensor(newton, bank, n * EPS, newton, ALU.add, ALU.mult), m2)
            banks.free(b, m)
            dve.do(lambda e: e.tensor_scalar(newton, newton, -0.5, 1.5, ALU.mult, ALU.add))
            made = dve.do(lambda e: e.tensor_tensor(r, r, newton, ALU.mult))
            newtons.free(nk, made)
            return k, r, made

        def scaled(dst, x, gain, r, ready):
            return dve.do(lambda e: e.scalar_tensor_tensor(dst, x, gain, r, ALU.mult, ALU.mult), *ready, alone=True)

        def apply_norm(gain, shift, k, r, made, keep=False, act_freed=()):
            marks = [None] * DC

            def chunk(c):
                wk, whole, w_freed = wholes.take()
                m = scaled_last[0] = scaled(whole, res[:, c, :], gain[:, c:c + 1], r, (made, *w_freed))
                if shift is not None:
                    m = act_e.do(lambda e: e.activation(whole, whole, ACT.Identity, bias=shift[:, c:c + 1]), m)
                yield
                marks[c] = split(whole, *act_hl[c], (m,), act_freed)
                wholes.free(wk, marks[c][1])

            scaled_last = [None]
            skewed([chunk(c) for c in range(DC)])
            if not keep:
                rstds.free(k, scaled_last[0])
            return marks

        def norm_stages(dst, src, ones, n, gain, done, freed, out_marks, apart=False):
            sb_, ssq, s_done = squares_of([src], ones, (done,))
            yield
            rough = rough_rstd(ssq, s_done, n)
            if apart:
                yield
            k, r, made = refined(sb_, ssq, n, *rough)
            m = scaled(dst, src, gain, r, (made, *freed))
            rstds.free(k, m)
            out_marks.append(m)

        def rope_stages(rings, parts, x, rot, cos, sin, ready, out_marks):
            cos_ring, sin_ring = rings
            b, bank, freed = banks.take()
            turned = mm(bank, [(rot, x)], ready, *freed)
            ck, tc, tc_freed = cos_ring.take()
            made = pool.do(lambda e: e.tensor_tensor(tc, x, cos, ALU.mult), ready, *tc_freed)
            yield
            sk, ts, ts_freed = sin_ring.take()
            m = dve.do(lambda e: e.tensor_tensor(ts, bank, sin, ALU.mult), turned, *ts_freed, alone=True)
            banks.free(b, m)
            for dst, rows in parts:
                m2 = dve.do(lambda e, dst=dst, rows=rows: e.tensor_tensor(dst, tc[rows, :], ts[rows, :], ALU.add),
                            made, m, alone=True)
            cos_ring.free(ck, m2)
            sin_ring.free(sk, m2)
            out_marks.append(m2)

        s_x, s_cols, s_consts = sem("x_loaded"), sem("cols_loaded"), sem("consts_loaded")
        cols_in = load(cols[:, :], ins["cols"], s_cols, 1)

        spans = {}
        at = 0
        for name, n, factor in (("norm1", 8, D ** 0.5), ("norm2", 8, D ** 0.5), ("a_norm", 8, D ** 0.5),
                                ("kv_norm", 8, D ** 0.5), ("b_norm", 8, D ** 0.5), ("final", 8, D ** 0.5),
                                ("q_lat", 3, Q_LORA ** 0.5), ("kv_lat", 2, KV_LORA ** 0.5),
                                ("q_nope", 1, NOPE ** 0.5 * (NOPE + ROPE) ** -0.5),
                                ("q_pe", 1, ROPE ** 0.5 * (NOPE + ROPE) ** -0.5),
                                ("k_nope", 1, NOPE ** 0.5), ("k_pe", 1, ROPE ** 0.5),
                                ("dq", 1, 1.0), ("dk", 1, DIFF_DQK ** 0.5),
                                ("subln", 1, P ** 0.5 * (1.0 - LAMBDA_INIT))):
            g = gains[:, at:at + n]
            spans[name] = g
            dve.do(lambda e, g=g, name=name, n=n, f=factor: e.tensor_scalar(g, col(name, 0, n), f, None, ALU.mult),
                   cols_in)
            at += n

        s_c = sem("c_loaded")

        def silu_row(dst, n, *marks):
            return act_e.do(lambda e: e.activation(dst, dst, ACT.Silu), load(dst, ins["c_rows"], s_c, n, *marks))

        def modulation(first, n, silu, silu_ready):
            for j in range(first, first + n):
                k, w, loaded = fetch(ins["ada_w"][j])
                slots.free(k, dve.do(lambda e, j=j, w=w: e.scalar_tensor_tensor(
                    w, w, 1.0, silu, ALU.mult, ALU.mult, accum_out=mod[:, j:j + 1]), loaded, silu_ready, alone=True))
            return dve.do(lambda e: e.tensor_tensor(mod[:, first:first + n], mod[:, first:first + n],
                                                    col("ada_b", first, n), ALU.add), cols_in)

        def modulated_gain(dst, scale_at):
            return dve.do(lambda e: e.scalar_tensor_tensor(dst, mod[:, scale_at:scale_at + 8], 1.0, dst,
                                                           ALU.add, ALU.mult))

        lat_at = 32 * S
        early_silu = arena[:, lat_at:lat_at + D]
        silu_ready = silu_row(early_silu, 1)
        modulation(0, 4, early_silu, silu_ready)
        x_in = load(res[:, :, :].rearrange("p c t -> p (c t)"), ins["x"], s_x, 1)
        consts_in = load(consts[:, :], ins["consts"], s_consts, 1)
        x_squares = squares_of([res[:, c, :] for c in range(DC)], const("ones"), (x_in, consts_in))
        modulation(4, 6, early_silu, silu_ready)
        prepare(AHEAD + 1)
        x_rstd = rstd_of(*x_squares, D)
        modulation(10, 6, early_silu, silu_ready)
        gain_ready = modulated_gain(spans["norm1"], 8)
        act_e.wait(gain_ready)
        dve.wait(gain_ready)
        h_ready = apply_norm(spans["norm1"], mod[:, 0:8], *x_rstd)

        pos = [0]

        def view(n, *dims):
            a = arena[:, pos[0]:pos[0] + n]
            pos[0] += n
            assert pos[0] <= ARENA, pos[0]
            if len(dims) == 2:
                return a.rearrange("p (a b) -> p a b", a=dims[0])
            if len(dims) >= 3:
                names = "abcd"[:len(dims)]
                return a.rearrange(f"p ({' '.join(names)}) -> p {' '.join(names)}", **dict(zip(names, dims)))
            return a

        q_nope = view(4 * S, 4, S)
        q_pe = view(2 * S, 2, S)
        k_nope = view(4 * S, 4, S)
        k_pe = view(2 * S, 2, S)
        v_mla = view(TB * S, TB, S)
        q_diff = view(4 * S, 4, S)
        k_diff = view(8 * S, 8, S)
        v_diff = view(TB * S, TB, S)
        head_end = pos[0]
        assert head_end == lat_at
        lat = view(3 * S, 3, S)
        normed_ring = Ring([view(S) for _ in range(4)])
        rope_rings = Ring([view(S) for _ in range(3)]), Ring([view(S) for _ in range(2)])
        halves = (slice(0, 64), slice(64, 128))

        for h in range(2):
            pool.do(lambda e, h=h: e.memset(k_pe[halves[1 - h], h, :], 0.0))
        for h in range(8):
            pool.do(lambda e, h=h: e.memset(k_diff[halves[1 - h % 2], h, :], 0.0))

        lats = [lat[:, c, :] for c in range(QC)]
        rope64 = (const("rot64"), const("cos"), const("sin"))

        def latent(n, gain):
            before = (pe.last, dve.last)
            if n == KVC:
                begin(3, act_hl, h_ready)
            for c in range(n):
                b, bank, done = linear(1, act_hl, h_ready)
                m = act_e.do(lambda e, c=c, bank=bank: e.activation(lat[:, c, :], bank, ACT.Copy), done, *before)
                banks.free(b, m)
            k, r, made = rstd_of(*squares_of([lat[:, c, :] for c in range(n)], const("ones"), (m,)), n * P)
            for c in range(n):
                m = scaled(lat[:, c, :], lat[:, c, :], gain[:, c:c + 1], r, (made,))
            rstds.free(k, m)
            return m

        def normed_head(make, dst, ones, n, gain):
            b, bank, done = make()
            yield
            got_ = []
            yield from norm_stages(dst, bank, ones, n, gain, done, (), got_)
            banks.free(b, got_[0])

        def rotated_head(make, gain, parts):
            b, bank, done = make()
            yield
            got_ = []
            nk, x, x_freed = normed_ring.take()
            yield from norm_stages(x, bank, const("ones64"), DIFF_DQK, gain, done, x_freed, got_)
            banks.free(b, got_[0])
            yield
            yield from rope_stages(rope_rings, parts, x, *rope64, got_[0], got_)
            normed_ring.free(nk, got_[1])

        def from_act():
            return lambda: linear(1, act_hl, h_ready)

        def from_lat(src, n, ready):
            return lambda: linear_whole(src, n, lats, (ready,))

        lat_ready = latent(KVC, spans["kv_lat"])
        skewed([normed_head(from_lat(ins["kv_up"][h], KVC, lat_ready), k_nope[:, h, :], const("ones"), NOPE,
                            spans["k_nope"]) for h in range(MLA_H)]
               + [rotated_head(from_act(), spans["k_pe"], [(k_pe[halves[j], j, :], halves[j]) for j in range(2)])])
        k, w, loaded = fetch(ins["kv_up_v"])
        w = w.rearrange("p (c n) -> p c n", c=KVC)
        for tb in range(TB):
            b, bank, freed = banks.take()
            done = mm(bank, [(lats[c][:, tb * P:(tb + 1) * P], w[:, c, :]) for c in range(KVC)], loaded, *freed)
            banks.free(b, act_e.do(lambda e, tb=tb, bank=bank: e.activation(v_mla[:, tb, :], bank, ACT.Copy), done))
        slots.free(k, done)
        lat_ready = latent(QC, spans["q_lat"])
        skewed([normed_head(from_lat(ins["q_up"][h], QC, lat_ready), q_nope[:, h, :], const("ones"), NOPE,
                            spans["q_nope"]) for h in range(MLA_H)]
               + [rotated_head(from_lat(ins["q_up"][MLA_H + j], QC, lat_ready), spans["q_pe"],
                               [(q_pe[:, j, :], slice(0, P))]) for j in range(2)]
               + [rotated_head(from_act(), spans["dq"], [(q_diff[:, h, :], slice(0, P))]) for h in range(DIFF_H)]
               + [rotated_head(from_act(), spans["dk"],
                               [(k_diff[halves[j], 2 * h + j, :], halves[j]) for j in range(2)])
                  for h in range(DIFF_H)])
        got, done = linear_tokens(4, 2, act_hl, h_ready)
        for tb, (b, bank) in enumerate(got):
            banks.free(b, act_e.do(lambda e, tb=tb, bank=bank: e.activation(v_diff[:, tb, :], bank, ACT.Copy), done))

        dve.do(lambda e: e.tensor_tensor(lam[:, 0:2], col("lam_q", 0, 2), col("lam_k", 0, 2), ALU.mult))
        b, bank, freed = banks.take()
        done = mm(bank[:, 0:2], [(const("ones"), lam[:, 0:2])], dve.last, *freed)
        m = act_e.do(lambda e, bank=bank: e.activation(lam[:, 2:4], bank[:, 0:2], ACT.Exp), done)
        banks.free(b, m)
        dve.do(lambda e: e.tensor_tensor(lam[:, 4:5], lam[:, 3:4], lam[:, 2:3], ALU.subtract), m)
        dve.do(lambda e: e.tensor_scalar(lam[:, 5:6], lam[:, 4:5], -LAMBDA_INIT, None, ALU.add))
        neg_lam = lam[:, 5:6]

        fence(act_e, dve, pe)
        pos[0] = head_end
        probs = Ring([view(S) for _ in range(5)])
        transposed = Ring([view(TB * S, TB, S) for _ in range(2)])
        both16 = const("mask16").bitcast(BF16)
        ident16, mask16 = both16[:, 0:P], both16[:, P:2 * P]
        stats = Ring([small[:, k, :] for k in range(8)])

        def exp_rows(score_pairs, qb):
            w = (qb + 1) * P
            b, bank, freed = banks.take()

            def emit(e):
                for n, (q, k) in enumerate(score_pairs):
                    e.matmul(bank[:, 0:w], q[:, qb * P:w], k[:, 0:w], start=n == 0, stop=False)
                return e.matmul(bank[:, w - P:w], ident16, mask16, start=False, stop=True)
            scored = pe.do(emit, *freed)
            sk, st, st_freed = stats.take()
            maxed = dve.do(lambda e: e.tensor_reduce(st[:, 0:1], bank[:, 0:w], AX_X, ALU.max, negate=True),
                           scored, *st_freed, alone=True)
            pk, p, p_freed = probs.take()
            exped = act_e.do(lambda e: e.activation(p[:, 0:w], bank[:, 0:w], ACT.Exp, bias=st[:, 0:1],
                                                    scale=1.0, accum_out=st[:, 1:2]), maxed, *p_freed)
            banks.free(b, exped)
            return pk, p[:, 0:w], sk, st, exped

        def transpose_rows(p, qb, dst, ready, freed, on):
            b, bank, b_freed = banks.take()

            def emit(e):
                for kb in range(qb + 1):
                    last = e.transpose(bank[:, kb * P:(kb + 1) * P], p[:, kb * P:(kb + 1) * P], const("ident"))
                return last
            turned = pe.do(emit, ready, *b_freed)
            src = bank[:, 0:(qb + 1) * P].rearrange("p (k q) -> p k q", q=P)
            to = dst[:, 0:qb + 1, qb * P:(qb + 1) * P]
            if on is dve:
                m = dve.do(lambda e: e.tensor_copy(to, src), turned, *freed, alone=True)
            else:
                m = act_e.do(lambda e: e.activation(to, src, ACT.Copy), turned, *freed)
            banks.free(b, m)
            return turned, m

        def values_mm(out_, v, turned, ready, first, last, *freed):
            def emit(e):
                for kb in range(TB):
                    x = e.matmul(out_[:, kb * P:S], v(kb), turned[:, kb, kb * P:S], start=first and kb == 0,
                                 stop=last and kb == TB - 1)
                return x
            return pe.do(emit, *ready, *freed)

        state = {}
        mixed_marks = [None] * DC

        def attend(h, qb):
            hd = h % 4
            if h < MLA_H:
                pk, p, sk, st, exped = exp_rows(
                    [(q_nope[:, h, :], k_nope[:, h, :]), (q_pe[:, h // 2, :], k_pe[:, h % 2, :])], qb)
                yield
                m = dve.do(lambda e: e.reciprocal(st[:, 2:3], st[:, 1:2]), exped, alone=True)
                m = dve.do(lambda e: e.tensor_scalar(p, p, st[:, 2:3], None, ALU.mult), m)
                stats.free(sk, m)
            else:
                pk, p, sk, st, exped = exp_rows([(q_diff[:, hd, :], k_diff[:, 2 * hd, :])], qb)
                pk2, p2, sk2, st2, exped2 = exp_rows([(q_diff[:, hd, :], k_diff[:, 2 * hd + 1, :])], qb)
                yield
                a = dve.do(lambda e: e.reciprocal(st[:, 2:3], st[:, 1:2]), exped, alone=True)
                b_ = dve.do(lambda e: e.reciprocal(st2[:, 2:3], st2[:, 1:2]), exped2, alone=True)
                m = dve.do(lambda e: e.tensor_scalar(p, p, st[:, 2:3], None, ALU.mult), a, alone=True)
                m2 = dve.do(lambda e: e.tensor_tensor(st2[:, 3:4], st2[:, 2:3], neg_lam, ALU.mult), b_, alone=True)
                stats.free(sk, m)
                m = dve.do(lambda e: e.scalar_tensor_tensor(p, p2, st2[:, 3:4], p, ALU.mult, ALU.add), m, m2)
                stats.free(sk2, m)
                probs.free(pk2, m)
            yield
            if qb == 0:
                state["t"] = transposed.take()
            tk, t, t_freed = state["t"]
            turned, copied = transpose_rows(p, qb, t, m, t_freed, act_e if qb % 2 else dve)
            state[qb] = copied
            probs.free(pk, turned)
            if qb < TB - 1:
                return
            b, bank, freed = banks.take()
            v = v_mla if h < MLA_H else v_diff
            done = values_mm(bank, lambda kb: v[:, kb, hd * P:(hd + 1) * P], t, [state[q] for q in range(TB)],
                             True, True, *freed)
            transposed.free(tk, done)
            wk, whole, w_freed = wholes.take()
            if h < MLA_H:
                m = act_e.do(lambda e: e.activation(whole, bank, ACT.Copy), done, *w_freed)
            else:
                yield
                got_ = []
                yield from norm_stages(whole, bank, const("ones"), P, spans["subln"], done, w_freed, got_,
                                       apart=True)
                m = got_[0]
            banks.free(b, m)
            both = split(whole, *act_hl[h], (m,), (state["mod"],) if h == DC - 1 else ())
            wholes.free(wk, both[1])
            mixed_marks[h] = both

        silu = act_tail[:, :]
        silu_ready = silu_row(silu, 2, pe.last)

        def modulate(first, n):
            state["mod"] = modulation(first, n, silu, silu_ready)
            yield

        tasks, at = [], 16
        for h in range(MLA_H + DIFF_H):
            for qb in range(TB):
                tasks += [modulate(at, 1), attend(h, qb)]
                at += 1
        assert at == 48
        skewed(tasks)
        mod_ready = dve.last

        def project_back(per, acts_, ready, gate):
            sums = RunningSquares()
            if per == 1:
                begin(3, acts_, ready)
            for n in range(DC):
                b, bank, done = linear(per, acts_, ready)
                g = gate[:, n:n + 1] if gate is not None else 1.0
                m = dve.do(lambda e, n=n, bank=bank, g=g: e.scalar_tensor_tensor(
                    res[:, n, :], bank, g, res[:, n, :], ALU.mult, ALU.add), done, alone=True)
                banks.free(b, m)
                if n:
                    sums.add()
                sums.square(n, m)
            return m, sums.result()

        x1, x1_squares = project_back(1, act_hl, mixed_marks, mod[:, 16:24])

        modulated_gain(spans["norm2"], 32)
        fence()
        dve.wait(dve.last)
        h2_ready = apply_norm(spans["norm2"], mod[:, 24:32], *rstd_of(*x1_squares, D))

        s_tables = sem("tables_loaded")
        a = CONSTS["cos"][0]
        tables_in = load(consts[:, a:a + 2 * S], ins["tables2"], s_tables, 1)
        pos[0] = 0
        g_t, i_t, j_t = (view(S) for _ in range(3))
        topv = view(TB * HP * TOPK, TB * HP, TOPK)
        topi_u = view(TB * HP * TOPK, TB * HP, TOPK).bitcast(U32)
        topi = view(HP * TOPK, HP, TOPK)
        cand = view(PEER_H * 256, PEER_H, 256)
        fv = view(HK, PEER_H, TOPK)
        fpos = view(HK, PEER_H, TOPK).bitcast(U32)
        part_u = view(HK, PEER_H, TOPK).bitcast(U32)
        part = view(HK, PEER_H, TOPK)
        picked = view(HK * TOPK)
        gij = view(3 * HK, 3, HK)
        gsum = view(PEER_H)
        hot_j = Ring([view(4 * P, 4, P) for _ in range(3)])
        hot_raw = Ring([view(4 * P, 4, P) for _ in range(2)])
        hot_i = Ring([view(4 * P, 4, P) for _ in range(3)])
        stash_ring = Ring([view(S) for _ in range(3)])
        stage_at = pos[0]
        stages = Ring([view(GT * P, P, GT) for _ in range(2)])
        pos[0] = stage_at
        keys = view(HP * P, HP, P)
        query_ring = Ring([view(S) for _ in range(2)])
        score_ring = Ring([view(S) for _ in range(3)])

        def top16(rows, ready):
            steps = (lambda e, v, i, x: e.max(v[:, 0:8], x),
                     lambda e, v, i, x: e.max_index(i[:, 0:8], v[:, 0:8], x),
                     lambda e, v, i, x: e.match_replace(x, v[:, 0:8], x, -3e38),
                     lambda e, v, i, x: e.max(v[:, 8:16], x),
                     lambda e, v, i, x: e.max_index(i[:, 8:16], v[:, 8:16], x))
            marks = [ready] * len(rows)
            for step in steps:
                marks = [dve.do(lambda e, row=row, step=step: step(e, *row), mark, alone=True)
                         for row, mark in zip(rows, marks)]
            return marks[-1]

        s_keys = sem("keys_loaded")
        keys_in = load(keys.rearrange("p a b -> p (a b)"), ins["keys"], s_keys, 1)

        def best_keys(hp):
            b, q_bank, done = linear(1, act_hl, h2_ready)
            qk, q, q_freed = query_ring.take()
            copied = act_e.do(lambda e: e.activation(q, q_bank, ACT.Copy), done, *q_freed)
            banks.free(b, copied)
            yield
            b, bank, freed = banks.take()

            def emit(e):
                for tb in range(TB):
                    rows = slice(tb * P, (tb + 1) * P)
                    last = e.matmul(bank[:, rows], q[:, rows], keys[:, hp, :], start=True, stop=True)
                return last
            done = pe.do(emit, copied, keys_in, *freed)
            query_ring.free(qk, done)
            sk, scores, s_freed = score_ring.take()
            copied = act_e.do(lambda e: e.activation(scores, bank, ACT.Copy), done, *s_freed)
            banks.free(b, copied)
            yield
            m = top16([(topv[:, tb * HP + hp, :], topi_u[:, tb * HP + hp, :], scores[:, tb * P:(tb + 1) * P])
                       for tb in range(TB)], copied)
            score_ring.free(sk, m)

        stash_sems = [sem(f"stash{k}_stored") for k in range(3)]
        stash_stores = [0] * 3
        stash_todo, stash_at, unfinished = list(STASHED), {}, []

        def store(dst, src, s, n):
            act_e.wait(act_e.last)
            act_e.steps.append(lambda e: e.dma_start(dst, src).then_inc(s, 16))
            return s, 16 * n

        def finish_stash():
            if unfinished:
                i, b, bank, done = unfinished.pop()
                k, a, freed = stash_ring.take()
                m = act_e.do(lambda e: e.activation(a, bank, ACT.Gelu), done, *freed)
                banks.free(b, m)
                stash_stores[k] += 1
                stash_at[i] = store(gelus_dram[STASHED.index(i)], a, stash_sems[k], stash_stores[k])
                stash_ring.free(k, stash_at[i])

        def stash_next():
            if stash_todo:
                i = stash_todo.pop(0)
                new = (i, *linear(1, act_hl, h2_ready))
                finish_stash()
                unfinished.append(new)

        def stash_task():
            stash_next()
            yield

        begin(3, act_hl, h2_ready)
        skewed([best_keys(hp) for hp in range(HP - 2)] + [stash_task(), best_keys(HP - 2), stash_task(),
                                                          best_keys(HP - 1), stash_task()])

        iota16 = const("iota")[:, 0:TOPK]

        def pick(dst, half):
            p3 = picked.rearrange("p (a b) -> p a b", b=TOPK)
            p4 = picked.rearrange("p (h k b) -> p h k b", h=PEER_H, k=TOPK)
            flat = part.rearrange("p h k -> p (h k)").unsqueeze(2).broadcast_to([P, HK, TOPK])
            dve.do(lambda e: e.tensor_tensor(p3, flat, iota16.unsqueeze(1).broadcast_to([P, HK, TOPK]), ALU.is_equal))
            lists = topi.rearrange("p (h two) k -> p h two k", two=2)[:, :, half, :]
            dve.do(lambda e: e.tensor_tensor(p4, p4, lists.unsqueeze(2).broadcast_to([P, PEER_H, TOPK, TOPK]),
                                             ALU.mult))
            return dve.do(lambda e: e.tensor_reduce(dst, p3, AX_X, ALU.add))

        turned_before = []

        def best_sums(tb):
            of_block = slice(tb * HP, (tb + 1) * HP)
            dve.do(lambda e: e.tensor_copy(topi, topi_u[:, of_block, :]))
            v4 = topv[:, of_block, :].rearrange("p (h two) k -> p h two k", two=2)
            summed = dve.do(lambda e: e.tensor_tensor(
                cand.rearrange("p h (a b) -> p h a b", a=TOPK),
                v4[:, :, 0, :].unsqueeze(3).broadcast_to([P, PEER_H, TOPK, TOPK]),
                v4[:, :, 1, :].unsqueeze(2).broadcast_to([P, PEER_H, TOPK, TOPK]), ALU.add))
            stash_next()
            for h0 in range(0, PEER_H, 4):
                top16([(fv[:, h, :], fpos[:, h, :], cand[:, h, :]) for h in range(h0, h0 + 4)], summed)
                stash_next()

        def gates_and_keys(tb):
            dve.do(lambda e: e.tensor_tensor(gij[:, 0, :].rearrange("p (h k) -> p h k", h=PEER_H), fv,
                                             fv[:, :, 0:1].broadcast_to([P, PEER_H, TOPK]), ALU.subtract),
                   *turned_before)
            exped = act_e.do(lambda e: e.activation(gij[:, 0, :], gij[:, 0, :], ACT.Exp), dve.last)
            dve.do(lambda e: e.tensor_single_scalar(part_u, fpos, 4, ALU.logical_shift_right))
            dve.do(lambda e: e.tensor_copy(part, part_u))
            pick(gij[:, 1, :], 0)
            stash_next()
            dve.do(lambda e: e.tensor_single_scalar(part_u, fpos, 15, ALU.bitwise_and))
            dve.do(lambda e: e.tensor_copy(part, part_u))
            pick(gij[:, 2, :], 1)
            g3 = gij[:, 0, :].rearrange("p (h k) -> p h k", h=PEER_H)
            dve.do(lambda e: e.tensor_reduce(gsum, g3, AX_X, ALU.add), exped)
            dve.do(lambda e: e.reciprocal(gsum, gsum))
            m = dve.do(lambda e: e.tensor_tensor(g3, g3, gsum.unsqueeze(2).broadcast_to([P, PEER_H, TOPK]), ALU.mult))
            b, bank, freed = banks.take()

            def emit(e):
                for j in range(3):
                    last = e.transpose(bank[:, j * P:(j + 1) * P], gij[:, j, :], const("ident"))
                return last
            done = pe.do(emit, m, *freed)
            turned_before[:] = [done]
            for j, dst in enumerate((g_t, i_t, j_t)):
                m = act_e.do(lambda e, j=j, dst=dst: e.activation(dst[:, tb * P:(tb + 1) * P],
                                                                  bank[:, j * P:(j + 1) * P], ACT.Copy), done)
            banks.free(b, m)
            stash_next()
            return m

        s_gates = [sem("gates_stored_a"), sem("gates_stored_b")]
        stores = [0, 0]
        staging = {}

        def dense_gates(q0, ready):
            wide = [P, 4, P]
            lanes = const("iota").unsqueeze(1).broadcast_to(wide)
            jk, hj, j_freed = hot_j.take()
            ik, hi, i_freed = hot_i.take()
            scale_here = q0 // 4 % 5 in (1, 3)
            if scale_here:
                for j in range(4):
                    hi_made = dve.do(lambda e, j=j: e.tensor_scalar(
                        hi[:, j, :], const("iota"), i_t[:, q0 + j:q0 + j + 1], g_t[:, q0 + j:q0 + j + 1],
                        ALU.is_equal, ALU.mult), ready, *i_freed, alone=True)
            else:
                rk, raw, r_freed = hot_raw.take()
                m = dve.do(lambda e: e.tensor_tensor(raw, lanes, i_t[:, q0:q0 + 4].unsqueeze(2).broadcast_to(wide),
                                                     ALU.is_equal), ready, *r_freed, alone=True)
            hj_made = dve.do(lambda e: e.tensor_tensor(hj, lanes, j_t[:, q0:q0 + 4].unsqueeze(2).broadcast_to(wide),
                                                       ALU.is_equal), *j_freed, alone=True)
            if not scale_here:
                for j in range(4):
                    hi_made = act_e.do(lambda e, j=j: e.activation(hi[:, j, :], raw[:, j, :], ACT.Copy,
                                                                   scale=g_t[:, q0 + j:q0 + j + 1]), m, *i_freed)
                hot_raw.free(rk, hi_made)
            yield
            b, bank, freed = banks.take()

            def emit(e):
                for j in range(4):
                    last = e.matmul(bank[:, j * P:(j + 1) * P], hj[:, j, :], hi[:, j, :], start=True, stop=True)
                return last
            done = pe.do(emit, hj_made, hi_made, *freed)
            hot_i.free(ik, done)
            hot_j.free(jk, done)
            yield
            at = q0 % GT
            if at == 0:
                staging["k"] = stages.take()
            gk, stage, stage_freed = staging["k"]
            src = bank.rearrange("p (t i) -> p i t", i=P)
            m = act_e.do(lambda e: e.activation(stage[:, :, at:at + 4], src, ACT.Copy), done, *stage_freed)
            banks.free(b, m)
            if at == GT - 4:
                stores[gk] += 1
                stages.free(gk, store(gates_dram[q0 // GT], stage.rearrange("p i t -> p (i t)"), s_gates[gk], stores[gk]))

        best_sums(0)
        for tb in range(TB):
            ready = gates_and_keys(tb)
            if tb + 1 < TB:
                best_sums(tb + 1)
            if tb == 0:
                act_e.wait(pe.last, dve.last)
            tasks = []
            for n, q0 in enumerate(range(tb * P, (tb + 1) * P, 4)):
                tasks.append(dense_gates(q0, ready))
                if n % STASH_EVERY == STASH_EVERY - 1:
                    tasks.append(stash_task())
            skewed(tasks)
        while stash_todo:
            stash_next()
        finish_stash()
        gates_ready = [(s_gates[k], 16 * stores[k]) for k in range(2)]
        stash_ready = [(stash_sems[k], 16 * stash_stores[k]) for k in range(3)]

        fence()
        for line in (sync, act_e, dve):
            line.wait(*gates_ready, *stash_ready)
        pos[0] = 0
        gates = Ring([view(EG * S, S // GT, EG, GT) for _ in range(2)])
        gate_sems = [sem(f"gates{k}_loaded") for k in range(2)]
        gate_loads = [0] * 2
        stashes = squares
        back_sems = [sem(f"stash{k}_loaded") for k in range(2)]
        back_loads = [0] * 2

        def views_r(n, width):
            base = pos[0]
            view(n * 2 * width)
            return [arena_r[:, base + k * 2 * width:base + (k + 1) * 2 * width].rearrange("p (s t) -> p s t", s=2)
                    for k in range(n)]

        coefs = Ring(views_r(EG + 2, S))
        down_w = Ring(views_r(EG + 2, SLOT))
        gate_tiles, coef_split, v_split, stash_tiles = [], [], [], {}

        def fetch_gates():
            i = len(gate_tiles) * EG
            if i < NKEYS:
                k, tile, freed = gates.take()
                gate_loads[k] += 1
                src = gates_dram[:, :, i * GT:(i + EG) * GT].rearrange("b j it -> j b it")
                gate_tiles.append((k, tile, load(tile.rearrange("p b i t -> p b (i t)"), src, gate_sems[k],
                                                 gate_loads[k], *freed)))

        stash_order = sorted(STASHED)

        def fetch_stash():
            if stash_order:
                i = stash_order.pop(0)
                k, tile, freed = stashes.take()
                back_loads[k] += 1
                stash_tiles[i] = (k, tile, load(tile, gelus_dram[STASHED.index(i)], back_sems[k], back_loads[k],
                                                *freed))

        def coefficients(i):
            gk, gate, gate_in = gate_tiles[i // EG]
            if i in STASHED:
                ring, (ak, a, gelu) = stashes, stash_tiles[i]
            else:
                b, bank, done = linear(1, act_hl, h2_ready)
                for _ in range(2):
                    split_down(i + 3)
                ring, (ak, a, a_freed) = wholes, wholes.take()
                gelu = act_e.do(lambda e: e.activation(a, bank, ACT.Gelu), done, *a_freed)
                banks.free(b, gelu)
            a3 = a.rearrange("p (b t) -> p b t", t=GT)
            m = dve.do(lambda e: e.tensor_tensor(a3, a3, gate[:, :, i % EG, :], ALU.mult), gelu, gate_in, alone=True)
            if i % EG == EG - 1:
                gates.free(gk, m)
                fetch_gates()
            ck, coef, c_freed = coefs.take()
            both = split(a, coef[:, 0, :], coef[:, 1, :], (m,), c_freed)
            ring.free(ak, both[1])
            if i in STASHED:
                fetch_stash()
            coef_split.append((ck, (coef[:, 0, :], coef[:, 1, :]), both))

        def split_down(end):
            i = len(v_split)
            if i < min(end, NKEYS) and down_w.idle:
                v_split.append(fetch_split(ins["peer_v"][i], down_w))

        def down(i0, sums=None):
            prepare(AHEAD + 1)
            for c in range(DC):
                b, bank, freed = banks.take()
                for i in range(i0, i0 + EG):
                    (_, coef, ready), (_, w, made) = coef_split[i], v_split[i]
                    done = mm(bank, three([x[:, c * P:(c + 1) * P] for x in w], coef), *ready, *made, *freed,
                              start=i == i0, stop=i == i0 + EG - 1)
                m = dve.do(lambda e, c=c, bank=bank: e.scalar_tensor_tensor(
                    res[:, c, :], bank, mod[:, 40 + c:41 + c], res[:, c, :], ALU.mult, ALU.add), done, alone=True)
                banks.free(b, m)
                if sums and c:
                    sums.add()
                if sums:
                    sums.square(c, m)
                if c == 1 and i0 + EG + 1 in STASHED:
                    coefficients(i0 + EG + 1)
                if c == 3:
                    split_down(NKEYS)
            for i in range(i0, i0 + EG):
                coefs.free(coef_split[i][0], done)
                down_w.free(v_split[i][0], done)

        for _ in range(2):
            fetch_gates()
        for _ in range(2):
            fetch_stash()
        for i in range(NKEYS):
            if len(coef_split) <= i:
                coefficients(i)
            split_down(i + 1)
            if i >= EG and i % EG == 0:
                down(i - EG)
        x2_squares = RunningSquares()
        down(NKEYS - EG, x2_squares)

        fence()
        dve.wait(dve.last)
        h_ready = apply_norm(spans["a_norm"], None, *rstd_of(*x2_squares.result(), D))
        conv_y = arena_r[:, 0:2 * CC * S].rearrange("p (s c t) -> p s c t", s=2, c=CC)
        conv_hl = [(conv_y[:, 0, c, :], conv_y[:, 1, c, :]) for c in range(CC)]
        conv_marks = []
        pos[0] = 2 * CC * S
        padded = Ring([view(S + 2) for _ in range(2)])
        work = Ring([view(S) for _ in range(8)])
        for k in range(2):
            pool.do(lambda e, k=k: e.memset(padded.items[k][:, 0:2], 0.0))
        dve.wait(pool.last)

        begin(3, act_hl, h_ready)
        for n in range(CC):
            got = [linear(1, act_hl, h_ready) for _ in ("c", "u", "b", "z")]
            (bc, c_bank, c_done), (bu, u_bank, u_done), (bb, b_bank, b_done), (bz, z_bank, z_done) = got
            wc, c_sb, c_freed = work.take()
            m = act_e.do(lambda e, c_sb=c_sb, c_bank=c_bank: e.activation(c_sb, c_bank, ACT.Copy), c_done, *c_freed)
            banks.free(bc, m)
            vk, vp, v_freed = padded.take()
            m = dve.do(lambda e, vp=vp, c_sb=c_sb, u_bank=u_bank: e.tensor_tensor(vp[:, 2:S + 2], c_sb, u_bank,
                                                                                ALU.mult), m, u_done, *v_freed)
            banks.free(bu, m)
            work.free(wc, m)
            wz, z_sb, z_freed = work.take()
            zm = act_e.do(lambda e, z_sb=z_sb, z_bank=z_bank: e.activation(z_sb, z_bank, ACT.Silu), z_done, *z_freed)
            banks.free(bz, zm)
            wt, acc, a_freed = work.take()
            dve.do(lambda e, acc=acc, vp=vp, n=n: e.tensor_scalar(acc, vp[:, 0:S], col("conv", n), None, ALU.mult),
                   *a_freed)
            for k in (1, 2):
                m = dve.do(lambda e, acc=acc, vp=vp, n=n, k=k: e.scalar_tensor_tensor(
                    acc, vp[:, k:k + S], col("conv", k * CC + n), acc, ALU.mult, ALU.add))
            padded.free(vk, m)
            m = dve.do(lambda e, acc=acc, b_bank=b_bank: e.tensor_tensor(acc, acc, b_bank, ALU.mult), b_done)
            banks.free(bb, m)
            m = pool.do(lambda e, acc=acc, z_sb=z_sb: e.tensor_tensor(acc, acc, z_sb, ALU.mult), m, zm)
            work.free(wz, m)
            both = split(acc, *conv_hl[n], (m,))
            work.free(wt, both[1])
            conv_marks.append(both)
        x3, x3_squares = project_back(2, conv_hl, conv_marks, None)

        fence()
        dve.wait(x3)
        x3_rstd = rstd_of(*x3_squares, D)
        kv_ready = apply_norm(spans["kv_norm"], None, *x3_rstd, keep=True)
        pos[0] = 0
        k_slc = view(GROUPS * S, GROUPS, S)
        k_win = view(GROUPS * S, GROUPS, S)
        v_sw = view(TB * S, TB, S)
        kcmp = view(GROUPS * NCP, GROUPS, NCP)
        vcmp = view(GROUPS * GROUPS * HD, GROUPS, GROUPS * HD)
        gate_rows = view(TB * 48, TB, 48)
        hidden = view(4 * P, 4, P)
        bias_cols = view(4)
        after_kv = pos[0]
        strm = [view(GROUPS * 528, GROUPS, 528) for _ in range(2)]
        pe_cols = view(32)
        w2 = view(2 * P * 2 , 2, 2 * P)
        hidden_v = view(2 * GROUPS * P, 2 * GROUPS, P)
        raw_keys = Ring([view(S) for _ in range(3)])
        rope_rings = Ring([view(S) for _ in range(2)]), Ring([view(S) for _ in range(2)])
        s_pos, s_w2 = sem("pos_loaded"), sem("w2_loaded")
        pos_in = load(pe_cols, ins["cmp_pos"], s_pos, 1)
        w2_in = load(w2.rearrange("p a b -> p (a b)"), ins["cmp_w2"], s_w2, 1)
        for g in range(GROUPS):
            other = halves[1 - g % 2]
            for t in (k_slc, k_win, kcmp):
                pool.do(lambda e, t=t, g=g, other=other: e.memset(t[other, g, :], 0.0))
        pool.do(lambda e: e.memset(vcmp, 0.0))
        for t in strm:
            pool.do(lambda e, t=t: e.memset(t[:, :, S - 1:528], 0.0))
        zeroed = pool.last

        begin(3, act_hl, kv_ready)
        for which in range(2):
            for g in range(GROUPS):
                b, bank, done = linear(1, act_hl, kv_ready)
                t = strm[which]
                m = act_e.do(lambda e, t=t, g=g, bank=bank: e.activation(t[0:64, g, 0:S], bank[0:64, :], ACT.Copy),
                             done, zeroed)
                m2 = dve.do(lambda e, t=t, g=g, bank=bank: e.tensor_copy(t[64:128, g, 0:S - 1], bank[64:128, 1:S]),
                            done, zeroed)
                banks.free(b, m, m2)
        strm_ready = (act_e.last, dve.last)
        pool.wait(tables_in)
        dve.wait(tables_in)
        rope16 = (const("rot16"), const("cos"), const("sin"))

        def rotated_keys(which, m_, dst):
            b, bank, done = linear(1, act_hl, kv_ready)
            xk, x, x_freed = raw_keys.take()
            m = act_e.do(lambda e: e.activation(x, bank, ACT.Copy), done, *x_freed)
            banks.free(b, m)
            yield
            got_ = []
            yield from rope_stages(rope_rings, [(dst[halves[j], 2 * m_ + j, :], halves[j]) for j in range(2)], x,
                                   *rope16, m, got_)
            raw_keys.free(xk, got_[0])

        skewed([rotated_keys(which, m_, dst) for which, dst in enumerate((k_slc, k_win)) for m_ in range(2)])
        got, done = linear_tokens(4, 2, act_hl, kv_ready)
        for tb, (b, bank) in enumerate(got):
            banks.free(b, act_e.do(lambda e, tb=tb, bank=bank: e.activation(v_sw[:, tb, :], bank, ACT.Copy), done))

        hb_ready = apply_norm(spans["b_norm"], None, *x3_rstd, act_freed=(done,))

        for which in range(2):
            w1 = [fetch(ins["cmp_w1"][which * 4 + i]) for i in range(4)]
            w1v = [w.rearrange("p (l n) -> p l n", l=4) for _, w, _ in w1]
            loaded = [x[2] for x in w1]
            for hc in range(2):
                b, bank, freed = banks.take()
                b2, bank2, freed2 = banks.take()

                def emit(e, which=which, hc=hc, bank=bank, bank2=bank2, w1v=w1v):
                    for l in range(CMP_PAIRS):
                        e.matmul(bank[:, 0:1], w1v[l // 4][:, l % 4, hc * P:(hc + 1) * P],
                                 pe_cols[:, which * 16 + l:which * 16 + l + 1], start=l == 0, stop=l == CMP_PAIRS - 1)
                    for l in range(CMP_PAIRS):
                        a = 2 * l
                        last = e.matmul(bank2[:, 0:P].rearrange("p (g n) -> p g n", g=GROUPS),
                                        w1v[l // 4][:, l % 4, hc * P:(hc + 1) * P],
                                        strm[which][:, :, a:a + CMP_STRIDE * (NCP - 1) + 1:CMP_STRIDE],
                                        start=l == 0, stop=l == CMP_PAIRS - 1)
                    return last
                done = pe.do(emit, *loaded, *strm_ready, pos_in, *freed, *freed2)
                slot = which * 2 + hc
                m = dve.do(lambda e, slot=slot, bank=bank: e.tensor_copy(bias_cols[:, slot:slot + 1], bank[:, 0:1]),
                           done)
                banks.free(b, m)
                m = act_e.do(lambda e, slot=slot, bank2=bank2: e.activation(
                    hidden[:, slot, :], bank2[:, 0:P], ACT.Gelu_apprx_tanh, bias=bias_cols[:, slot:slot + 1]), m)
                banks.free(b2, m)
            for k, _, _ in w1:
                slots.free(k, done)
        b, bank, freed = banks.take()
        done = mm(bank[:, 0:P], [(w2[:, hc, 0:P], hidden[:, hc, :]) for hc in range(2)], m, w2_in, *freed)
        for g in range(GROUPS):
            hf = halves[g % 2]
            m = dve.do(lambda e, g=g, hf=hf, bank=bank: e.tensor_copy(kcmp[hf, g, :], bank[hf, g * NCP:(g + 1) * NCP]),
                       done)
        banks.free(b, m)
        m4 = dve.do(lambda e: e.tensor_copy(
            hidden_v.rearrange("p a (i n) -> p a i n", i=GROUPS),
            hidden[:, 2:4, :].rearrange("p c (g n) -> p (c g) n", g=GROUPS).unsqueeze(2).broadcast_to(
                [P, 2 * GROUPS, GROUPS, NCP])), act_e.last)
        b, bank, freed = banks.take()

        def emit(e, bank=bank):
            for g in range(GROUPS):
                for hc in range(2):
                    last = e.matmul(bank[:, g * HD:(g + 1) * HD], hidden_v[:, hc * GROUPS + g, :], w2[:, hc, P:P + HD], start=hc == 0,
                                    stop=hc == 1)
            return last
        done = pe.do(emit, m4, *freed)
        for g in range(GROUPS):
            for i in range(GROUPS):
                rows = slice(i * NCP, (i + 1) * NCP)
                m = dve.do(lambda e, g=g, i=i, rows=rows, bank=bank: e.tensor_copy(
                    vcmp[rows, g, i * HD:(i + 1) * HD], bank[rows, g * HD:(g + 1) * HD]), done)
        banks.free(b, m)

        fence()
        pos[0] = after_kv
        q_raw = view(DC * S, DC, S)
        z_ring = Ring([view(S) for _ in range(2)])
        rope_mem = [view(S) for _ in range(4)]
        rope_rings = Ring(rope_mem[0:2]), Ring(rope_mem[2:4])
        pc_t = view(GROUPS * S, GROUPS, S)
        cmp_ring = Ring([(view(NSA_H * NCP), view(2 * NSA_H)) for _ in range(2)])
        cmp_mem = cmp_ring.items[0][0]

        got_g = banks.take()
        k, w, made = next_split()
        w = [x.rearrange("p (c n) -> p c n", c=DC) for x in w]
        for tb in range(TB):
            rows = slice(tb * P, (tb + 1) * P)
            done = mm(got_g[1][:, tb * 48:(tb + 1) * 48],
                      [p for c in range(DC) for p in three([x[:, rows] for x in act_hl[c]], [x[:, c, :] for x in w])],
                      *made, *got_g[2], *(m for marks in hb_ready for m in marks))
        splits.free(k, done)
        m = act_e.do(lambda e: e.activation(gate_rows.rearrange("p a b -> p (a b)"), got_g[1][:, 0:TB * 48],
                                            ACT.Sigmoid), done)
        banks.free(got_g[0], m)
        for c in range(DC):
            b, bank, done = linear(1, act_hl, hb_ready)
            m = act_e.do(lambda e, c=c, bank=bank: e.activation(q_raw[:, c, :], bank, ACT.Copy, scale=HD ** -0.5), done)
            banks.free(b, m)
        q_ready = act_e.last
        gates4 = gate_rows.rearrange("p t (h b) -> p t h b", b=3)

        keys_ready = dve.last

        def compressed(qb):
            b, bank, freed = banks.take()

            def emit(e):
                for c in range(DC):
                    for j in range(2):
                        g = 2 * (c // 4) + j
                        n = g * 4 + c % 4
                        last = e.matmul(bank[:, n * NCP:(n + 1) * NCP], q_raw[:, c, qb * P:(qb + 1) * P],
                                        kcmp[:, g, :], start=True, stop=True)
                return last
            done = pe.do(emit, q_ready, keys_ready, *freed)
            yield
            wide = [P, NSA_H, NCP]
            a0, b0 = qb * NCP, (qb + 1) * NCP
            add = const("cmp_add")[:, a0:b0].unsqueeze(1).broadcast_to(wide)
            mul = const("cmp_mul")[:, a0:b0].unsqueeze(1).broadcast_to(wide)
            ck, (mem, st), c_freed = cmp_ring.take()
            p = mem.rearrange("p (h n) -> p h n", n=NCP)
            mx, sm = st[:, 0:NSA_H], st[:, NSA_H:2 * NSA_H]
            m = dve.do(lambda e: e.tensor_tensor(p, bank.rearrange("p (h n) -> p h n", n=NCP), add, ALU.add),
                       done, *c_freed)
            banks.free(b, m)
            dve.do(lambda e: e.tensor_reduce(mx, p, AX_X, ALU.max))
            m = dve.do(lambda e: e.tensor_tensor(p, p, mx.unsqueeze(2).broadcast_to(wide), ALU.subtract))
            m = act_e.do(lambda e: e.activation(p, p, ACT.Exp), m)
            yield
            dve.do(lambda e: e.tensor_tensor(p, p, mul, ALU.mult), m)
            dve.do(lambda e: e.tensor_reduce(sm, p, AX_X, ALU.add))
            dve.do(lambda e: e.tensor_scalar(sm, sm, 1e-30, None, ALU.max))
            dve.do(lambda e: e.reciprocal(sm, sm))
            dve.do(lambda e: e.tensor_tensor(sm, sm, gates4[:, qb, :, 0], ALU.mult))
            m = dve.do(lambda e: e.tensor_tensor(p, p, sm.unsqueeze(2).broadcast_to(wide), ALU.mult))
            b, t_bank, freed = banks.take()

            def emit_turn(e):
                for g in range(GROUPS):
                    last = e.transpose(t_bank[:, g * P:(g + 1) * P],
                                       p[:, 4 * g:4 * g + 4, :].rearrange("p h n -> p (h n)"), const("ident"))
                return last
            done = pe.do(emit_turn, m, *freed)
            cmp_ring.free(ck, done)
            m = act_e.do(lambda e: e.activation(pc_t[:, :, qb * P:(qb + 1) * P],
                                                t_bank.rearrange("p (g q) -> p g q", g=GROUPS), ACT.Copy), done)
            banks.free(b, m)

        skewed([compressed(qb) for qb in range(TB)])
        pc_ready = act_e.last
        after_cmp = pos[0]

        def rotated_queries(c):
            yield from rope_stages(rope_rings, [(q_raw[:, c, :], slice(0, P))], q_raw[:, c, :], *rope16, q_ready, [])

        skewed([rotated_queries(c) for c in range(DC)])
        q_rot = q_raw

        fence(dve, act_e, pe)
        probs = Ring([*rope_mem, cmp_mem])
        turned_ring = Ring([[view(TB * S, TB, S) for _ in range(2)]])
        nsa, y_marks = {}, []

        def nsa_attend(c, j, qb, branch):
            g = 2 * (c // 4) + j
            i = c % 4
            keys_ = (k_slc, k_win)[branch]
            pk, p, sk, st, exped = exp_rows([(q_rot[:, c, :], keys_[:, g, :])], qb)
            yield
            gate = gates4[:, qb, g * 4 + i, branch + 1:branch + 2]
            m = dve.do(lambda e: e.reciprocal(st[:, 2:3], st[:, 1:2]), exped, alone=True)
            m = dve.do(lambda e: e.tensor_tensor(st[:, 3:4], st[:, 2:3], gate, ALU.mult), m)
            m = dve.do(lambda e: e.tensor_scalar(p, p, st[:, 3:4], None, ALU.mult), m)
            stats.free(sk, m)
            yield
            if qb == 0 and branch == 0:
                nsa["t"] = turned_ring.take()
            tk, t, t_freed = nsa["t"]
            turned, copied = transpose_rows(p, qb, t[branch], m, t_freed, act_e if branch else dve)
            nsa[qb, branch] = copied
            probs.free(pk, turned)
            if (qb, branch) != (TB - 1, 1):
                return
            if j == 0:
                nsa["bank"] = banks.take()
            b, bank, freed = nsa["bank"]
            o = bank[halves[j], :]
            marks = [nsa[q, br] for q in range(TB) for br in range(2)]
            for br in range(2):
                values_mm(o, lambda kb, br=br: v_sw[:, kb, br * 256 + g * HD:br * 256 + (g + 1) * HD], t[br],
                          marks if br == 0 else (), br == 0, False, *(freed if br == 0 else ()))
            done = pe.do(lambda e: e.matmul(o, vcmp[:, g, i * HD:(i + 1) * HD], pc_t[:, g, :], start=False, stop=True),
                         pc_ready)
            turned_ring.free(tk, done)
            if j == 0:
                return
            yield
            zb, z_bank, z_done = linear(1, act_hl, hb_ready)
            zk, z, z_freed = z_ring.take()
            zm = act_e.do(lambda e: e.activation(z, z_bank, ACT.Silu), z_done, *z_freed)
            banks.free(zb, zm)
            m = dve.do(lambda e: e.tensor_tensor(q_rot[:, c, :], bank, z, ALU.mult), zm, done, alone=True)
            banks.free(b, m)
            z_ring.free(zk, m)
            y_marks.append(m)

        skewed([nsa_attend(c, j, qb, branch) for c in range(DC) for j in range(2) for qb in range(TB)
                for branch in range(2)])
        fence(act_e, dve)
        y_split = [split(q_rot[:, c, :], *act_hl[c], (y_marks[c],)) for c in range(DC)]
        x4, x4_squares = project_back(1, act_hl, y_split, None)

        fence(dve, act_e)
        pos[0] = 0
        result = view(DC * S, DC, S)
        k, r, made = rstd_of(*x4_squares, D)
        s_out = sem("out_stored")
        for c in range(DC):
            m = scaled(result[:, c, :], res[:, c, :], spans["final"][:, c:c + 1], r, (made,))
            stored = load(out[c], result[:, c, :], s_out, c + 1, m)
        sync.wait(stored)

        with nc.Block() as block:
            @block.sync
            def _(e):
                sync.run(e)

            @block.tensor
            def _(e):
                pe.run(e)

            @block.vector
            def _(e):
                dve.run(e)

            @block.scalar
            def _(e):
                act_e.run(e)

            @block.gpsimd
            def _(e):
                pool.run(e)


def rotation(dim, block):
    r = np.zeros((P, P), np.float32)
    for b in range(0, P, block):
        for i in range(dim // 2):
            r[b + i + dim // 2, b + i] = -1.0
            r[b + i, b + i + dim // 2] = 1.0
    return r


def make_consts():
    c = np.zeros((P, NCONSTS), np.float32)

    def put(name, a):
        c[:, CONSTS[name][0]:CONSTS[name][1]] = a

    put("ident", np.eye(P, dtype=np.float32))
    put("ones", 1.0)
    put("ones64", np.kron(np.eye(2), np.ones((64, 64))))
    put("rot64", rotation(64, 64))
    put("rot16", rotation(16, 64))
    put("iota", np.arange(P)[None, :])
    mask = np.where(np.arange(P)[None, :] > np.arange(P)[:, None], NEG, 0.0)
    both = np.concatenate([np.eye(P), mask], axis=1).astype(np.float32)
    put("mask16", (both.view(np.uint32) >> 16).astype(np.uint16).view(np.float32))
    pos = np.arange(S, dtype=np.float32)
    inv = (np.float32(1.0) / (np.float32(10000.0) ** (np.arange(32, dtype=np.float32) / np.float32(32)))).astype(np.float32)
    ang = (pos[None, :] * inv[:, None]).astype(np.float32)
    put("cos", np.tile(np.cos(ang), (4, 1)))
    put("sin", np.tile(np.sin(ang), (4, 1)))
    inv = (np.float32(500000.0) ** (-np.arange(0, 16, 2, dtype=np.float32) / np.float32(16))).astype(np.float32)
    ang = (pos[None, :] * inv[:, None]).astype(np.float32)
    cos, sin = np.ones((64, S), np.float32), np.zeros((64, S), np.float32)
    cos[0:16], sin[0:16] = np.tile(np.cos(ang), (2, 1)), np.tile(np.sin(ang), (2, 1))
    tables2 = np.concatenate([np.tile(cos, (2, 1)), np.tile(sin, (2, 1))], axis=1)
    t = np.arange(P)[:, None, None] + P * np.arange(TB)[None, :, None]
    n = np.arange(NCP)[None, None, :]
    ok = (n * CMP_STRIDE + CMP_BLOCK - 1 <= t) & (n < NCMP)
    put("eps", np.array([n * EPS for n in EPS_N])[None, :])
    put("cmp_add", np.where(ok, 0.0, NEG).reshape(P, -1))
    put("cmp_mul", ok.astype(np.float32).reshape(P, -1))
    return c, tables2


def chunked(w):
    k, n = w.shape
    return np.ascontiguousarray(w.reshape(k // P, P, n // P, P).transpose(2, 1, 0, 3)).reshape(n // P, P, -1)


def moving(w, per):
    k, n = w.shape
    return np.ascontiguousarray(w.reshape(k // P // per, per, P, n).transpose(0, 2, 1, 3)).reshape(k // P // per, P, -1)


def columns(v):
    return np.asarray(v).reshape(-1, P).T


def lay_out(a):
    g = {k: np.asarray(v) for k, v in a.items()}
    cols = np.zeros((P, NCOLS), np.float32)

    def put(name, v):
        cols[:, COLS[name][0]:COLS[name][1]] = v

    twice = lambda v: np.concatenate([v, v])[:, None]
    put("ada_b", columns(g["ada_b"][0]))
    put("norm1", columns(g["norm1_g"][0]))
    put("norm2", columns(g["norm2_g"][0]))
    put("a_norm", columns(g["a_norm_2"][0]))
    put("kv_norm", columns(g["kv_norm_2"]))
    put("b_norm", columns(g["b_norm_2"][0]))
    put("final", columns(g["final_norm_2"]))
    put("q_lat", columns(g["mla_q_lat_g"][0]))
    put("kv_lat", columns(g["mla_kv_lat_g"][0]))
    put("q_nope", g["mla_q_g"][0][:NOPE, None])
    put("q_pe", twice(g["mla_q_g"][0][NOPE:]))
    put("k_nope", g["mla_k_g"][0][:NOPE, None])
    put("k_pe", twice(g["mla_k_g"][0][NOPE:]))
    put("dq", twice(g["diff_q_g"][0]))
    put("dk", twice(g["diff_k_g"][0]))
    put("subln", g["diff_subln_g"][0][:, None])
    put("conv", columns(g["a_conv_w_2"][0]))
    for name, one, two in (("lam_q", "diff_lq1", "diff_lq2"), ("lam_k", "diff_lk1", "diff_lk2")):
        cols[0:64, COLS[name][0]] = g[one][0]
        cols[0:64, COLS[name][0] + 1] = g[two][0]

    consts, tables2 = make_consts()
    w = g["w_in"][0]
    o0, o1, o2 = Q_LORA, Q_LORA + KV_LORA, Q_LORA + KV_LORA + ROPE
    o3, o4 = o2 + 512, o2 + 1024
    kpe = w[:, o1:o2]
    w_in = np.concatenate([w[:, o0:o1], kpe, kpe, w[:, :o0], w[:, o2:o4]], axis=1)
    qu = g["mla_w_q_up"][0].reshape(Q_LORA, MLA_H, NOPE + ROPE)
    q_up = np.concatenate([qu[:, :, :NOPE].reshape(Q_LORA, -1), qu[:, :, NOPE:].reshape(Q_LORA, -1)], axis=1)
    ku = g["mla_w_kv_up"][0].reshape(KV_LORA, MLA_H, NOPE + MLA_V)
    kv = g["w_kv_2"].reshape(D, 6, GROUPS, HD)
    kc = np.concatenate([kv[:, 0:2], kv[:, 0:2]], axis=3).reshape(D, -1)
    ks = np.concatenate([kv[:, 2].reshape(D, -1), kv[:, 4].reshape(D, -1)], axis=1)
    vsw = np.concatenate([kv[:, 3].reshape(D, -1), kv[:, 5].reshape(D, -1)], axis=1)
    order = [h for m in range(2) for i in range(4) for h in (8 * m + i, 8 * m + 4 + i)]
    bw = g["b_w_in_2"][0]
    bq = bw[:, :D].reshape(D, NSA_H, HD)[:, order].reshape(D, D)
    bz = bw[:, D + 48:].reshape(D, NSA_H, HD)[:, order].reshape(D, D)
    bo = g["b_w_out_2"][0].reshape(NSA_H, HD, D)[order].reshape(D, D)
    w1 = [g[n].reshape(CMP_PAIRS // 4, 4, P, CMP_HID).transpose(0, 2, 1, 3).reshape(4, P, -1)
          for n in ("cmp_w1_k_2", "cmp_w1_v_2")]
    pos = [g[n].reshape(CMP_PAIRS, P).T for n in ("cmp_pos_k_2", "cmp_pos_v_2")]
    w2k, w2v = (g[n].reshape(2, P, HD).transpose(1, 0, 2) for n in ("cmp_w2_k_2", "cmp_w2_v_2"))
    a_w_in = chunked(g["a_w_in_2"][0]).reshape(4, CC, P, -1)[[1, 2, 0, 3]].transpose(1, 0, 2, 3).reshape(4 * CC, P, -1)
    w_out = chunked(g["a_w_out_2"][0]).reshape(DC, P, 2, -1).transpose(0, 2, 1, 3).reshape(2 * DC, P, -1)
    return {
        "x": g["x"][0].T.reshape(DC, P, S).transpose(1, 0, 2).reshape(P, -1),
        "cols": cols,
        "consts": consts,
        "tables2": tables2,
        "c_rows": np.repeat(g["c"], P, axis=0),
        "ada_w": g["ada_w"][0].T.reshape(48, P, D),
        "w_in": chunked(w_in),
        "w_dv": moving(w[:, o4:], 2),
        "q_up": chunked(q_up),
        "kv_up": chunked(ku[:, :, :NOPE].reshape(KV_LORA, -1)),
        "kv_up_v": moving(ku[:, :, NOPE:].reshape(KV_LORA, -1), 2)[0],
        "w_out": chunked(g["w_out"][0]),
        "peer_q": chunked(g["peer_w_q"][0]),
        "keys": g["peer_sub_keys"][0].reshape(HP, NKEYS, P).transpose(2, 0, 1).reshape(P, -1),
        "peer_u": g["peer_u"][0].reshape(NKEYS, P, DC, P).transpose(0, 3, 2, 1).reshape(NKEYS, P, -1),
        "peer_v": g["peer_v"][0].reshape(NKEYS, P, D),
        "a_w_in": a_w_in,
        "a_w_out": w_out,
        "w_kvc": chunked(kc),
        "w_kvs": chunked(ks),
        "w_vsw": moving(vsw, 2),
        "cmp_w1": np.concatenate(w1),
        "cmp_pos": np.concatenate(pos, axis=1),
        "cmp_w2": np.concatenate([w2k, w2k, w2v, w2v], axis=2).reshape(P, -1),
        "w_gates": moving(bw[:, D:D + 48], DC),
        "b_q": chunked(bq),
        "b_z": chunked(bz),
        "b_w_out": chunked(bo),
    }


def kernel(**inputs):
    import concourse.bacc as bacc
    from concourse.bass_utils import run_bass_kernel_spmd

    nc = bacc.Bacc("TRN2", target_bir_lowering=False, num_devices=1)
    arrays = {f"in_{k}": np.ascontiguousarray(v) for k, v in lay_out(inputs).items()}
    ins = {k[3:]: nc.dram_tensor(k, list(v.shape), F32, kind="ExternalInput").ap() for k, v in arrays.items()}
    out = nc.dram_tensor("out", [DC, P, S], F32, kind="ExternalOutput").ap()
    build(nc, ins, out)
    r = run_bass_kernel_spmd(nc, [arrays], core_ids=[0])
    return np.ascontiguousarray(r.results[0]["out"].reshape(D, S).T).reshape(1, S, D)
```
